# Optimizing a Trainium2 kernel written in Bass

```python
import math
import jax, jax.numpy as jnp
from jax import lax
import numpy as np

D_MODEL = 1024
BATCH = 1
SEQ = 512
DEPTH = 1

GRID_W = 64
CTX_LEN = 256
N_HEADS_M = 4
D_MLSTM = 1024
HEAD_DIM_M = D_MLSTM // N_HEADS_M
MLSTM_CHUNK = 128
CONV_W = 3
N_GROUPS_S = 4
D_SGU = 1024
GROUP_DIM_S = D_SGU // N_GROUPS_S
SGU_CHUNK = 128
D_FF = 2816
N_MOD = 9
POS_BASE = 10000.0
F_BIAS_LO = 3.0
F_BIAS_HI = 6.0
EPS = 1e-6
PROJ_SIZES = (D_MLSTM, D_MLSTM, D_MLSTM, 4 * N_HEADS_M, D_MLSTM, D_SGU, D_SGU, D_MODEL, D_MODEL)
N_STATE_PIECES = 4
D_PROJ = sum(PROJ_SIZES)


def rmsnorm(x, g):
    x32 = x.astype(jnp.float32)
    y = x32 * lax.rsqrt(jnp.mean(x32 * x32, axis=-1, keepdims=True) + EPS)
    return (y * g.astype(jnp.float32)).astype(x.dtype)

def modulate(x, shift, scale):
    return x * (1.0 + scale[:, None, :]) + shift[:, None, :]

def ffn_sublayer(h, shift, scale, gate, g, w_in, w_out):
    hn = modulate(rmsnorm(h, g), shift, scale)
    a, b = jnp.split(hn @ w_in, 2, axis=-1)
    y = (jax.nn.silu(a) * b) @ w_out
    return h + 0.5 * gate[:, None, :] * y

def grid_pos_emb(rows):
    t = jnp.arange(rows * GRID_W)
    r = (t // GRID_W).astype(jnp.float32)
    col = (t % GRID_W).astype(jnp.float32)
    quarter = D_MODEL // 4
    freqs = jnp.exp(-math.log(POS_BASE) * jnp.arange(quarter, dtype=jnp.float32) / quarter)
    ar = r[:, None] * freqs
    ac = col[:, None] * freqs
    return jnp.concatenate([jnp.sin(ar), jnp.cos(ar), jnp.sin(ac), jnp.cos(ac)], axis=-1)

def split_cols(p, sizes):
    out = []
    off = 0
    for s in sizes:
        out.append(p[..., off:off + s])
        off += s
    return out

def project(h, shift, scale, g, w_in, sizes):
    hn = modulate(rmsnorm(h, g), shift, scale)
    return split_cols(hn @ w_in[:, :sum(sizes)], sizes)

def short_conv(x, w, b):
    pad = CONV_W // 2
    s = x.shape[1]
    xp = jnp.pad(x, ((0, 0), (pad, pad), (0, 0)))
    return sum(xp[:, j:j + s] * w[j] for j in range(CONV_W)) + b

def to_heads(t):
    b, s, _ = t.shape
    return t.reshape(b, s, N_HEADS_M, HEAD_DIM_M).transpose(0, 2, 1, 3).astype(jnp.float32)

def mlstm_prep(q, k, v, gates, conv_w, conv_b, b_gates):
    qk = jax.nn.silu(short_conv(jnp.concatenate([q, k], axis=-1), conv_w, conv_b))
    q, k = jnp.split(qk, 2, axis=-1)
    q = to_heads(q) * HEAD_DIM_M ** -0.5
    k = to_heads(k)
    v = to_heads(v)
    gt = jnp.moveaxis((gates + b_gates).astype(jnp.float32), -1, 1)
    nh = N_HEADS_M
    fwd = (gt[:, :nh], jax.nn.log_sigmoid(gt[:, nh:2 * nh]))
    bwd = (gt[:, 2 * nh:3 * nh], jax.nn.log_sigmoid(gt[:, 3 * nh:]))
    return q, k, v, fwd, bwd

def zero_state(bsz):
    return (jnp.zeros((bsz, N_HEADS_M, HEAD_DIM_M, HEAD_DIM_M), jnp.float32),
            jnp.zeros((bsz, N_HEADS_M, HEAD_DIM_M), jnp.float32),
            jnp.zeros((bsz, N_HEADS_M), jnp.float32))

def mlstm_scan(q, k, v, li, lf, state, reverse, emit):
    if reverse:
        q, k, v = jnp.flip(q, 2), jnp.flip(k, 2), jnp.flip(v, 2)
        li, lf = jnp.flip(li, 2), jnp.flip(lf, 2)
    bsz, nh, s, dh = q.shape
    nc = s // MLSTM_CHUNK

    def to_chunks(t):
        return jnp.moveaxis(t.reshape(t.shape[:2] + (nc, MLSTM_CHUNK) + t.shape[3:]), 2, 0)

    tri = jnp.tril(jnp.ones((MLSTM_CHUNK, MLSTM_CHUNK), dtype=bool))

    def body(carry, xs):
        c_st, n_st, m_st = carry
        qc, kc, vc, lic, lfc = xs
        b = jnp.cumsum(lfc, axis=-1)
        g = b[..., -1]
        w = g[..., None] - b + lic
        m_new = jnp.maximum(g + m_st, jnp.max(w, axis=-1))
        ws = jnp.exp(w - m_new[..., None])
        decay = jnp.exp(g + m_st - m_new)
        c_new = decay[..., None, None] * c_st + jnp.einsum('bhsv,bhsk->bhvk', vc * ws[..., None], kc)
        n_new = decay[..., None] * n_st + jnp.einsum('bhs,bhsk->bhk', ws, kc)
        if not emit:
            return (c_new, n_new, m_new), None
        dm = b[..., :, None] - b[..., None, :] + lic[..., None, :]
        dm = jnp.where(tri, dm, -jnp.inf)
        a = b + m_st[..., None]
        m_t = jnp.maximum(a, jnp.max(dm, axis=-1))
        s_ts = jnp.einsum('bhtk,bhsk->bhts', qc, kc) * jnp.exp(dm - m_t[..., None])
        inter = jnp.exp(a - m_t)
        num = jnp.einsum('bhts,bhsv->bhtv', s_ts, vc) + inter[..., None] * jnp.einsum('bhvk,bhtk->bhtv', c_st, qc)
        den = jnp.sum(s_ts, axis=-1) + inter * jnp.einsum('bhk,bhtk->bht', n_st, qc)
        h = num / jnp.maximum(jnp.abs(den), jnp.exp(-m_t))[..., None]
        return (c_new, n_new, m_new), h

    state, hs = lax.scan(body, state, (to_chunks(q), to_chunks(k), to_chunks(v), to_chunks(li), to_chunks(lf)))
    if not emit:
        return None, state
    h = jnp.moveaxis(hs, 0, 2).reshape(bsz, nh, s, dh)
    if reverse:
        h = jnp.flip(h, 2)
    return h, state

def head_layernorm(h, g):
    mu = jnp.mean(h, axis=-1, keepdims=True)
    hc = h - mu
    y = hc * lax.rsqrt(jnp.mean(hc * hc, axis=-1, keepdims=True) + EPS)
    bsz, nh, s, dh = h.shape
    return y.transpose(0, 2, 1, 3).reshape(bsz, s, nh * dh) * g.astype(jnp.float32)

def spatial_gating(u, v, g, w_s, b_s):
    bsz, s, _ = v.shape
    nc = s // SGU_CHUNK
    vn = rmsnorm(v, g).reshape(bsz, nc, SGU_CHUNK, N_GROUPS_S, GROUP_DIM_S)
    mixed = jnp.einsum('gts,bnsgc->bntgc', w_s, vn) + jnp.swapaxes(b_s, 0, 1)[:, :, None]
    return u * mixed.reshape(bsz, s, D_SGU)

def merge_branches(pieces, h_m, g_head, g_sgu, w_s, b_s, w_a, w_b, w_o):
    o, u, vs, ga, gb = pieces
    y_a = jax.nn.sigmoid(o) * head_layernorm(h_m, g_head).astype(o.dtype)
    y_b = spatial_gating(jax.nn.gelu(u), jax.nn.gelu(vs), g_sgu, w_s, b_s)
    mixed = jax.nn.sigmoid(ga) * (y_a @ w_a) + jax.nn.sigmoid(gb) * (y_b @ w_b)
    return mixed @ w_o

def first_inputs(seed: int = 0) -> dict:
    key = jax.random.key(seed)
    ks = jax.random.split(key, 28)
    f32 = jnp.float32
    L = DEPTH

    def nrm(k, shape, s):
        return jax.random.normal(k, shape, f32) * s

    def gain(k, shape):
        return 1.0 + 0.05 * jax.random.normal(k, shape, f32)

    i_bias = nrm(ks[10], (L, 2, N_HEADS_M), 0.1)
    f_bias = jnp.linspace(F_BIAS_LO, F_BIAS_HI, N_HEADS_M, dtype=f32) + nrm(ks[11], (L, 2, N_HEADS_M), 0.1)
    return {
        'x': nrm(ks[0], (BATCH, SEQ, D_MODEL), 1.0),
        'c': nrm(ks[1], (BATCH, D_MODEL), 1.0),
        'ctx': nrm(ks[2], (BATCH, CTX_LEN, D_MODEL), 1.0),
        'c_ctx': nrm(ks[3], (D_MODEL,), 1.0),
        'w_ada': nrm(ks[4], (L, D_MODEL, N_MOD * D_MODEL), 0.5 * D_MODEL ** -0.5),
        'b_ada': nrm(ks[5], (L, N_MOD * D_MODEL), 0.01),
        'g_ffn1': gain(ks[6], (L, D_MODEL)),
        'w_ffn1_in': nrm(ks[7], (L, D_MODEL, 2 * D_FF), D_MODEL ** -0.5),
        'w_ffn1_out': nrm(ks[8], (L, D_FF, D_MODEL), D_FF ** -0.5),
        'g_mix': gain(ks[9], (L, D_MODEL)),
        'w_in': nrm(ks[12], (L, D_MODEL, D_PROJ), D_MODEL ** -0.5),
        'b_gates': jnp.stack([i_bias, f_bias], axis=2).reshape(L, 4 * N_HEADS_M),
        'conv_qk_w': nrm(ks[13], (L, CONV_W, 2 * D_MLSTM), CONV_W ** -0.5),
        'conv_qk_b': nrm(ks[14], (L, 2 * D_MLSTM), 0.01),
        'g_head': gain(ks[15], (L, D_MLSTM)),
        'g_sgu': gain(ks[16], (L, D_SGU)),
        'w_s': nrm(ks[17], (L, N_GROUPS_S, SGU_CHUNK, SGU_CHUNK), SGU_CHUNK ** -0.5),
        'b_s': 1.0 + nrm(ks[18], (L, N_GROUPS_S, SGU_CHUNK), 0.1),
        'w_branch_a': nrm(ks[19], (L, D_MLSTM, D_MODEL), D_MLSTM ** -0.5),
        'w_branch_b': nrm(ks[20], (L, D_SGU, D_MODEL), D_SGU ** -0.5),
        'w_out': nrm(ks[21], (L, D_MODEL, D_MODEL), D_MODEL ** -0.5),
        'g_ffn2': gain(ks[22], (L, D_MODEL)),
        'w_ffn2_in': nrm(ks[23], (L, D_MODEL, 2 * D_FF), D_MODEL ** -0.5),
        'w_ffn2_out': nrm(ks[24], (L, D_FF, D_MODEL), D_FF ** -0.5),
        'g_final': gain(ks[25], (D_MODEL,)),
    }

def first_block(x, c, ctx, c_ctx, w_ada, b_ada, g_ffn1, w_ffn1_in, w_ffn1_out, g_mix, w_in, b_gates,
              conv_qk_w, conv_qk_b, g_head, g_sgu, w_s, b_s, w_branch_a, w_branch_b, w_out,
              g_ffn2, w_ffn2_in, w_ffn2_out, g_final):
    rows = x.shape[1] // GRID_W
    bsz = x.shape[0]
    h = x + grid_pos_emb(rows).astype(x.dtype)[None]
    hc = ctx
    for layer in range(DEPTH):
        is_last = layer == DEPTH - 1
        mods = jnp.split(jax.nn.silu(c) @ w_ada[layer] + b_ada[layer], N_MOD, axis=-1)
        mods_c = jnp.split(jax.nn.silu(c_ctx)[None] @ w_ada[layer] + b_ada[layer], N_MOD, axis=-1)

        h = ffn_sublayer(h, mods[0], mods[1], mods[2], g_ffn1[layer], w_ffn1_in[layer], w_ffn1_out[layer])
        hc = ffn_sublayer(hc, mods_c[0], mods_c[1], mods_c[2], g_ffn1[layer], w_ffn1_in[layer], w_ffn1_out[layer])

        p_lat = project(h, mods[3], mods[4], g_mix[layer], w_in[layer], PROJ_SIZES)
        ctx_sizes = PROJ_SIZES[:N_STATE_PIECES] if is_last else PROJ_SIZES
        p_ctx = project(hc, mods_c[3], mods_c[4], g_mix[layer], w_in[layer], ctx_sizes)
        q_l, k_l, v_l, gf_l, gb_l = mlstm_prep(*p_lat[:N_STATE_PIECES], conv_qk_w[layer], conv_qk_b[layer], b_gates[layer])
        q_c, k_c, v_c, gf_c, gb_c = mlstm_prep(*p_ctx[:N_STATE_PIECES], conv_qk_w[layer], conv_qk_b[layer], b_gates[layer])

        state0 = zero_state(bsz)
        hcf, st_f = mlstm_scan(q_c, k_c, v_c, gf_c[0], gf_c[1], state0, False, not is_last)
        hcb, st_b = mlstm_scan(q_c, k_c, v_c, gb_c[0], gb_c[1], state0, True, not is_last)
        hlf, _ = mlstm_scan(q_l, k_l, v_l, gf_l[0], gf_l[1], st_f, False, True)
        hlb, _ = mlstm_scan(q_l, k_l, v_l, gb_l[0], gb_l[1], st_b, True, True)

        y_lat = merge_branches(p_lat[N_STATE_PIECES:], hlf + hlb, g_head[layer], g_sgu[layer], w_s[layer], b_s[layer],
                               w_branch_a[layer], w_branch_b[layer], w_out[layer])
        h = h + mods[5][:, None, :] * y_lat
        if not is_last:
            y_ctx = merge_branches(p_ctx[N_STATE_PIECES:], hcf + hcb, g_head[layer], g_sgu[layer], w_s[layer], b_s[layer],
                                   w_branch_a[layer], w_branch_b[layer], w_out[layer])
            hc = hc + mods_c[5][:, None, :] * y_ctx
            hc = ffn_sublayer(hc, mods_c[6], mods_c[7], mods_c[8], g_ffn2[layer], w_ffn2_in[layer], w_ffn2_out[layer])

        h = ffn_sublayer(h, mods[6], mods[7], mods[8], g_ffn2[layer], w_ffn2_in[layer], w_ffn2_out[layer])
    return rmsnorm(h, g_final)


HEAD_DIM = 64
N_FOX_HEADS = 8
N_SB_HEADS = 8
FOX_WIDTH = N_FOX_HEADS * HEAD_DIM
SB_WIDTH = N_SB_HEADS * HEAD_DIM
MIX_WIDTH = FOX_WIDTH + SB_WIDTH
IN_COLS = 3 * FOX_WIDTH + 3 * SB_WIDTH + N_FOX_HEADS
Q_BLOCK = 128
N_MEM = 256
N_MEM_HEADS = 4
MEM_HEAD_DIM = D_MODEL // N_MEM_HEADS
D_FF_2 = ((8 * D_MODEL // 3 + 255) // 256) * 256
CONV_WIDTH = 3


def _rmsnorm(x, g):
    xf = x.astype(jnp.float32)
    y = xf * lax.rsqrt(jnp.mean(xf * xf, axis=-1, keepdims=True) + EPS)
    return (y * g.astype(jnp.float32)).astype(x.dtype)

def _heads(t, n):
    b, s, w = t.shape
    return t.reshape(b, s, n, w // n).transpose(0, 2, 1, 3)

def _merge(t):
    b, n, s, d = t.shape
    return t.transpose(0, 2, 1, 3).reshape(b, s, n * d)

def _sweep(fn, q, *per_query):
    b, h, s, d = q.shape
    n = s // Q_BLOCK
    qb = q.reshape(b, h, n, Q_BLOCK, d).transpose(2, 0, 1, 3, 4)
    extras = [e.reshape(b, h, n, Q_BLOCK).transpose(2, 0, 1, 3) for e in per_query]
    out = lax.map(lambda a: fn(*a), (jnp.arange(n), qb, *extras))
    return out.transpose(1, 2, 0, 3, 4).reshape(b, h, s, d)

def _fox_attention(q, k, v, log_f):
    s_len = q.shape[2]
    scale = HEAD_DIM ** -0.5
    c = jnp.cumsum(log_f.astype(jnp.float32), axis=-1)
    kpos = jnp.arange(s_len)

    def block(i, qi, ci):
        qpos = i * Q_BLOCK + jnp.arange(Q_BLOCK)
        logits = jnp.einsum('bhqd,bhkd->bhqk', qi, k, preferred_element_type=jnp.float32) * scale
        logits = logits + ci[..., None] - c[:, :, None, :]
        logits = jnp.where(kpos[None, :] <= qpos[:, None], logits, -jnp.inf)
        p = jax.nn.softmax(logits, axis=-1)
        return jnp.einsum('bhqk,bhkd->bhqd', p.astype(v.dtype), v)

    return _sweep(block, q, c)

def _stick_breaking_attention(q, k, v):
    s_len = q.shape[2]
    scale = HEAD_DIM ** -0.5
    kpos = jnp.arange(s_len)

    def block(i, qi):
        qpos = i * Q_BLOCK + jnp.arange(Q_BLOCK)
        z = jnp.einsum('bhqd,bhkd->bhqk', qi, k, preferred_element_type=jnp.float32) * scale
        strict = kpos[None, :] < qpos[:, None]
        log_keep = jnp.where(strict, jax.nn.log_sigmoid(-z), 0.0)
        after = lax.cumsum(log_keep, axis=3, reverse=True) - log_keep
        a = jnp.where(strict, jnp.exp(jax.nn.log_sigmoid(z) + after), 0.0)
        return jnp.einsum('bhqk,bhkd->bhqd', a.astype(v.dtype), v)

    return _sweep(block, q)

def _memory_cross_attention(h, m, w_q, w_kv, w_o):
    q = _heads(jnp.einsum('bsd,dc->bsc', h, w_q), N_MEM_HEADS)
    kv = jnp.einsum('bmd,dc->bmc', m, w_kv)
    k, v = jnp.split(kv, 2, axis=-1)
    k, v = _heads(k, N_MEM_HEADS), _heads(v, N_MEM_HEADS)
    logits = jnp.einsum('bhqd,bhkd->bhqk', q, k, preferred_element_type=jnp.float32) * (MEM_HEAD_DIM ** -0.5)
    p = jax.nn.softmax(logits, axis=-1)
    o = jnp.einsum('bhqk,bhkd->bhqd', p.astype(v.dtype), v)
    return jnp.einsum('bsc,cd->bsd', _merge(o), w_o)

def _causal_dwconv(u, w, b):
    s_len = u.shape[1]
    up = jnp.pad(u, ((0, 0), (CONV_WIDTH - 1, 0), (0, 0)))
    y = b
    for i in range(CONV_WIDTH):
        y = y + up[:, i:i + s_len] * w[i]
    return y

def second_inputs(seed: int = 0) -> dict:
    key = jax.random.key(seed)
    ks = jax.random.split(key, 24)
    f32 = jnp.float32

    def nrm(k, shape, fan_in):
        return jax.random.normal(k, shape, f32) * (fan_in ** -0.5)

    def gain(k, shape):
        return 1.0 + 0.02 * jax.random.normal(k, shape, f32)

    return {
        "x": jax.random.normal(ks[0], (BATCH, SEQ, D_MODEL), f32),
        "mem": jax.random.normal(ks[1], (BATCH, N_MEM, D_MODEL), f32),
        "attn_norm_g": gain(ks[2], (DEPTH, D_MODEL)),
        "w_in": nrm(ks[3], (DEPTH, D_MODEL, IN_COLS), D_MODEL),
        "b_forget": jnp.linspace(1.0, 6.0, N_FOX_HEADS, dtype=f32)[None, :]
                    + 0.1 * jax.random.normal(ks[4], (DEPTH, N_FOX_HEADS), f32),
        "fox_out_g": gain(ks[5], (DEPTH, FOX_WIDTH)),
        "sb_out_g": gain(ks[6], (DEPTH, SB_WIDTH)),
        "w_out": nrm(ks[7], (DEPTH, MIX_WIDTH, D_MODEL), MIX_WIDTH),
        "xattn_norm_g": gain(ks[8], (DEPTH, D_MODEL)),
        "mem_norm_g": gain(ks[9], (DEPTH, D_MODEL)),
        "w_mq": nrm(ks[10], (DEPTH, D_MODEL, D_MODEL), D_MODEL),
        "w_mkv": nrm(ks[11], (DEPTH, D_MODEL, 2 * D_MODEL), D_MODEL),
        "w_mo": nrm(ks[12], (DEPTH, D_MODEL, D_MODEL), D_MODEL),
        "ffn_norm_g": gain(ks[13], (DEPTH, D_MODEL)),
        "w_up": nrm(ks[14], (DEPTH, D_MODEL, 2 * D_FF_2), D_MODEL),
        "conv_w": nrm(ks[15], (DEPTH, CONV_WIDTH, 2 * D_FF_2), CONV_WIDTH),
        "conv_b": 0.02 * jax.random.normal(ks[16], (DEPTH, 2 * D_FF_2), f32),
        "w_down": nrm(ks[17], (DEPTH, D_FF_2, D_MODEL), D_FF_2),
        "final_norm_g": gain(ks[18], (D_MODEL,)),
    }

def second_block(x, mem, attn_norm_g, w_in, b_forget, fox_out_g, sb_out_g, w_out,
              xattn_norm_g, mem_norm_g, w_mq, w_mkv, w_mo,
              ffn_norm_g, w_up, conv_w, conv_b, w_down, final_norm_g):
    split_at = np.cumsum([FOX_WIDTH, FOX_WIDTH, FOX_WIDTH, SB_WIDTH, SB_WIDTH, SB_WIDTH]).tolist()
    for l in range(DEPTH):
        h = _rmsnorm(x, attn_norm_g[l])
        proj = jnp.einsum('bsd,dc->bsc', h, w_in[l])
        fq, fk, fv, sq, sk, sv, f_logit = jnp.split(proj, split_at, axis=-1)
        log_f = jax.nn.log_sigmoid(f_logit.astype(jnp.float32) + b_forget[l].astype(jnp.float32))
        log_f = log_f.transpose(0, 2, 1)
        fox_o = _merge(_fox_attention(_heads(fq, N_FOX_HEADS), _heads(fk, N_FOX_HEADS),
                                      _heads(fv, N_FOX_HEADS), log_f))
        sb_o = _merge(_stick_breaking_attention(_heads(sq, N_SB_HEADS), _heads(sk, N_SB_HEADS),
                                                _heads(sv, N_SB_HEADS)))
        mixed = jnp.concatenate([_rmsnorm(fox_o, fox_out_g[l]), _rmsnorm(sb_o, sb_out_g[l])], axis=-1)
        x = x + jnp.einsum('bsc,cd->bsd', mixed, w_out[l])

        h = _rmsnorm(x, xattn_norm_g[l])
        m = _rmsnorm(mem, mem_norm_g[l])
        x = x + _memory_cross_attention(h, m, w_mq[l], w_mkv[l], w_mo[l])

        h = _rmsnorm(x, ffn_norm_g[l])
        u = jnp.einsum('bsd,df->bsf', h, w_up[l])
        u = _causal_dwconv(u, conv_w[l], conv_b[l])
        gate, val = jnp.split(u, 2, axis=-1)
        x = x + jnp.einsum('bsf,fd->bsd', jax.nn.silu(gate) * val, w_down[l])
    return _rmsnorm(x, final_norm_g)


def setup_inputs(seed=0):
    out = dict(first_inputs(seed))
    for name, value in second_inputs(seed + 1).items():
        if name != "x":
            out[name + "_2"] = value
    return out


def reference(
    x, c, ctx, c_ctx, w_ada, b_ada, g_ffn1, w_ffn1_in, w_ffn1_out, g_mix, w_in, b_gates,
    conv_qk_w, conv_qk_b, g_head, g_sgu, w_s, b_s, w_branch_a, w_branch_b, w_out, g_ffn2,
    w_ffn2_in, w_ffn2_out, g_final, mem_2, attn_norm_g_2, w_in_2, b_forget_2, fox_out_g_2,
    sb_out_g_2, w_out_2, xattn_norm_g_2, mem_norm_g_2, w_mq_2, w_mkv_2, w_mo_2, ffn_norm_g_2,
    w_up_2, conv_w_2, conv_b_2, w_down_2, final_norm_g_2,
):
    x = first_block(
        x, c, ctx, c_ctx, w_ada, b_ada, g_ffn1, w_ffn1_in, w_ffn1_out, g_mix, w_in, b_gates,
        conv_qk_w, conv_qk_b, g_head, g_sgu, w_s, b_s, w_branch_a, w_branch_b, w_out, g_ffn2,
        w_ffn2_in, w_ffn2_out, g_final,
    )
    return second_block(
        x, mem_2, attn_norm_g_2, w_in_2, b_forget_2, fox_out_g_2, sb_out_g_2, w_out_2,
        xattn_norm_g_2, mem_norm_g_2, w_mq_2, w_mkv_2, w_mo_2, ffn_norm_g_2, w_up_2, conv_w_2,
        conv_b_2, w_down_2, final_norm_g_2,
    )


_drawn_inputs = setup_inputs


def setup_inputs(seed=0):
    import zlib

    import numpy as np

    out = dict(_drawn_inputs(seed))
    spreads = {}
    factors = {'ctx': 7.961,
     'c_ctx': 3.986,
     'b_ada': 6.887,
     'g_ffn1': 8.0,
     'g_mix': 5.544,
     'conv_qk_w': 7.344,
     'conv_qk_b': 8.0,
     'g_head': 8.0,
     'g_sgu': 8.0,
     'b_s': 6.136,
     'g_ffn2': 8.0,
     'attn_norm_g_2': 3.306,
     'fox_out_g_2': 4.66,
     'sb_out_g_2': 5.294,
     'xattn_norm_g_2': 8.0,
     'mem_norm_g_2': 8.0,
     'ffn_norm_g_2': 4.81,
     'conv_b_2': 5.215,
     'final_norm_g_2': 2.781}
    for name, (base, spread) in spreads.items():
        noise = np.random.default_rng([zlib.crc32(name.encode()), seed]).standard_normal(out[name].shape)
        drawn = base * np.exp(spread * noise) if base else spread * noise
        out[name] = __import__('jax').numpy.asarray(drawn.astype(out[name].dtype))
    for name, factor in factors.items():
        out[name] = (out[name] * factor).astype(out[name].dtype)
    return out
```

```python
from contextlib import ExitStack

import numpy as np

import concourse.bass as bass
from concourse import mybir

F32 = mybir.dt.float32
F32R = mybir.dt.float32r
ALU = mybir.AluOpType
ACT = mybir.ActivationFunctionType
AX = mybir.AxisListType

P = 128
D = 1024
KT = D // P
S = 512
C = 256
FF = 2816
FT = FF // P
PARTS = [(0, 8), (8, 8), (16, 6)]
UNIT = 16 * P
EPS = 1e-6
BIG = float(2.0 ** 100)
NMOD = 9
HM, DHM = 4, 256
CH = 128
HA, DHA = 8, 64
HX, DHX = 4, 256

VECTORS = [("c", 1), ("c_ctx", 1), ("b_ada", NMOD), ("g_ffn1", 1), ("g_mix", 1), ("g_head", 1), ("g_sgu", 1),
           ("g_ffn2", 1), ("g_final", 1), ("conv_qk_w", 6), ("conv_qk_b", 2), ("attn_norm_g_2", 1),
           ("fox_out_g_2", 0.5), ("sb_out_g_2", 0.5), ("xattn_norm_g_2", 1), ("mem_norm_g_2", 1),
           ("ffn_norm_g_2", 1), ("conv_w_2", 3 * 2 * FF / D), ("conv_b_2", 2 * FF / D), ("final_norm_g_2", 1)]
VCOL = {}
NVCOL = 0
for _name, _width in VECTORS:
    VCOL[_name] = NVCOL
    NVCOL += int(_width * KT)

CONSTS = ["ident", "ones", "neg_ones", "neg_le", "neg_ge", "npen_le", "npen_ge", "npen_lt"]


class Phase:

    def __init__(self, name, kind, weight, cols, n, x, segs=("x",), kts=KT, k0=0, natural=False, **more):
        self.name, self.kind, self.weight, self.cols, self.n = name, kind, weight, cols, n
        self.x, self.segs, self.kts, self.k0, self.natural = x, segs, kts, k0, natural
        self.more = more
        self.act_steps = ACT_STEPS.get(kind, 0)
        self.own_steps = OWN_STEPS.get(kind, 0) * len(segs)
        self.out_steps = OUT_STEPS.get(kind, 0)


ACT_STEPS = {"swiglu": 1, "convswiglu": 2, "convqk": 1, "sig_mul": 1, "func": 1}
OWN_STEPS = {"swiglu": 2, "convswiglu": 6, "convqk": 4, "sig_mul": 4, "mixb": 6}
OUT_STEPS = {"convqk": 1}
TOKENS = {"x": S, "ctx": C, "mem": C}


def ffn_phases(name, w_in, w_out, segs, gates, conv=False):
    out = []
    for k0, kn in PARTS:
        out.append(Phase(f"{name}_in{k0}", "convswiglu" if conv else "swiglu", w_in, (k0 * P, FF + k0 * P), kn, "xn",
                         segs, f0=k0))
        out.append(Phase(f"{name}_out{k0}", "resid", w_out, 0, KT // 2, "hid", segs, kts=kn, k0=k0, gates=gates))
    return out


class Norm:

    def __init__(self, name, src, seg, gain, shift=None, tiles=KT, out="split", out_tile=0, needs=()):
        self.name, self.src, self.seg, self.gain, self.shift = name, src, seg, gain, shift
        self.tiles, self.out, self.out_tile, self.needs = tiles, out, out_tile, needs
        self.tokens = TOKENS[seg]


def program(nc, d, out):
    with ExitStack() as ctx:
        top = [(nc.sbuf_base + 31) // 32 * 32]

        def reserve(size):
            at = top[0]
            top[0] += (size + 31) // 32 * 32
            return at

        def place(name, columns, at, dtype=F32, partitions=P):
            return nc.alloc_sbuf_tensor_at(name, [partitions, columns], dtype, offset=at)

        TILE = S * 4
        at_resid, at_ctx, at_xh, at_xl = reserve(KT * TILE), reserve(KT * C * 4), reserve(KT * TILE), reserve(KT * TILE)
        at_b = [reserve(KT * TILE) for _ in range(4)] + [reserve(2 * HM * 2 * (DHM + 1) * 4)]
        at_raw = reserve(2 * UNIT * 4)
        at_wh, at_wl = reserve(2 * UNIT * 4), reserve(2 * UNIT * 4)
        at_s = reserve(5 * TILE)

        resid = place("resid", KT * S, at_resid)
        hctx = place("hctx", KT * C, at_ctx)
        xn_h = place("xn_h", KT * S, at_xh, F32R)
        xn_l = place("xn_l", KT * S, at_xl, F32R)
        hid_h = place("hid_h", KT * S, at_b[0], F32R)
        hid_l = place("hid_l", KT * S, at_b[1], F32R)
        xc_h = place("xc_h", KT * C, at_b[4], F32R)
        xc_l = place("xc_l", KT * C, at_b[4] + KT * C * 4, F32R)
        hidc_h = place("hidc_h", KT * C, at_b[2], F32R)
        hidc_l = place("hidc_l", KT * C, at_b[2] + KT * C * 4, F32R)
        sqc = [place(f"sqc{i}", C, at_b[3] + i * C * 4) for i in range(2)]
        tmpc = [place(f"tmpc{i}", C, at_b[3] + (2 + i) * C * 4) for i in range(2)]
        yc = [place(f"yc{i}", C, at_ctx + i * C * 4) for i in range(2)]
        ada_slots = [0, 1, 3, 4]
        buf = [place(f"buf{i}", KT * S, at) for i, at in enumerate(at_b)]
        raw = [place(f"raw{i}", UNIT, at_raw + i * UNIT * 4) for i in range(2)]
        w_h = [place(f"w_h{i}", UNIT, at_wh + i * UNIT * 4, F32R) for i in range(2)]
        w_l = [place(f"w_l{i}", UNIT, at_wl + i * UNIT * 4, F32R) for i in range(2)]
        sq = [place(f"sq{i}", S, at_s + i * TILE) for i in range(2)]
        tmp = [place(f"tmp{i}", S, at_s + (2 + i) * TILE) for i in range(2)]
        rstd = place("rstd", S, at_s + 4 * TILE)
        ada_rows = [place(f"ada_rows{i}", S, at_xh + i * TILE) for i in range(4)]
        conv_b = [place(f"conv_b{i}", S, at_ctx + i * TILE) for i in range(2)]

        consts = place("consts", len(CONSTS) * P, reserve(len(CONSTS) * P * 4))
        vec = place("vec", NVCOL, reserve(NVCOL * 4))
        silu_c = place("silu_c", KT * 2, reserve(KT * 2 * 4))
        mods = place("mods", NMOD * KT * 2, reserve(NMOD * KT * 2 * 4))
        DER = ["ctx_gs1", "ctx_sh1", "ctx_ga1", "ctx_gs2", "ctx_sh2", "gs1", "sh1", "ga1", "gs2", "sh2", "ga2",
               "gs3", "sh3", "ga3"]
        der = place("der", len(DER) * KT, reserve(len(DER) * KT * 4))
        NG = (C + S) // CH
        gate_w = place("gate_w", KT * 4 * HM, reserve(KT * 4 * HM * 4))
        gate_b = place("gate_b", 4 * HM, reserve(4 * HM * 4))
        b_s = place("b_s", CH, reserve(CH * 4))
        lf, li, lt, neg_b, a_col, total, cm_last, m_in, m_end = [
            place(name, 64, reserve(64 * 4)) for name in
            ("lf", "li", "lt", "neg_b", "a_col", "total", "cm_last", "m_in", "m_end")]
        decay_ws = place("decay_ws", 128, reserve(128 * 4))
        rows = place("rows", 2 * CH, reserve(2 * CH * 4))
        rows_in = place("rows_in", 2 * CH, at_s)
        diag = place("diag", 64, at_s + 2 * CH * 4)
        kc = place("kc", KT * C, at_b[3])
        vc = place("vc", KT * C, at_b[3] + KT * C * 4)
        state = place("state", 2 * HM * 2 * (DHM + 1), at_b[4])
        slot_at = [at_ctx, at_s]
        def scratch(name, columns, at):
            return [place(f"{name}{i}", columns, slot_at[i] + at * 4) for i in range(2)]
        m_inter, pen_d, emt = scratch("m_inter", CH, 0), scratch("pen_d", CH, CH), scratch("emt", CH, 2 * CH)
        p_st, q_int = scratch("p_st", CH, 3 * CH), scratch("q_int", 2 * CH, 4 * CH)
        n_bc, k_nat = scratch("n_bc", 2 * CH, 6 * CH), scratch("k_nat", 2 * CH, 8 * CH)
        den, h_new = scratch("den", CH, 10 * CH), scratch("h_new", 2 * CH, 11 * CH)
        emt.append(place("emt2", CH, reserve(CH * 4)))
        wv = scratch("wv", DHM + 1, 13 * CH)
        h_rstd = place("h_rstd", HM * S, at_ctx)
        v_nat = [place(f"v_nat{i}", D, at_ctx + i * D * 4) for i in range(2)]
        w_st = place("w_st", 4 * CH, at_b[4])
        HALF = KT // 2 * S
        half_buf = lambda name, i, h: place(name, HALF, at_b[i] + h * HALF * 4)
        fq, fk, sq_t, sk = half_buf("fq", 0, 0), half_buf("fk", 0, 1), half_buf("sq_t", 1, 0), half_buf("sk", 1, 1)
        fv, sv = half_buf("fv", 2, 0), half_buf("sv", 2, 1)
        fox_o, sb_o = half_buf("fox_o", 4, 0), half_buf("sb_o", 4, 1)
        SB_COLS = S * (S // CH + 1) // 2
        sp_a = [place(f"sp_a{i}", SB_COLS, at_b[3] + i * SB_COLS * 4) for i in range(3)]
        crow = place("crow", S, at_xl + 3 * TILE)
        p_t = [place(f"p_t{i}", S // CH * S, at_xh + i * KT * TILE // 2) for i in range(2)]
        p_nat = [place(f"p_nat{i}", S, at_xl + i * TILE) for i in range(3)]
        mem_k, mem_v = half_buf("mem_k", 2, 0), half_buf("mem_v", 2, 1)
        wf = place("wf", KT * HA, reserve(KT * HA * 4))
        bf = place("bf", HA, reserve(HA * 4))
        N_ATT = (HA + HX) * (S // CH)
        fl, flt = place("fl", S // CH * HA, reserve(S // CH * HA * 4)), place("flt", S // CH * HA, reserve(S // CH * HA * 4))
        neg_max, p_sum, p_inv = [place(n, N_ATT, reserve(N_ATT * 4)) for n in ("neg_max", "p_sum", "p_inv")]
        assert top[0] <= nc.sbuf_usable_end, (top[0], nc.sbuf_usable_end)

        bank = [ctx.enter_context(nc.psum_tensor(f"bank{i}", [P, 512], F32)) for i in range(8)]

        SUMS = 6

        def banks(slot, seg):
            if seg == "ctx":
                return [bank[3 * slot + 2][:, 0:C], bank[3 * slot + 2][:, C:2 * C]]
            return [bank[3 * slot + n][:, 0:TOKENS[seg]] for n in range(2)]

        def inputs(x, seg):
            if seg == "ctx":
                return (xc_h, xc_l, C) if x == "xn" else (hidc_h, hidc_l, C)
            return (xn_h, xn_l, S) if x == "xn" else (hid_h, hid_l, S)

        def const(name):
            i = CONSTS.index(name)
            return consts[:, i * P:(i + 1) * P]

        def vcol(name, i=0):
            return vec[:, bass.ds(i + VCOL[name], 1)]

        def dcol(name, i=0):
            return der[:, bass.ds(i + DER.index(name) * KT, 1)]

        def tile(t, i, n=S, stride=S):
            return t[:, bass.ds(i * stride, n)]

        def sem(name):
            return ctx.enter_context(nc.semaphore(name))

        loaded = [sem("loaded0"), sem("loaded1")]
        hi_ready = sem("hi_ready")
        lo_ready = sem("lo_ready")
        mm_done = sem("mm_done")
        bank_free = sem("bank_free")
        act_out = sem("act_out")
        dve_step = sem("dve_step")
        conv_out = sem("conv_out")
        const_in, vec_in, ctx_in, x_in = sem("const_in"), sem("vec_in"), sem("ctx_in"), sem("x_in")
        pos_added = sem("pos_added")
        ada_in = [sem(f"ada_in{i}") for i in range(4)]
        c_ready, ada_mm, ada_row, ada_turned = sem("c_ready"), sem("ada_mm"), sem("ada_row"), sem("ada_turned")
        ada_taken, chain = sem("ada_taken"), sem("chain")
        sq_ready, sq_used = sem("sq_ready"), sem("sq_used")
        var_ready, std_ready, rstd_ready = sem("var_ready"), sem("std_ready"), sem("rstd_ready")
        scaled, xh_ready, xn_ready = sem("scaled"), sem("xh_ready"), sem("xn_ready")
        out_stored = sem("out_stored")
        gate_in, bs_in, ws_in = sem("gate_in"), sem("bs_in"), sem("ws_in")
        f_ready = sem("f_ready")
        gates_mm, abs_ready, ln_ready, lf_ready = sem("gates_mm"), sem("abs_ready"), sem("ln_ready"), sem("lf_ready")
        sums_mm, a_ready, rows_mm, diag_ready = sem("sums_mm"), sem("a_ready"), sem("rows_mm"), sem("diag_ready")
        last_mm, diff_ready, ws_ready = sem("last_mm"), sem("diff_ready"), sem("ws_ready")
        ml_a, ml_kt, ml_row, ml_exp, ml_kn = sem("ml_a"), sem("ml_kt"), sem("ml_row"), sem("ml_exp"), sem("ml_kn")
        ml_q, ml_p, ml_num, ml_upd, ml_h, ml_st = sem("ml_q"), sem("ml_p"), sem("ml_num"), sem("ml_upd"), sem("ml_h"), sem("ml_st")
        hn_mu, hn_c, hn_sq, hn_var, hn_v, hn_std = [sem("hn_" + s) for s in ("mu", "c", "sq", "var", "v", "std")]
        hn_done = sem("hn_done")
        sg_t, sg_v, sg_m, sg_y = sem("sg_t"), sem("sg_v"), sem("sg_m"), sem("sg_y")
        wf_in, mem_in = sem("wf_in"), sem("mem_in")
        fg_mm, fg_pre, fg_ln, fg_lf, fg_rows, fg_crow = [sem("fg_" + s) for s in ("mm", "pre", "ln", "lf", "rows", "crow")]
        at_logits, at_max, at_exp, at_p = sem("at_logits"), sem("at_max"), sem("at_exp"), sem("at_p")
        at_tr, at_copy, at_pv, at_out = sem("at_tr"), sem("at_copy"), sem("at_pv"), sem("at_out")
        sb_z, sb_abs, sb_e, sb_ln, sb_sp = sem("sb_z"), sem("sb_abs"), sem("sb_e"), sem("sb_ln"), sem("sb_sp")
        sb_cum, sb_a, sb_pv, sb_out = sem("sb_cum"), sem("sb_a"), sem("sb_pv"), sem("sb_out")

        src_ctx = lambda k: hctx[:, k * C:(k + 1) * C]
        src_x = lambda k: resid[:, k * S:(k + 1) * S]
        residual = {"x": (resid, S), "ctx": (hctx, C)}
        at = lambda i: lambda k: tile(buf[i], k)
        nat = lambda t, width: lambda ch, k: t[:, :].rearrange("p (c w) -> p c w", w=width)[:, ch:ch + 2, bass.ds(k * 256, 256)]
        qkv = [2 * D, 2 * D + D, 2 * D + D + 4 * HM]
        o_at = 3 * D + 4 * HM
        stages = []
        stages.append(Norm("ctx_ffn1", src_ctx, "ctx", lambda k: dcol("ctx_gs1", k), "ctx_sh1"))
        stages.append(Norm("ffn1", src_x, "x", lambda k: dcol("gs1", k), "sh1"))
        stages += ffn_phases("ffn1", "w_ffn1_in", "w_ffn1_out", ("x", "ctx"), ("ga1", "ctx_ga1"))
        stages.append(Norm("ctx_mix", src_ctx, "ctx", lambda k: dcol("ctx_gs2", k), "ctx_sh2"))
        stages.append(Norm("mix", src_x, "x", lambda k: dcol("gs2", k), "sh2"))
        stages.append(Phase("q", "convqk", "w_in", 0, 4, "xn", c0=0, dst={"x": at(0)}))
        stages.append(Phase("k", "convqk", "w_in", D, 4, "xn", ("x", "ctx"), c0=KT,
                            dst={"x": at(1), "ctx": lambda k: tile(kc, k, C, C)}))
        stages.append(Phase("v", "natstore", "w_in", 2 * D, 4, "xn", ("x", "ctx"), natural=True,
                            dst={"x": nat(buf[2], D), "ctx": nat(vc, D)}))
        stages += [dict(stage="gates"), dict(stage="mlstm"), dict(stage="headnorm")]
        stages.append(Phase("ga", "func", "w_in", o_at + 3 * D, 4, "xn", func=ACT.Sigmoid, dst=at(2)))
        stages.append(Phase("o", "sig_mul", "w_in", o_at, 4, "xn", by=buf[3], after=[(hn_done, 8)]))
        stages.append(Phase("branch_a", "mul", "w_branch_a", 0, 4, "hid", dst=buf[2]))
        stages.append(Phase("u", "func", "w_in", o_at + D, 4, "xn", func=ACT.Gelu_apprx_tanh, dst=at(0)))
        stages.append(Phase("vs", "func", "w_in", o_at + 2 * D, 4, "xn", func=ACT.Gelu_apprx_tanh, dst=at(1)))
        stages.append(Phase("gb", "func", "w_in", o_at + 4 * D, 4, "xn", func=ACT.Sigmoid, dst=at(3)))
        stages.append(Norm("sgu", at(1), "x", lambda k: vcol("g_sgu", k), out="f32"))
        stages.append(dict(stage="sgu"))
        stages.append(Phase("branch_b", "mixb", "w_branch_b", 0, 4, "xn", by=buf[3], plus=buf[2], after=[(sg_y, 4)]))
        stages.append(Phase("out", "resid", "w_out", 0, 4, "hid", gates=("ga2",)))
        stages.append(Norm("ffn2", src_x, "x", lambda k: dcol("gs3", k), "sh3"))
        stages += ffn_phases("ffn2", "w_ffn2_in", "w_ffn2_out", ("x",), ("ga3",))
        stages.append(Norm("final", src_x, "x", lambda k: vcol("g_final", k), out="f32"))

        chunk_of = [list(range(NG)), [1, 0, 5, 4, 3, 2]]
        ml_steps = [(pos, di, e) for pos in range(NG) for di in range(2) for e in range(HM)]
        N_CTX = C // CH * 2 * HM
        N_X = len(ml_steps) - N_CTX
        N_UPD = len(ml_steps) - 2 * HM
        gcol = lambda di, g, e: di * 32 + g * HM + e
        update_bank = lambda w, kk: bank[(4 if w < N_CTX and w % 2 else 6) + kk][:, 0:DHM + 1]
        stages.append(Norm("attn", src_x, "x", lambda k: vcol("attn_norm_g_2", k)))
        W2 = HA * DHA
        for i, (name, to) in enumerate((("fq", fq), ("fk", fk), ("fv", fv), ("sq", sq_t), ("sk", sk), ("sv", sv))):
            if name[1] == "v":
                stages.append(Phase(name, "natstore", "w_in_2", i * W2, 2, "xn", natural=True, dst={"x": nat(to, W2)}))
            else:
                stages.append(Phase(name, "store", "w_in_2", i * W2, 2, "xn", scale=DHA ** -0.5 if name[1] == "q" else 1.0,
                                    dst=lambda k, to=to: tile(to, k)))
            if name == "fq":
                stages.append(dict(stage="fgates"))
        stages += [dict(stage="fox"), dict(stage="sb")]
        stages.append(Norm("fox_out", lambda k: tile(fox_o, k), "x", lambda k: vcol("fox_out_g_2", k), tiles=4,
                           needs=[(at_out, HA), (sb_out, HA)]))
        stages.append(Norm("sb_out", lambda k: tile(sb_o, k), "x", lambda k: vcol("sb_out_g_2", k), tiles=4, out_tile=4,
                           needs=[(sb_out, HA)]))
        stages.append(Phase("out_2", "resid", "w_out_2", 0, 4, "xn", gates=(None,)))
        stages.append(Norm("mem", src_ctx, "mem", lambda k: vcol("mem_norm_g_2", k), needs=[(mem_in, 16)]))
        stages.append(Phase("mem_k", "store", "w_mkv_2", 0, 4, "xn", ("mem",), scale=1.0, dst=lambda k: tile(mem_k, k, C, C)))
        stages.append(Phase("mem_v", "natstore", "w_mkv_2", D, 4, "xn", ("mem",), natural=True, dst={"mem": nat(mem_v, D)}))
        stages.append(Norm("xattn", src_x, "x", lambda k: vcol("xattn_norm_g_2", k)))
        stages.append(Phase("mem_q", "store", "w_mq_2", 0, 4, "xn", scale=DHX ** -0.5, dst=at(3)))
        stages.append(dict(stage="xattn"))
        stages.append(Phase("mem_o", "resid", "w_mo_2", 0, 4, "hid", gates=(None,), after=[(at_out, HA + HX)]))
        stages.append(Norm("ffn3", src_x, "x", lambda k: vcol("ffn_norm_g_2", k)))
        stages += ffn_phases("ffn3", "w_up_2", "w_down_2", ("x",), (None,), conv=True)
        stages.append(Norm("final_2", src_x, "x", lambda k: vcol("final_norm_g_2", k), out="f32"))
        phases = [st for st in stages if isinstance(st, Phase)]

        NQ = S // CH
        att_steps = [(h, i) for h in range(HA + HX) for i in range(NQ)]
        ATT = {"fox": (0, HA * NQ), "xattn": (HA * NQ, N_ATT)}
        def keys_of(n):
            h, i = att_steps[n]
            return (i + 1) * CH if h < HA else C
        def heads_after(n, first):
            return [n // NQ] if n >= first and n % NQ == NQ - 1 else []
        SB_BANKS = [S, S, 2 * CH]
        SB_AT = {0: (0, 0), 1: (1, 0), 3: (1, 3 * CH), 2: (2, 0)}
        SB_WIDTH = lambda j: S - j * CH
        def sb_part(t, j):
            b, c = SB_AT[j]
            return t[:, b * S + c:b * S + c + SB_WIDTH(j)]

        units = acts = owns = outs = norms = ntiles = nsplit = 0
        fresh = None
        made = None
        in_place = False
        for st in stages:
            if isinstance(st, Phase):
                st.base, st.act_base, st.own_base, st.out_base = units, acts, owns, outs
                units += st.n
                acts += st.n * st.act_steps
                owns += st.n * st.own_steps
                outs += st.n * st.out_steps
                st.wait_for = None
                if st.x == "xn" and fresh is not None:
                    st.wait_for, fresh = ("norm", fresh.tile_base - fresh.out_tile), None
                if st.x == "hid":
                    st.wait_for = made
                if st.kind in ("swiglu", "convswiglu"):
                    made = ("units", st.base, 1)
                if st.kind in ("sig_mul", "mixb"):
                    made = ("units", st.base, 2)
            elif isinstance(st, Norm):
                st.index, st.tile_base, st.split_base, st.units_before = norms, ntiles, nsplit, units
                st.in_place_before = ntiles if in_place else 0
                in_place = st.out != "split"
                norms += 1
                ntiles += st.tiles
                if st.out == "split":
                    nsplit += st.tiles
                    fresh = st
            else:
                st.update(units=units, outs=outs, ntiles=ntiles)
        ALL = units
        N_ADA = NMOD * D // 512

        def run_units(eng, ph, body, peel=0):
            first = max(peel, 2 - ph.base, 0)
            for k in range(min(first, ph.n)):
                body(k, (ph.base + k) % 2)
            pairs = max(ph.n - first, 0) // 2
            if pairs >= 2:
                with eng.Fori(0, pairs) as i:
                    for j in range(2):
                        body(i * 2 + (first + j), (ph.base + first + j) % 2)
                first += 2 * pairs
            for k in range(first, ph.n):
                body(k, (ph.base + k) % 2)

        def half_count(base, k, slot):
            if isinstance(k, int):
                return (base + k) // 2 + 1
            return (k + (base - slot)) // 2 + 1

        block = ctx.enter_context(nc.Block())

        @block.sync
        def _(sp):
            sp.dma_start(vec[:, :], d["vectors"]).then_inc(vec_in, 16)
            sp.dma_start(consts[:, :], d["consts"]).then_inc(const_in, 16)
            w_ada = d["w_ada"].rearrange("(k p) n -> p k n", p=P)

            def ada_unit(u, slot):
                if not isinstance(u, int) or u >= 4:
                    sp.wait_ge(ada_mm, u - 3)
                view = buf[ada_slots[slot]][:, :].rearrange("p (k n) -> p k n", n=512)
                sp.dma_start(view, w_ada[:, :, bass.ds(u * 512, 512)]).then_inc(ada_in[slot], 16)

            for u in range(4):
                ada_unit(u, u)
            sp.dma_start(hctx[:, :].rearrange("p (k n) -> p k n", n=C),
                         d["ctx"].rearrange("(k p) n -> p k n", p=P)).then_inc(ctx_in, 16)
            sp.dma_start(resid[:, :].rearrange("p (k n) -> p k n", n=S),
                         d["x"].rearrange("(k p) n -> p k n", p=P)).then_inc(x_in, 16)
            sp.dma_start(buf[2][:, :].rearrange("p (k n) -> p k n", n=S),
                         d["pos"].rearrange("(k p) n -> p k n", p=P)).then_inc(x_in, 16)
            with sp.Fori(1, N_ADA // 4) as i:
                for j in range(4):
                    ada_unit(i * 4 + j, j)
            for u in range(N_ADA // 4 * 4, N_ADA):
                ada_unit(u, u % 4)

            def gemm(ph):
                w = d[ph.weight].rearrange("(k p) n -> p k n", p=P)

                def unit(k, slot):
                    u = k + ph.base
                    if not isinstance(u, int) or u >= 2:
                        sp.wait_ge(lo_ready, u - 1)
                    view = raw[slot][:, 0:ph.kts * 256].rearrange("p (k n) -> p k n", n=256)
                    if isinstance(ph.cols, tuple):
                        for n in range(2):
                            sp.dma_start(view[:, :, n * P:(n + 1) * P],
                                         w[:, ph.k0:ph.k0 + ph.kts, bass.ds(k * P + ph.cols[n], P)])\
                                .then_inc(loaded[slot], 16)
                    else:
                        half = ph.kts // 2
                        for k0, k1 in ((0, half), (half, ph.kts)):
                            sp.dma_start(view[:, k0:k1, :],
                                         w[:, ph.k0 + k0:ph.k0 + k1, bass.ds(k * 256 + ph.cols, 256)])\
                                .then_inc(loaded[slot], 16)

                run_units(sp, ph, unit)

            for st in stages:
                if isinstance(st, Phase):
                    gemm(st)
            sp.wait_ge(xn_ready, ntiles)
            sp.dma_start(out.rearrange("(k p) n -> p k n", p=P),
                         resid[:, :].rearrange("p (k n) -> p k n", n=S)).then_inc(out_stored, 16)
            sp.wait_ge(out_stored, 16)

        @block.gpsimd
        def _(pool):
            def rests(u, slot):
                pool.wait_ge(hi_ready, u + 1)
                nc.gpsimd.tensor_tensor(w_l[slot][:, :], raw[slot][:, :], w_h[slot][:, :].bitcast(F32),
                                        ALU.subtract).then_inc(lo_ready, 1)

            def rests_between(first, end):
                for u in range(first, min(first + first % 2, end)):
                    rests(u, u % 2)
                first += first % 2
                with pool.Fori(first // 2, end // 2) as i:
                    for j in range(2):
                        rests(i * 2 + j, j)
                if end % 2:
                    rests(end - 1, 0)

            done = 0
            def mlstm(st):
                for j in range(N_X):
                    pos, di, e = ml_steps[N_CTX + j]
                    g, s = chunk_of[di][pos], j % 2
                    pool.wait_ge(ml_exp, j + 1)
                    pool.wait_ge(ml_st, N_CTX + j - 2 * HM + 1)
                    if j >= 2:
                        pool.wait_ge(ml_num, j - 1)
                    q = buf[0][:, :].rearrange("p (k t) -> p k t", t=S)[:, 2 * e:2 * e + 2, (g - 2) * CH:(g - 1) * CH]
                    nc.gpsimd.tensor_tensor(q_int[s][:, :].rearrange("p (k t) -> p k t", k=2), q,
                                            m_inter[s][:, :].unsqueeze(1).to_broadcast([P, 2, CH]), ALU.mult)
                    o = (di * HM + e) * 2 * (DHM + 1)
                    n = state[:, o:o + 2 * (DHM + 1)].rearrange("p (k n) -> p k n", k=2)[:, :, DHM:DHM + 1]
                    nc.gpsimd.tensor_copy(n_bc[s][:, :].rearrange("p (k t) -> p k t", k=2), n.to_broadcast([P, 2, CH]))\
                        .then_inc(ml_q, 1)

            POOL_STAGE = {"mlstm": mlstm}
            for st in stages:
                if isinstance(st, dict) and st["stage"] in POOL_STAGE:
                    ahead = min(st["units"] + 1, ALL)
                    rests_between(done, ahead)
                    done = ahead
                    POOL_STAGE[st["stage"]](st)
            rests_between(done, ALL)

        @block.scalar
        def _(act):
            def heads(u, slot, count):
                act.wait_ge(loaded[slot], count * 32)
                if not isinstance(u, int) or u >= 2:
                    act.wait_ge(mm_done, u - 1)
                nc.scalar.activation(w_h[slot][:, :], raw[slot][:, :], ACT.Copy).then_inc(hi_ready, 1)

            def gemm(ph):
                def unit(k, slot):
                    u = k + ph.base
                    if not (ph is phases[-1] and isinstance(k, int) and k == ph.n - 1):
                        heads(u + 1, 1 - slot, half_count(ph.base, k + 1, 1 - slot))
                    if ph.kind in ACT_STEPS:
                        act.wait_ge(mm_done, u + 1)
                    if ph.kind == "swiglu":
                        for seg, s in zip(ph.segs, (sq, sqc)):
                            ins = nc.scalar.activation(s[slot][:, 0:TOKENS[seg]], banks(slot, seg)[0], ACT.Silu)
                        ins.then_inc(act_out, 1)
                    elif ph.kind == "convswiglu":
                        b = banks(slot, "x")
                        for n, y in enumerate((sq[slot], conv_b[slot])):
                            ct = k + (n * FT + ph.more["f0"])
                            ins = nc.scalar.activation(y[:, :], b[n], ACT.Identity,
                                                       bias=vcol("conv_b_2", ct), scale=vcol("conv_w_2", ct + 4 * FT))
                        ins.then_inc(act_out, 1)
                        act.wait_ge(dve_step, k * 6 + (ph.own_base + 3))
                        nc.scalar.activation(sq[slot][:, :], sq[slot][:, :], ACT.Silu).then_inc(act_out, 1)
                    elif ph.kind == "convqk":
                        if not isinstance(k, int) or k + ph.out_base:
                            act.wait_ge(conv_out, k + ph.out_base)
                        for seg, y in zip(ph.segs, (sq, yc)):
                            for n in range(2):
                                ct = k * 2 + (n + ph.more["c0"])
                                ins = nc.scalar.activation(y[n][:, 0:TOKENS[seg]], banks(slot, seg)[n], ACT.Identity,
                                                           bias=vcol("conv_qk_b", ct),
                                                           scale=vcol("conv_qk_w", ct + 2 * KT))
                        ins.then_inc(act_out, 1)
                        act.wait_ge(bank_free, u + 1)
                        for seg, y in zip(ph.segs, (sq, yc)):
                            for n in range(2):
                                ins = nc.scalar.activation(ph.more["dst"][seg](k * 2 + n), y[n][:, 0:TOKENS[seg]],
                                                           ACT.Silu)
                        ins.then_inc(conv_out, 1)
                    elif ph.kind == "sig_mul":
                        act.wait_ge(bank_free, u)
                        for n in range(2):
                            ins = nc.scalar.activation(sq[n][:, :], banks(slot, "x")[n], ACT.Sigmoid)
                        ins.then_inc(act_out, 1)
                    elif ph.kind == "func":
                        for n in range(2):
                            ins = nc.scalar.activation(ph.more["dst"](k * 2 + n), banks(slot, "x")[n],
                                                       ph.more["func"])
                        ins.then_inc(act_out, 1)

                run_units(act, ph, unit, peel=ph.n if ph is phases[-1] else int(ph.out_steps))

            def norm(n):
                T = n.tokens
                if n.units_before:
                    act.wait_ge(bank_free, n.units_before)
                elif n.index == 0:
                    act.wait_ge(ctx_in, 16)
                if n.in_place_before:
                    act.wait_ge(xn_ready, n.in_place_before)
                if n.src is src_x and n.index < 2:
                    act.wait_ge(pos_added, 1)
                for s, value in n.needs:
                    act.wait_ge(s, value)
                for k in range(n.tiles):
                    t = n.tile_base + k
                    if t >= 2:
                        act.wait_ge(sq_used, t - 1)
                    nc.scalar.activation(sq[t % 2][:, 0:T], n.src(k), ACT.Square).then_inc(sq_ready, 1)
                act.wait_ge(var_ready, n.index + 1)
                nc.scalar.activation(rstd[:, 0:T], rstd[:, 0:T], ACT.Sqrt).then_inc(std_ready, 1)
                if n.out == "split":
                    for k in range(n.tiles):
                        act.wait_ge(scaled, n.split_base + k + 1)
                        head, _, stride = inputs("xn", n.seg)
                        dst = head[:, (n.out_tile + k) * stride:(n.out_tile + k) * stride + T]
                        if n.shift:
                            ins = nc.scalar.activation(dst, tmp[k % 2][:, 0:T], ACT.Identity, bias=dcol(n.shift, k))
                        else:
                            ins = nc.scalar.activation(dst, tmp[k % 2][:, 0:T], ACT.Copy)
                        ins.then_inc(xh_ready, 1)

            act.wait_ge(vec_in, 16)
            cv = VCOL["c"]
            nc.scalar.activation(silu_c[:, :].rearrange("p (k w) -> p w k", w=2),
                                 vec[:, cv:cv + 2 * KT].rearrange("p (w k) -> p w k", w=2), ACT.Silu)\
                .then_inc(c_ready, 1)
            act.dma_start(gate_w[:, :].rearrange("p (k n) -> p k n", n=4 * HM),
                          d["gate_w"].rearrange("(k p) n -> p k n", p=P)).then_inc(gate_in, 16)
            act.dma_start(gate_b[:, :], d["gate_b"]).then_inc(gate_in, 16)
            act.dma_start(b_s[0:4, :], d["b_s"]).then_inc(bs_in, 16)

            act.dma_start(wf[:, :].rearrange("p (k n) -> p k n", n=HA), d["wf"].rearrange("(k p) n -> p k n", p=P))\
                .then_inc(wf_in, 16)
            act.dma_start(bf[:, :], d["bf"]).then_inc(wf_in, 16)

            def gates(st):
                act.wait_ge(f_ready, 1)
                nc.scalar.activation(lt[:, :], lf[:, :], ACT.Abs).then_inc(abs_ready, 1)
                act.wait_ge(abs_ready, 1)
                nc.scalar.activation(lt[:, :], lt[:, :], ACT.Exp, scale=-1.0).then_inc(ln_ready, 1)
                act.wait_ge(ln_ready, 1)
                nc.scalar.activation(lt[:, :], lt[:, :], ACT.Ln, bias=1.0).then_inc(ln_ready, 1)
                act.wait_ge(diff_ready, 1)
                nc.scalar.activation(decay_ws[:, :], decay_ws[:, :], ACT.Exp).then_inc(ws_ready, 1)

            def mlstm(st):
                def exps(j):
                    pos, di, e = ml_steps[N_CTX + j]
                    c, s = gcol(di, chunk_of[di][pos], e), j % 2
                    act.wait_ge(ml_row, j + 1)
                    nc.scalar.activation(pen_d[s][:, :], pen_d[s][:, :], ACT.Exp, scale=-1.0, bias=a_col[:, c:c + 1])
                    nc.scalar.activation(m_inter[s][:, :], m_inter[s][:, :], ACT.Exp, scale=-1.0, bias=m_in[:, c:c + 1])
                    nc.scalar.activation(emt[j % 3][:, :], emt[j % 3][:, :], ACT.Exp).then_inc(ml_exp, 1)

                def naturals(w):
                    pos, di, e = ml_steps[w]
                    g, s = chunk_of[di][pos], w % 2
                    ws = decay_ws[:, 64 + gcol(di, g, e):65 + gcol(di, g, e)]
                    act.wait_ge(ml_kt, w + 1)
                    if w >= 2:
                        act.wait_ge(ml_upd, w - 1)
                    v = vc[:, g * D:(g + 1) * D] if g < 2 else buf[2][:, (g - 2) * D:(g - 1) * D]
                    nc.scalar.activation(k_nat[s][:, :], bank[2 + s][:, 0:2 * CH], ACT.Copy, scale=DHM ** -0.5)
                    nc.scalar.activation(wv[s][:, 0:DHM], v[:, e * DHM:(e + 1) * DHM], ACT.Copy, scale=ws)
                    nc.scalar.activation(wv[s][:, DHM:DHM + 1], ws, ACT.Copy).then_inc(ml_kn, 1)

                act.wait_ge(bank_free, st["units"])
                for w in range(N_CTX):
                    naturals(w)
                for j in range(N_X):
                    exps(j)
                    if N_CTX + j < N_UPD:
                        naturals(N_CTX + j)
                act.wait_ge(ml_num, N_X)
                act.dma_start(w_st[:, :], d["w_st"]).then_inc(ws_in, 16)

            def headnorm(st):
                for k in range(KT):
                    act.wait_ge(hn_c, k + 1)
                    if k >= 2:
                        act.wait_ge(hn_var, k - 1)
                    nc.scalar.activation(sq[k % 2][:, :], buf[3][:, k * S:(k + 1) * S], ACT.Square).then_inc(hn_sq, 1)
                act.wait_ge(hn_v, HM)
                nc.scalar.activation(h_rstd[:, :], h_rstd[:, :], ACT.Sqrt).then_inc(hn_std, 1)

            def sgu(st):
                for n in range(S // CH):
                    act.wait_ge(sg_t, n + 1)
                    if n >= 2:
                        act.wait_ge(sg_m, n - 1)
                    for h in range(2):
                        ins = nc.scalar.activation(v_nat[n % 2][:, h * 512:(h + 1) * 512], bank[n % 2 * 2 + h][:, :], ACT.Copy)
                    ins.then_inc(sg_v, 1)

            def fgates(st):
                act.wait_ge(bank_free, st["units"])
                act.dma_start(hctx[:, :].rearrange("p (k n) -> p k n", n=C),
                              d["mem"].rearrange("(k p) n -> p k n", p=P)).then_inc(mem_in, 16)
                act.wait_ge(fg_pre, 1)
                nc.scalar.activation(flt[:, :], fl[:, :], ACT.Abs).then_inc(fg_ln, 1)
                act.wait_ge(fg_ln, 1)
                nc.scalar.activation(flt[:, :], flt[:, :], ACT.Exp, scale=-1.0).then_inc(fg_ln, 1)
                act.wait_ge(fg_ln, 2)
                nc.scalar.activation(flt[:, :], flt[:, :], ACT.Ln, bias=1.0).then_inc(fg_ln, 1)

            def softmax_attention(st):
                n0, n1 = ATT[st["stage"]]
                for n in range(n0, n1 + 2):
                    if n < n1:
                        act.wait_ge(at_max, n + 1)
                        if n >= 3:
                            act.wait_ge(at_tr, n - 2)
                        T = keys_of(n)
                        nc.scalar.activation(p_nat[n % 3][:, 0:T], bank[n % 3][:, 0:T], ACT.Exp, bias=neg_max[:, n:n + 1],
                                             accum_out=p_sum[:, n:n + 1]).then_inc(at_exp, 1)
                    if n - 2 >= n0:
                        m = n - 2
                        h, i = att_steps[m]
                        act.wait_ge(at_tr, m + 1)
                        if i == 0 and h >= 2:
                            act.wait_ge(at_pv, h - 1)
                        T = keys_of(m)
                        to = p_t[h % 2][:, :].rearrange("p (j t) -> p j t", t=S)[:, 0:T // CH, i * CH:(i + 1) * CH]
                        nc.scalar.activation(to, bank[3 + m % 2][:, 0:T].rearrange("p (j t) -> p j t", t=CH), ACT.Copy)\
                            .then_inc(at_copy, 1)

            def sb(st):
                def logs(h):
                    s, sp = h % 2, sp_a[h % 3]
                    act.wait_ge(sb_z, h + 1)
                    if h >= 3:
                        act.wait_ge(sb_pv, h - 2)
                    for b, T in enumerate(SB_BANKS):
                        nc.scalar.activation(sp[:, b * S:b * S + T], bank[3 * s + b][:, 0:T], ACT.Abs).then_inc(sb_abs, 1)
                    act.wait_ge(sb_abs, 3 * h + 3)
                    nc.scalar.activation(sp[:, :], sp[:, :], ACT.Exp, scale=-1.0).then_inc(sb_e, 1)
                    act.wait_ge(sb_e, h + 1)
                    nc.scalar.activation(sp[:, :], sp[:, :], ACT.Ln, bias=1.0).then_inc(sb_ln, 1)

                def weights(h):
                    s = h % 2
                    act.wait_ge(sb_cum, h + 1)
                    for b, T in enumerate(SB_BANKS):
                        ins = nc.scalar.activation(sp_a[h % 3][:, b * S:b * S + T], bank[3 * s + b][:, 0:T], ACT.Exp)
                    ins.then_inc(sb_a, 1)

                for h in range(HA + 1):
                    if h < HA:
                        logs(h)
                    if h:
                        weights(h - 1)

            ACT_STAGE = {"gates": gates, "mlstm": mlstm, "headnorm": headnorm, "sgu": sgu, "fgates": fgates, "fox": softmax_attention, "sb": sb,
                         "xattn": softmax_attention}
            heads(0, 0, 1)
            for st in stages:
                if isinstance(st, Phase):
                    gemm(st)
                elif isinstance(st, Norm):
                    norm(st)
                else:
                    ACT_STAGE[st["stage"]](st)

        @block.tensor
        def _(pe):
            def gemm(ph):
                for s, value in ph.more.get("after", ()):
                    pe.wait_ge(s, value)

                def unit(k, slot):
                    u = k + ph.base
                    pe.wait_ge(lo_ready, u + 1)
                    if not isinstance(u, int) or u >= 2:
                        pe.wait_ge(bank_free, u - 1)
                    first = isinstance(k, int) and k == 0 and ph.wait_for

                    def input_ready(kt):
                        if first and ph.wait_for[0] == "norm":
                            pe.wait_ge(xn_ready, ph.wait_for[1] + kt + 1)
                        elif first:
                            pe.wait_ge(bank_free, ph.wait_for[1] + kt // ph.wait_for[2] + 1)

                    if ph.natural:
                        for seg in ph.segs:
                            head, rest, stride = inputs(ph.x, seg)
                            for ch in range(TOKENS[seg] // P):
                                to = bank[3 * slot + 2 * (seg == "ctx") + ch // 2][:, (ch % 2) * 256:(ch % 2 + 1) * 256]
                                for kt in range(ph.kts):
                                    if ch == 0 and seg == ph.segs[0]:
                                        input_ready(kt)
                                    xs = slice(kt * stride + ch * P, kt * stride + (ch + 1) * P)
                                    ws = slice(kt * 256, (kt + 1) * 256)
                                    pe.matmul(to, head[:, xs], w_h[slot][:, ws], start=(kt == 0), stop=False)
                                    pe.matmul(to, rest[:, xs], w_h[slot][:, ws], start=False, stop=False)
                                    ins = pe.matmul(to, head[:, xs], w_l[slot][:, ws], start=False,
                                                    stop=(kt == ph.kts - 1))
                    else:
                        for kt in range(ph.kts):
                            input_ready(kt)
                            for n in range(2):
                                ws = slice(kt * 256 + n * P, kt * 256 + (n + 1) * P)
                                for w, part in ((w_h, 0), (w_h, 1), (w_l, 0)):
                                    for seg in ph.segs:
                                        x = inputs(ph.x, seg)
                                        xs = slice(kt * x[2], kt * x[2] + TOKENS[seg])
                                        opens = kt == 0 and w is w_h and part == 0 and not (seg == "ctx" and n)
                                        ins = pe.matmul(banks(slot, seg)[n], w[slot][:, ws], x[part][:, xs],
                                                        start=opens, stop=(kt == ph.kts - 1 and w is w_l),
                                                        skip_group_check=(seg == "ctx"))
                    ins.then_inc(mm_done, 1)

                run_units(pe, ph, unit, peel=1 if ph.wait_for else 0)

            def norm(n):
                for k in range(n.tiles):
                    t = n.tile_base + k
                    pe.wait_ge(sq_ready, t + 1)
                    if k == 0 and n.index:
                        pe.wait_ge(var_ready, n.index)
                    pe.matmul(bank[SUMS][:, 0:n.tokens], const("ones"), sq[t % 2][:, 0:n.tokens], start=(k == 0),
                              stop=(k == n.tiles - 1)).then_inc(sq_used, 1)

            pe.wait_ge(c_ready, 1)

            def ada_unit(u, slot, count):
                pe.wait_ge(ada_in[slot], count * 16)
                if not isinstance(u, int) or u >= 4:
                    pe.wait_ge(ada_taken, u - 3)
                for kt in range(KT):
                    ins = pe.matmul(bank[slot][0:2, :], silu_c[:, kt * 2:kt * 2 + 2],
                                    buf[ada_slots[slot]][:, kt * 512:(kt + 1) * 512], start=(kt == 0),
                                    stop=(kt == KT - 1))
                ins.then_inc(ada_mm, 1)

            def ada_turn(u, slot):
                pe.wait_ge(ada_row, u + 1)
                for n in range(4):
                    ins = pe.matmul(bank[4 + slot][:, n * 2:n * 2 + 2], ada_rows[slot][0:2, n * P:(n + 1) * P],
                                    const("ident")[0:2, 0:2], start=True, stop=True)
                ins.then_inc(ada_turned, 1)

            pe.wait_ge(const_in, 16)
            for u in range(4):
                ada_unit(u, u, 1)
                if u:
                    ada_turn(u - 1, u - 1)
            with pe.Fori(1, N_ADA // 4) as i:
                for j in range(4):
                    ada_unit(i * 4 + j, j, i + 1)
                    ada_turn(i * 4 + (j - 1), (j - 1) % 4)
            for u in range(N_ADA // 4 * 4, N_ADA):
                ada_unit(u, u % 4, u // 4 + 1)
                ada_turn(u - 1, (u - 1) % 4)
            ada_turn(N_ADA - 1, (N_ADA - 1) % 4)
            pe.wait_ge(ada_taken, N_ADA)
            def one_hot(n, r):
                return const("ident")[0:n, r:r + 1].to_broadcast([n, P])

            def gates(st):
                pe.wait_ge(gate_in, 32)
                for g in range(NG):
                    seg, ch = ("ctx", g) if g < 2 else ("x", g - 2)
                    head, rest, stride = inputs("xn", seg)
                    for kt in range(KT):
                        for part in (head, rest):
                            xs = part[:, kt * stride + ch * CH:kt * stride + (ch + 1) * CH].bitcast(F32)
                            ins = pe.matmul(bank[7][:, g * 16:(g + 1) * 16], xs, gate_w[:, kt * 16:(kt + 1) * 16],
                                            start=(kt == 0 and part is head), stop=(kt == KT - 1 and part is rest))
                ins.then_inc(gates_mm, 1)
                pe.wait_ge(lf_ready, 1)
                pe.wait_ge(bank_free, st["units"])
                pe.matmul(bank[5][:, 0:32], const("neg_le"), lf[:, 0:32], start=True, stop=True)
                pe.matmul(bank[5][:, 32:64], const("neg_ge"), lf[:, 32:64], start=True, stop=True)
                pe.matmul(bank[5][:, 64:128], const("ones"), lf[:, :], start=True, stop=True).then_inc(sums_mm, 1)
                pe.wait_ge(a_ready, 1)
                pe.transpose(bank[4][0:64, 0:CH], a_col[:, :], const("ident"))
                pe.transpose(bank[4][0:64, CH:2 * CH], neg_b[:, :], const("ident")).then_inc(rows_mm, 1)
                pe.wait_ge(diag_ready, 1)
                pe.matmul(bank[5][:, 0:64], const("ones")[0:64, :], diag[0:64, :], start=True, stop=True).then_inc(last_mm, 1)

            def mlstm(st):
                def key(g, ct):
                    if g < 2:
                        return kc[:, ct * C + g * CH:ct * C + (g + 1) * CH]
                    return buf[1][:, ct * S + (g - 2) * CH:ct * S + (g - 1) * CH]

                def chain_state(di, e, kk, a, b):
                    o = ((di * HM + e) * 2 + kk) * (DHM + 1)
                    return state[:, o + a:o + b]

                def keys_by_token(w):
                    pos, di, e = ml_steps[w]
                    if w >= 2:
                        pe.wait_ge(ml_kn, w - 1)
                    for kk in range(2):
                        ins = pe.transpose(bank[2 + w % 2][:, kk * CH:(kk + 1) * CH], key(chunk_of[di][pos], e * 2 + kk),
                                           const("ident"))
                    ins.then_inc(ml_kt, 1)

                def scores(j):
                    pos, di, e = ml_steps[N_CTX + j]
                    g = chunk_of[di][pos]
                    if j >= 2:
                        pe.wait_ge(ml_p, j - 1)
                    pe.matmul(bank[j % 2][:, 0:2 * CH], one_hot(64, gcol(di, g, e)), rows[0:64, :], start=True, stop=True)
                    for kk in range(2):
                        ct = e * 2 + kk
                        ins = pe.matmul(bank[j % 2][:, 2 * CH:3 * CH], key(g, ct),
                                        buf[0][:, ct * S + (g - 2) * CH:ct * S + (g - 1) * CH], start=(kk == 0), stop=(kk == 1))
                    ins.then_inc(ml_a, 1)

                def outputs(j):
                    pos, di, e = ml_steps[N_CTX + j]
                    g, s = chunk_of[di][pos], j % 2
                    pe.wait_ge(ml_p, j + 1)
                    pe.wait_ge(ml_q, j + 1)
                    if j >= 2:
                        pe.wait_ge(ml_h, j - 1)
                    to = bank[4 + s]
                    for vv in range(2):
                        o = (g - 2) * D + e * DHM + vv * CH
                        pe.matmul(to[:, vv * CH:(vv + 1) * CH], buf[2][:, o:o + CH], p_st[s][:, :], start=True, stop=False)
                        for kk in range(2):
                            pe.matmul(to[:, vv * CH:(vv + 1) * CH], chain_state(di, e, kk, vv * CH, (vv + 1) * CH),
                                      q_int[s][:, kk * CH:(kk + 1) * CH], start=False, stop=(kk == 1))
                    pe.matmul(to[:, 2 * CH:3 * CH], const("ones"), p_st[s][:, :], start=True, stop=False)
                    for kk in range(2):
                        ins = pe.matmul(to[:, 2 * CH:3 * CH], n_bc[s][:, kk * CH:(kk + 1) * CH],
                                        q_int[s][:, kk * CH:(kk + 1) * CH], start=False, stop=(kk == 1))
                    ins.then_inc(ml_num, 1)

                def update(w):
                    pe.wait_ge(ml_kn, w + 1)
                    taken = w - 1 if w < N_CTX else w
                    if taken > 0:
                        pe.wait_ge(ml_st, taken)
                    for kk in range(2):
                        ins = pe.matmul(update_bank(w, kk), k_nat[w % 2][:, kk * CH:(kk + 1) * CH], wv[w % 2][:, :],
                                        start=True, stop=True)
                    ins.then_inc(ml_upd, 1)

                pe.wait_ge(conv_out, st["outs"])
                pe.wait_ge(ws_ready, 1)
                for w in range(N_CTX + 1):
                    if w < N_CTX:
                        keys_by_token(w)
                    if w:
                        update(w - 1)
                for j in range(N_X + 1):
                    w = N_CTX + j
                    if j < N_X:
                        scores(j)
                        if w < N_UPD:
                            keys_by_token(w)
                    if j:
                        outputs(j - 1)
                        if w - 1 < N_UPD:
                            update(w - 1)

            def headnorm(st):
                pe.wait_ge(ml_h, N_X)
                for e in range(HM):
                    for i in range(2):
                        ct = e * 2 + i
                        ins = pe.matmul(bank[e][:, :], const("ones"), buf[3][:, ct * S:(ct + 1) * S], start=(i == 0), stop=(i == 1))
                    ins.then_inc(hn_mu, 1)
                for k in range(KT):
                    pe.wait_ge(hn_sq, k + 1)
                    pe.matmul(bank[4 + k // 2][:, :], const("ones"), sq[k % 2][:, :], start=(k % 2 == 0), stop=(k % 2 == 1))\
                        .then_inc(hn_var, 1)

            def sgu(st):
                def turn(n):
                    if n >= 2:
                        pe.wait_ge(sg_v, n - 1)
                    for ct in range(KT):
                        ins = pe.transpose(bank[n % 2 * 2 + ct // 4][:, ct % 4 * CH:(ct % 4 + 1) * CH],
                                           buf[1][:, ct * S + n * CH:ct * S + (n + 1) * CH], const("ident"))
                    ins.then_inc(sg_t, 1)

                def mix(n):
                    pe.wait_ge(sg_v, n + 1)
                    if n >= 2:
                        pe.wait_ge(sg_y, n - 1)
                    for ct in range(KT):
                        to, g = bank[4 + n % 2 * 2 + ct // 4][:, ct % 4 * CH:(ct % 4 + 1) * CH], ct // 2
                        pe.matmul(to, v_nat[n % 2][:, ct * CH:(ct + 1) * CH], w_st[:, g * CH:(g + 1) * CH], start=True, stop=False)
                        ins = pe.matmul(to, one_hot(4, g), b_s[0:4, :], start=False, stop=True)
                    ins.then_inc(sg_m, 1)

                pe.wait_ge(xn_ready, st["ntiles"])
                pe.wait_ge(ws_in, 16)
                pe.wait_ge(bs_in, 16)
                for n in range(S // CH + 1):
                    if n < S // CH:
                        turn(n)
                    if n:
                        mix(n - 1)

            def fgates(st):
                pe.wait_ge(wf_in, 32)
                pe.wait_ge(xn_ready, st["ntiles"])
                for c in range(S // CH):
                    for kt in range(KT):
                        for part in (xn_h, xn_l):
                            xs = part[:, kt * S + c * CH:kt * S + (c + 1) * CH].bitcast(F32)
                            ins = pe.matmul(bank[7][:, c * HA:(c + 1) * HA], xs, wf[:, kt * HA:(kt + 1) * HA],
                                            start=(kt == 0 and part is xn_h), stop=(kt == KT - 1 and part is xn_l))
                ins.then_inc(fg_mm, 1)

            def softmax_attention(st):
                n0, n1 = ATT[st["stage"]]

                def logits(n):
                    h, i = att_steps[n]
                    T = keys_of(n)
                    to = bank[n % 3][:, 0:T]
                    if n >= 3:
                        pe.wait_ge(at_exp, n - 2)
                    if h < HA:
                        pair, half = h // 2, slice(h % 2 * DHA, (h % 2 + 1) * DHA)
                        pe.matmul(to, fq[half, pair * S + i * CH:pair * S + (i + 1) * CH], fk[half, pair * S:pair * S + T],
                                  start=True, stop=False)
                        pe.matmul(to, one_hot(HA, h), crow[0:HA, 0:T], start=False, stop=False)
                        ins = pe.matmul(bank[n % 3][:, T - CH:T], const("ident"), const("npen_ge"), start=False, stop=True)
                    else:
                        for kk in range(DHX // P):
                            ct = (h - HA) * (DHX // P) + kk
                            ins = pe.matmul(to, buf[3][:, ct * S + i * CH:ct * S + (i + 1) * CH], mem_k[:, ct * C:(ct + 1) * C],
                                            start=(kk == 0), stop=(kk == DHX // P - 1))
                    ins.then_inc(at_logits, 1)

                def turn(n):
                    pe.wait_ge(at_p, n + 1)
                    if n >= 2:
                        pe.wait_ge(at_copy, n - 1)
                    for j in range(keys_of(n) // CH):
                        ins = pe.transpose(bank[3 + n % 2][:, j * CH:(j + 1) * CH], p_nat[n % 3][:, j * CH:(j + 1) * CH],
                                           const("ident"))
                    ins.then_inc(at_tr, 1)

                def values(h):
                    pe.wait_ge(at_copy, (h + 1) * NQ)
                    if h < HA:
                        if h >= 2:
                            pe.wait_ge(at_out, h - 1)
                        for j in range(NQ):
                            vs = fv[:, j * W2 + h // 2 * P:j * W2 + (h // 2 + 1) * P]
                            ins = pe.matmul(bank[5 + h % 2][:, j * CH:S], vs, p_t[h % 2][:, j * S + j * CH:(j + 1) * S],
                                            start=(j == 0), stop=(j == NQ - 1))
                    else:
                        pe.wait_ge(at_out, h)
                        for n in range(DHX // P):
                            for j in range(C // CH):
                                o = j * D + (h - HA) * DHX + n * P
                                ins = pe.matmul(bank[5 + n][:, :], mem_v[:, o:o + P], p_t[h % 2][:, j * S:(j + 1) * S],
                                                start=(j == 0), stop=(j == C // CH - 1))
                    ins.then_inc(at_pv, 1)

                pe.wait_ge(bank_free, st["units"])
                if n0 == 0:
                    pe.wait_ge(fg_lf, 1)
                    for c in range(NQ):
                        for b in range(c + 1):
                            ins = pe.matmul(bank[7][0:HA, c * CH:(c + 1) * CH], fl[:, b * HA:(b + 1) * HA],
                                            const("neg_le" if b == c else "neg_ones"), start=(b == 0), stop=(b == c))
                    ins.then_inc(fg_rows, 1)
                    pe.wait_ge(fg_crow, 1)
                for n in range(n0, n1 + 3):
                    if n < n1:
                        logits(n)
                    if n0 <= n - 2 < n1:
                        turn(n - 2)
                    for h in heads_after(n - 3, n0):
                        values(h)

            def sb(st):
                def scores(h):
                    s, half = h % 2, slice(h % 2 * DHA, (h % 2 + 1) * DHA)
                    if h >= 2:
                        pe.wait_ge(sb_a, h - 1)
                    for j in range(NQ):
                        b, c = SB_AT[j]
                        o = h // 2 * S + j * CH
                        ins = pe.matmul(bank[3 * s + b][:, c:c + SB_WIDTH(j)], sk[half, o:o + CH],
                                        sq_t[half, o:(h // 2 + 1) * S], start=(c == 0), stop=True, skip_group_check=True)
                    ins.then_inc(sb_z, 1)

                def sums(h):
                    s = h % 2
                    pe.wait_ge(sb_sp, h + 1)
                    for j in range(NQ):
                        b, c = SB_AT[j]
                        W = SB_WIDTH(j)
                        for jj in range(j, NQ):
                            pe.matmul(bank[3 * s + b][:, c + W - SB_WIDTH(jj):c + W], const("neg_ge" if jj == j else "neg_ones"),
                                      sb_part(sp_a[h % 3], jj), start=False, stop=False, skip_group_check=True)
                        ins = pe.matmul(bank[3 * s + b][:, c:c + CH], const("ident"), const("npen_lt"), start=False, stop=True,
                                        skip_group_check=True)
                    ins.then_inc(sb_cum, 1)

                def values(h):
                    pe.wait_ge(sb_a, h + 1)
                    if h >= 2:
                        pe.wait_ge(sb_out, h - 1)
                    for j in range(NQ):
                        vs = sv[:, j * W2 + h // 2 * P:j * W2 + (h // 2 + 1) * P]
                        ins = pe.matmul(bank[6 + h % 2][:, j * CH:S], vs, sb_part(sp_a[h % 3], j), start=(j == 0),
                                        stop=(j == NQ - 1))
                    ins.then_inc(sb_pv, 1)

                pe.wait_ge(at_out, HA)
                scores(0)
                for h in range(HA + 1):
                    if h + 1 < HA:
                        scores(h + 1)
                    if h < HA:
                        sums(h)
                    if h:
                        values(h - 1)

            PE_STAGE = {"gates": gates, "mlstm": mlstm, "headnorm": headnorm, "sgu": sgu, "fgates": fgates, "fox": softmax_attention, "sb": sb,
                         "xattn": softmax_attention}
            for st in stages:
                if isinstance(st, Phase):
                    gemm(st)
                elif isinstance(st, Norm):
                    norm(st)
                else:
                    PE_STAGE[st["stage"]](st)

        @block.vector
        def _(dve):
            steps = [0]

            def then(ins):
                steps[0] += 1
                ins.then_inc(chain, 1)
                dve.wait_ge(chain, steps[0])

            def gemm(ph):
                def unit(k, slot):
                    u = k + ph.base
                    own = lambda i: k * ph.own_steps + (ph.own_base + i)
                    if ph.act_steps:
                        dve.wait_ge(act_out, k * ph.act_steps + (ph.act_base + 1))
                    else:
                        dve.wait_ge(mm_done, u + 1)

                    def split(fulls, where, done):
                        count = len(fulls)
                        for i, (full, (head, rest)) in enumerate(zip(fulls, where)):
                            dve.wait_ge(dve_step, own(done + i + 1))
                            nc.vector.tensor_copy(head, full).then_inc(dve_step, 1)
                        for i, (full, (head, rest)) in enumerate(zip(fulls, where)):
                            dve.wait_ge(dve_step, own(done + count + i + 1))
                            ins = nc.vector.tensor_tensor(rest, full, head.bitcast(F32), ALU.subtract)
                        ins.then_inc(bank_free, 1)

                    def hidden(seg, i):
                        head, rest, stride = inputs("hid", seg)
                        return tile(head, i, TOKENS[seg], stride), tile(rest, i, TOKENS[seg], stride)

                    if ph.kind == "swiglu":
                        fulls = []
                        for seg, s, t in zip(ph.segs, (sq, sqc), (tmp, tmpc)):
                            fulls.append(t[slot][:, 0:TOKENS[seg]])
                            nc.vector.tensor_tensor(fulls[-1], s[slot][:, 0:TOKENS[seg]], banks(slot, seg)[1],
                                                    ALU.mult).then_inc(dve_step, 1)
                        split(fulls, [hidden(seg, k) for seg in ph.segs], 0)
                    elif ph.kind == "convswiglu":
                        b = banks(slot, "x")
                        y = (sq[slot], conv_b[slot])
                        tap = lambda n, w: vcol("conv_w_2", k + (n * FT + ph.more["f0"] + 2 * FT * w))
                        for back in (1, 2):
                            for n in range(2):
                                if back == 2:
                                    dve.wait_ge(dve_step, own(n + 1))
                                nc.vector.scalar_tensor_tensor(y[n][:, back:S], b[n][:, 0:S - back], tap(n, 2 - back),
                                                               y[n][:, back:S], ALU.mult, ALU.add)\
                                    .then_inc(dve_step, 1)
                        dve.wait_ge(dve_step, own(4))
                        dve.wait_ge(act_out, k * 2 + (ph.act_base + 2))
                        nc.vector.tensor_tensor(tmp[slot][:, :], y[0][:, :], y[1][:, :], ALU.mult).then_inc(dve_step, 1)
                        split([tmp[slot][:, :]], [hidden("x", k)], 4)
                    elif ph.kind == "resid":
                        for seg, gate in zip(ph.segs, ph.more["gates"]):
                            h, stride = residual[seg]
                            for n in range(2):
                                to, b = tile(h, k * 2 + n, TOKENS[seg], stride), banks(slot, seg)[n]
                                if gate:
                                    ins = nc.vector.scalar_tensor_tensor(to, b, dcol(gate, k * 2 + n), to, ALU.mult,
                                                                         ALU.add)
                                else:
                                    ins = nc.vector.tensor_tensor(to, b, to, ALU.add)
                        ins.then_inc(bank_free, 1)
                    elif ph.kind == "convqk":
                        tap = lambda n, w: vcol("conv_qk_w", k * 2 + (n + ph.more["c0"] + 2 * KT * w))
                        todo = [(y[n], banks(slot, seg)[n], n, TOKENS[seg])
                                for seg, y in zip(ph.segs, (sq, yc)) for n in range(2)]
                        for y, b, n, T in todo:
                            nc.vector.scalar_tensor_tensor(y[:, 1:T], b[:, 0:T - 1], tap(n, 0), y[:, 1:T],
                                                           ALU.mult, ALU.add).then_inc(dve_step, 1)
                        for i, (y, b, n, T) in enumerate(todo):
                            dve.wait_ge(dve_step, own(i + 1))
                            ins = nc.vector.scalar_tensor_tensor(y[:, 0:T - 1], b[:, 1:T], tap(n, 2), y[:, 0:T - 1],
                                                                 ALU.mult, ALU.add).then_inc(dve_step, 1)
                        dve.wait_ge(dve_step, own(2 * len(todo)))
                        dve.wait_ge(bank_free, u)
                        dve.sem_inc(bank_free, 1)
                    elif ph.kind == "sig_mul":
                        dve.wait_ge(bank_free, u)
                        fulls = [tmp[n][:, :] for n in range(2)]
                        for n in range(2):
                            nc.vector.tensor_tensor(fulls[n], sq[n][:, :], tile(ph.more["by"], k * 2 + n), ALU.mult)\
                                .then_inc(dve_step, 1)
                        split(fulls, [hidden("x", k * 2 + n) for n in range(2)], 0)
                    elif ph.kind == "mixb":
                        dve.wait_ge(bank_free, u)
                        fulls = [tmp[n][:, :] for n in range(2)]
                        for n in range(2):
                            nc.vector.tensor_tensor(fulls[n], banks(slot, "x")[n], tile(ph.more["by"], k * 2 + n),
                                                    ALU.mult).then_inc(dve_step, 1)
                        for n in range(2):
                            dve.wait_ge(dve_step, own(n + 1))
                            nc.vector.tensor_tensor(fulls[n], fulls[n], tile(ph.more["plus"], k * 2 + n), ALU.add)\
                                .then_inc(dve_step, 1)
                        split(fulls, [hidden("x", k * 2 + n) for n in range(2)], 2)
                    elif ph.kind == "func":
                        dve.wait_ge(bank_free, u)
                        dve.sem_inc(bank_free, 1)
                    elif ph.kind == "mul":
                        for n in range(2):
                            to = tile(ph.more["dst"], k * 2 + n)
                            ins = nc.vector.tensor_tensor(to, banks(slot, "x")[n], to, ALU.mult)
                        ins.then_inc(bank_free, 1)
                    elif ph.kind == "store":
                        for n in range(2):
                            ins = nc.vector.tensor_scalar(ph.more["dst"](k * 2 + n), banks(slot, ph.segs[0])[n],
                                                          ph.more["scale"], None, ALU.mult)
                        ins.then_inc(bank_free, 1)
                    elif ph.kind == "natstore":
                        for seg in ph.segs:
                            for n in range(TOKENS[seg] // 256):
                                b = bank[3 * slot + 2 * (seg == "ctx") + n]
                                ins = nc.vector.tensor_copy(ph.more["dst"][seg](2 * n, k),
                                                            b[:, :].rearrange("p (c w) -> p c w", w=256))
                        ins.then_inc(bank_free, 1)

                run_units(dve, ph, unit)

            def norm(n):
                T = n.tokens
                dve.wait_ge(sq_used, n.tile_base + n.tiles)
                nc.vector.tensor_scalar(rstd[:, 0:T], bank[SUMS][:, 0:T], 1.0 / (n.tiles * P), EPS, ALU.mult, ALU.add)\
                    .then_inc(var_ready, 1)
                dve.wait_ge(std_ready, n.index + 1)
                nc.vector.reciprocal(rstd[:, 0:T], rstd[:, 0:T]).then_inc(rstd_ready, 1)
                dve.wait_ge(rstd_ready, n.index + 1)
                if n.out != "split":
                    for k in range(n.tiles):
                        nc.vector.scalar_tensor_tensor(n.src(k), n.src(k), n.gain(k), rstd[:, 0:T], ALU.mult,
                                                       ALU.mult).then_inc(xn_ready, 1)
                    return
                for k in range(n.tiles + 1):
                    if k < n.tiles:
                        if k >= 2 or n.tile_base:
                            dve.wait_ge(xn_ready, n.tile_base + max(k - 1, 0))
                        nc.vector.scalar_tensor_tensor(tmp[k % 2][:, 0:T], n.src(k), n.gain(k), rstd[:, 0:T],
                                                       ALU.mult, ALU.mult).then_inc(scaled, 1)
                    if k:
                        dve.wait_ge(xh_ready, n.split_base + k)
                        head, rest, stride = inputs("xn", n.seg)
                        o = (n.out_tile + k - 1) * stride
                        head, rest, full = head[:, o:o + T], rest[:, o:o + T], tmp[(k - 1) % 2][:, 0:T]
                        if n.shift:
                            ins = nc.vector.scalar_tensor_tensor(rest, full, dcol(n.shift, k - 1), head.bitcast(F32),
                                                                 ALU.add, ALU.subtract)
                        else:
                            ins = nc.vector.tensor_tensor(rest, full, head.bitcast(F32), ALU.subtract)
                        ins.then_inc(xn_ready, 1)

            dve.wait_ge(x_in, 32)
            nc.vector.tensor_tensor(resid[:, :], resid[:, :], buf[2][:, :], ALU.add).then_inc(pos_added, 1)
            dve.wait_ge(vec_in, 16)

            def ada_unit(u, slot):
                dve.wait_ge(ada_turned, u + 1)
                bias = vec[:, bass.ds(u * 4 + VCOL["b_ada"], 4)].unsqueeze(2).to_broadcast([P, 4, 2])
                nc.vector.tensor_tensor(mods[:, bass.ds(u * 8, 8)].rearrange("p (j w) -> p j w", w=2),
                                        bank[4 + slot][:, 0:8].rearrange("p (j w) -> p j w", w=2),
                                        bias, ALU.add).then_inc(ada_taken, 1)

            def ada_take(u, slot):
                dve.wait_ge(ada_mm, u + 1)
                nc.vector.tensor_copy(ada_rows[slot][0:2, :], bank[slot][0:2, :]).then_inc(ada_row, 1)

            for u in range(4):
                ada_take(u, u)
                if u:
                    ada_unit(u - 1, u - 1)
            with dve.Fori(1, N_ADA // 4) as i:
                for j in range(4):
                    ada_take(i * 4 + j, j)
                    ada_unit(i * 4 + (j - 1), (j - 1) % 4)
            for u in range(N_ADA // 4 * 4, N_ADA):
                ada_take(u, u % 4)
                ada_unit(u - 1, (u - 1) % 4)
            ada_unit(N_ADA - 1, (N_ADA - 1) % 4)
            dve.wait_ge(ada_taken, N_ADA)
            mod = lambda j, w: mods[:, :].rearrange("p (j k w) -> p j k w", j=NMOD, w=2)[:, j, :, w]
            dst = lambda name: der[:, DER.index(name) * KT:(DER.index(name) + 1) * KT]
            gains = {"1": "g_ffn1", "2": "g_mix", "3": "g_ffn2"}
            for name in DER:
                w, j = int(name.startswith("ctx")), 3 * int(name[-1]) - 3
                what = name[-3:-1]
                if what == "gs":
                    g = VCOL[gains[name[-1]]]
                    ins = nc.vector.scalar_tensor_tensor(dst(name), mod(j + 1, w), 1.0, vec[:, g:g + KT], ALU.add,
                                                         ALU.mult)
                elif what == "sh":
                    ins = nc.vector.tensor_copy(dst(name), mod(j, w))
                else:
                    ins = nc.vector.tensor_scalar(dst(name), mod(j + 2, w), 1.0 if name[-1] == "2" else 0.5, None,
                                                  ALU.mult)
                then(ins)
            def gates(st):
                dve.wait_ge(gates_mm, 1)
                dve.wait_ge(gate_in, 32)
                then(nc.vector.memset(lf[:, :], 0.0))
                then(nc.vector.memset(li[:, :], 0.0))
                pre = bank[7][:, 0:NG * 16].rearrange("p (g n) -> p g n", n=16)
                for di in range(2):
                    for to, typ in ((li, 0), (lf, 1)):
                        o = di * 2 * HM + typ * HM
                        view = to[:, di * 32:di * 32 + NG * HM].rearrange("p (g e) -> p g e", e=HM)
                        bias = gate_b[:, o:o + HM].unsqueeze(1).to_broadcast([P, NG, HM])
                        then(nc.vector.tensor_tensor(view, pre[:, :, o:o + HM], bias, ALU.add))
                dve.sem_inc(f_ready, 1)
                dve.wait_ge(ln_ready, 2)
                nc.vector.scalar_tensor_tensor(lf[:, :], lf[:, :], 0.0, lt[:, :], ALU.min, ALU.subtract).then_inc(lf_ready, 1)
                dve.wait_ge(sums_mm, 1)
                then(nc.vector.tensor_copy(neg_b[:, :], bank[5][:, 0:64]))
                then(nc.vector.tensor_copy(total[:, :], bank[5][:, 64:128]))
                nc.vector.tensor_tensor(a_col[:, :], li[:, :], neg_b[:, :], ALU.add).then_inc(a_ready, 1)
                dve.wait_ge(rows_mm, 1)
                then(nc.vector.tensor_copy(rows_in[0:64, :], bank[4][0:64, 0:2 * CH]))
                then(nc.vector.tensor_copy(rows[0:64, CH:2 * CH], rows_in[0:64, CH:2 * CH]))
                fw, bw = rows_in[0:32, 0:CH], rows_in[32:64, 0:CH][:, ::-1]
                then(nc.vector.tensor_tensor_scan(rows[0:32, 0:CH], fw, fw, -BIG, ALU.max, ALU.max))
                then(nc.vector.tensor_tensor_scan(rows[32:64, 0:CH][:, ::-1], bw, bw, -BIG, ALU.max, ALU.max))
                then(nc.vector.tensor_scalar(diag[0:32, :], const("ident")[0:32, 0:64], rows[0:32, CH - 1:CH], None, ALU.mult))
                nc.vector.tensor_scalar(diag[32:64, :], const("ident")[32:64, 0:64], rows[32:64, 0:1], None, ALU.mult)\
                    .then_inc(diag_ready, 1)
                dve.wait_ge(last_mm, 1)
                then(nc.vector.tensor_copy(cm_last[:, :], bank[5][:, 0:64]))
                then(nc.vector.memset(m_in[:, :], 0.0))
                then(nc.vector.tensor_copy(m_end[:, :], cm_last[:, :]))
                for pos in range(NG):
                    for di in range(2):
                        c = gcol(di, chunk_of[di][pos], 0)
                        then(nc.vector.tensor_tensor(m_end[:, c:c + HM], m_in[:, c:c + HM], cm_last[:, c:c + HM], ALU.max))
                        if pos < NG - 1:
                            t = gcol(di, chunk_of[di][pos + 1], 0)
                            then(nc.vector.tensor_tensor(m_in[:, t:t + HM], m_end[:, c:c + HM], total[:, c:c + HM], ALU.add))
                nc.vector.tensor_tensor(decay_ws[:, 0:64], m_in[:, :], m_end[:, :], ALU.subtract)
                nc.vector.tensor_tensor(decay_ws[:, 64:128], a_col[:, :], m_end[:, :], ALU.subtract).then_inc(diff_ready, 1)

            def mlstm(st):
                def chain_state(di, e):
                    o = (di * HM + e) * 2 * (DHM + 1)
                    return state[:, o:o + 2 * (DHM + 1)].rearrange("p (k n) -> p k n", k=2)

                def maxima(j):
                    pos, di, e = ml_steps[N_CTX + j]
                    c, s = gcol(di, chunk_of[di][pos], e), j % 2
                    m = m_in[:, c:c + 1]
                    dve.wait_ge(ml_a, j + 1)
                    if j >= 2:
                        dve.wait_ge(ml_p, j - 1)
                        dve.wait_ge(ml_q, j - 1)
                    if j >= 3:
                        dve.wait_ge(ml_h, j - 2)
                    then(nc.vector.tensor_scalar(m_inter[s][:, :], bank[s][:, 0:CH], m, None, ALU.max))
                    nc.vector.scalar_tensor_tensor(pen_d[s][:, :], bank[s][:, 0:CH], m, const(("npen_le", "npen_ge")[di]),
                                                   ALU.max, ALU.subtract)
                    nc.vector.tensor_tensor(emt[j % 3][:, :], bank[s][:, CH:2 * CH], m_inter[s][:, :], ALU.subtract)\
                        .then_inc(ml_row, 1)

                def weigh(j):
                    pos, di, e = ml_steps[N_CTX + j]
                    g, s = chunk_of[di][pos], j % 2
                    dve.wait_ge(ml_exp, j + 1)
                    if j >= 2:
                        dve.wait_ge(ml_num, j - 1)
                    nc.vector.scalar_tensor_tensor(p_st[s][:, :], bank[s][:, 2 * CH:3 * CH], DHM ** -0.5, pen_d[s][:, :],
                                                   ALU.mult, ALU.mult).then_inc(ml_p, 1)

                def hidden_out(j):
                    pos, di, e = ml_steps[N_CTX + j]
                    c, s = chunk_of[di][pos] - 2, j % 2
                    dve.wait_ge(ml_num, j + 1)
                    then(nc.vector.scalar_tensor_tensor(den[s][:, :], bank[4 + s][:, 2 * CH:3 * CH], -1.0, emt[j % 3][:, :],
                                                        ALU.mult, ALU.max))
                    then(nc.vector.tensor_tensor(den[s][:, :], bank[4 + s][:, 2 * CH:3 * CH], den[s][:, :], ALU.max))
                    then(nc.vector.reciprocal(den[s][:, :], den[s][:, :]))
                    num = bank[4 + s][:, 0:2 * CH].rearrange("p (k t) -> p k t", k=2)
                    by = den[s][:, :].unsqueeze(1).to_broadcast([P, 2, CH])
                    h = buf[3][:, :].rearrange("p (k t) -> p k t", t=S)[:, 2 * e:2 * e + 2, c * CH:(c + 1) * CH]
                    if (c < 2) == (di == 0):
                        nc.vector.tensor_tensor(h, num, by, ALU.mult).then_inc(ml_h, 1)
                    else:
                        new = h_new[s][:, :].rearrange("p (k t) -> p k t", k=2)
                        then(nc.vector.tensor_tensor(new, num, by, ALU.mult))
                        nc.vector.tensor_tensor(h, h, new, ALU.add).then_inc(ml_h, 1)

                def carry(w):
                    pos, di, e = ml_steps[w]
                    c = gcol(di, chunk_of[di][pos], e)
                    dve.wait_ge(ml_upd, w + 1)
                    if pos:
                        dve.wait_ge(ml_st, w - 2 * HM + 1)
                    for kk in range(2):
                        to, new = chain_state(di, e)[:, kk, :], update_bank(w, kk)
                        if pos:
                            ins = nc.vector.scalar_tensor_tensor(to, to, decay_ws[:, c:c + 1], new, ALU.mult, ALU.add)
                        else:
                            ins = nc.vector.tensor_copy(to, new)
                    ins.then_inc(ml_st, 1)

                dve.wait_ge(ws_ready, 1)
                for w in range(N_CTX):
                    carry(w)
                for j in range(N_X + 2):
                    if 1 <= j <= N_X:
                        weigh(j - 1)
                    if j < N_X:
                        maxima(j)
                    if j >= 2:
                        if N_CTX + j - 2 < N_UPD:
                            carry(N_CTX + j - 2)
                        hidden_out(j - 2)

            def headnorm(st):
                for k in range(KT):
                    dve.wait_ge(hn_mu, k // 2 + 1)
                    h = buf[3][:, k * S:(k + 1) * S]
                    nc.vector.scalar_tensor_tensor(h, bank[k // 2][:, :], -1.0 / DHM, h, ALU.mult, ALU.add).then_inc(hn_c, 1)
                for e in range(HM):
                    dve.wait_ge(hn_var, 2 * e + 2)
                    nc.vector.tensor_scalar(h_rstd[:, e * S:(e + 1) * S], bank[4 + e][:, :], 1.0 / DHM, EPS, ALU.mult, ALU.add)\
                        .then_inc(hn_v, 1)
                dve.wait_ge(hn_std, 1)
                then(nc.vector.reciprocal(h_rstd[:, :], h_rstd[:, :]))
                for k in range(KT):
                    h = buf[3][:, k * S:(k + 1) * S]
                    nc.vector.scalar_tensor_tensor(h, h, vcol("g_head", k), h_rstd[:, k // 2 * S:(k // 2 + 1) * S], ALU.mult,
                                                   ALU.mult).then_inc(hn_done, 1)

            def sgu(st):
                for n in range(S // CH):
                    dve.wait_ge(sg_m, n + 1)
                    for h in range(2):
                        part = lambda t: t[:, :].rearrange("p (k t) -> p k t", t=S)[:, 4 * h:4 * h + 4, n * CH:(n + 1) * CH]
                        full = tmp[h][:, :].rearrange("p (k t) -> p k t", t=CH)
                        if n:
                            dve.wait_ge(sg_y, n)
                        then(nc.vector.tensor_tensor(full, bank[4 + n % 2 * 2 + h][:, :].rearrange("p (k t) -> p k t", t=CH),
                                                     part(buf[0]), ALU.mult))
                        then(nc.vector.tensor_copy(part(xn_h), full))
                        ins = nc.vector.tensor_tensor(part(xn_l), full, part(xn_h).bitcast(F32), ALU.subtract)
                    ins.then_inc(sg_y, 1)

            def fgates(st):
                dve.wait_ge(fg_mm, 1)
                dve.wait_ge(wf_in, 32)
                nc.vector.tensor_tensor(fl[:, :].rearrange("p (c h) -> p c h", h=HA),
                                        bank[7][:, 0:S // CH * HA].rearrange("p (c h) -> p c h", h=HA),
                                        bf[:, :].unsqueeze(1).to_broadcast([P, S // CH, HA]), ALU.add).then_inc(fg_pre, 1)
                dve.wait_ge(fg_ln, 3)
                nc.vector.scalar_tensor_tensor(fl[:, :], fl[:, :], 0.0, flt[:, :], ALU.min, ALU.subtract).then_inc(fg_lf, 1)

            def softmax_attention(st):
                n0, n1 = ATT[st["stage"]]

                def maxima(n):
                    dve.wait_ge(at_logits, n + 1)
                    nc.vector.tensor_reduce(neg_max[:, n:n + 1], bank[n % 3][:, 0:keys_of(n)], AX.X, ALU.max, negate=True)\
                        .then_inc(at_max, 1)

                def normalise(n):
                    dve.wait_ge(at_exp, n + 1)
                    p = p_nat[n % 3][:, 0:keys_of(n)]
                    then(nc.vector.reciprocal(p_inv[:, n:n + 1], p_sum[:, n:n + 1]))
                    nc.vector.tensor_scalar(p, p, p_inv[:, n:n + 1], None, ALU.mult).then_inc(at_p, 1)

                def result(h):
                    dve.wait_ge(at_pv, h + 1)
                    if h < HA:
                        half = slice(h % 2 * DHA, (h % 2 + 1) * DHA)
                        nc.vector.tensor_copy(fox_o[half, h // 2 * S:(h // 2 + 1) * S], bank[5 + h % 2][half, :])\
                            .then_inc(at_out, 1)
                    else:
                        for n in range(DHX // P):
                            ct = (h - HA) * (DHX // P) + n
                            then(nc.vector.tensor_copy(tile(hid_h, ct), bank[5 + n][:, :]))
                            ins = nc.vector.tensor_tensor(tile(hid_l, ct), bank[5 + n][:, :], tile(hid_h, ct).bitcast(F32),
                                                          ALU.subtract)
                        ins.then_inc(at_out, 1)

                if n0 == 0:
                    dve.wait_ge(fg_rows, 1)
                    nc.vector.tensor_copy(crow[0:HA, :], bank[7][0:HA, :]).then_inc(fg_crow, 1)
                for n in range(n0, n1 + 4):
                    if n < n1:
                        maxima(n)
                    for h in heads_after(n - 4, n0):
                        result(h)
                    if n0 <= n - 1 < n1:
                        normalise(n - 1)

            def sb(st):
                def softplus(h):
                    s = h % 2
                    dve.wait_ge(sb_ln, h + 1)
                    for b, T in enumerate(SB_BANKS):
                        sp = sp_a[h % 3][:, b * S:b * S + T]
                        then(nc.vector.scalar_tensor_tensor(sp, bank[3 * s + b][:, 0:T], 0.0, sp, ALU.max, ALU.add))
                    for j in range(NQ):
                        sp = sb_part(sp_a[h % 3], j)[:, 0:CH]
                        ins = nc.vector.scalar_tensor_tensor(sp, const("npen_lt"), 0.0, sp, ALU.is_ge, ALU.mult)
                    ins.then_inc(sb_sp, 1)

                def result(h):
                    half = slice(h % 2 * DHA, (h % 2 + 1) * DHA)
                    dve.wait_ge(sb_pv, h + 1)
                    nc.vector.tensor_copy(sb_o[half, h // 2 * S:(h // 2 + 1) * S], bank[6 + h % 2][half, :]).then_inc(sb_out, 1)

                for h in range(HA + 1):
                    if h < HA:
                        softplus(h)
                    if h:
                        result(h - 1)

            DVE_STAGE = {"gates": gates, "mlstm": mlstm, "headnorm": headnorm, "sgu": sgu, "fgates": fgates, "fox": softmax_attention, "sb": sb,
                         "xattn": softmax_attention}
            for st in stages:
                if isinstance(st, Phase):
                    gemm(st)
                elif isinstance(st, Norm):
                    norm(st)
                else:
                    DVE_STAGE[st["stage"]](st)


WEIGHTS = ["w_ada", "w_ffn1_in", "w_ffn1_out", "w_in", "w_branch_a", "w_branch_b", "w_out", "w_ffn2_in", "w_ffn2_out",
           "w_in_2", "w_out_2", "w_mq_2", "w_mkv_2", "w_mo_2", "w_up_2", "w_down_2"]


def _constants():
    i = np.arange(P)
    row, col = i[:, None], i[None, :]
    one, big = np.float32(1), np.float32(BIG)
    mats = {"ident": (row == col) * one, "ones": np.ones((P, P), np.float32), "neg_ones": -np.ones((P, P), np.float32),
            "neg_le": -((row <= col) * one), "neg_ge": -((row >= col) * one),
            "npen_le": -((row > col) * big), "npen_ge": -((row < col) * big), "npen_lt": -((row >= col) * big)}
    return np.concatenate([mats[n].astype(np.float32) for n in CONSTS], axis=1)


def _positions():
    t = np.arange(S)
    freqs = np.exp(-np.log(np.float32(10000.0)) * np.arange(D // 4, dtype=np.float32) / np.float32(D // 4))
    ar = (t // 64).astype(np.float32)[:, None] * freqs
    ac = (t % 64).astype(np.float32)[:, None] * freqs
    return np.ascontiguousarray(np.concatenate([np.sin(ar), np.cos(ar), np.sin(ac), np.cos(ac)], axis=-1).T)


def kernel(**inputs):
    import concourse.bacc as bacc
    from concourse.bass_utils import run_bass_kernel_spmd as run

    v = {name: np.asarray(a) for name, a in inputs.items()}
    nc = bacc.Bacc("TRN2", target_bir_lowering=False, num_devices=1)
    arrays = {
        "vectors": np.concatenate([np.ascontiguousarray(v[name]).reshape(-1, P).T for name, _ in VECTORS], axis=1),
        "consts": _constants(),
        "pos": _positions(),
        "x": v["x"][0].T,
        "ctx": v["ctx"][0].T,
        "gate_w": v["w_in"][0][:, 3 * D:3 * D + 4 * HM],
        "gate_b": np.broadcast_to(v["b_gates"], (P, 4 * HM)),
        "w_st": v["w_s"][0].transpose(2, 0, 1).reshape(CH, 4 * CH),
        "b_s": v["b_s"][0],
        "mem": v["mem_2"][0].T,
        "wf": v["w_in_2"][0][:, 6 * HA * DHA:],
        "bf": np.broadcast_to(v["b_forget_2"], (P, HA)),
    }
    for name in WEIGHTS:
        arrays[name] = v[name][0]
    maps, d = {}, {}
    for name, a in arrays.items():
        maps[f"in_{name}"] = np.ascontiguousarray(a)
        d[name] = nc.dram_tensor(f"in_{name}", a.shape, F32, kind="ExternalInput").ap()
    out = nc.dram_tensor("out_t", (D, S), F32, kind="ExternalOutput").ap()
    program(nc, d, out)
    got = run(nc, [maps], core_ids=[0]).results[0]["out_t"]
    return np.ascontiguousarray(got.T)[None]
```

```python
from contextlib import ExitStack

import numpy as np

import concourse.bass as bass
from concourse import mybir

F32 = mybir.dt.float32
F32R = mybir.dt.float32r
ALU = mybir.AluOpType
ACT = mybir.ActivationFunctionType
AX = mybir.AxisListType

P = 128
D = 1024
KT = D // P
S = 512
C = 256
FF = 2816
FT = FF // P
PARTS = [(0, 8), (8, 8), (16, 6)]
UNIT = 16 * P
EPS = 1e-6
BIG = float(2.0 ** 100)
NMOD = 9
CHUNK = 256
N_CHUNK = (NMOD - 3) * D // CHUNK
HM, DHM = 4, 256
CH = 128
HA, DHA = 8, 64
HX, DHX = 4, 256

VECTORS = [("c", 1), ("c_ctx", 1), ("b_ada", NMOD), ("g_ffn1", 1), ("g_mix", 1), ("g_head", 1), ("g_sgu", 1),
           ("g_ffn2", 1), ("g_final", 1), ("conv_qk_w", 6), ("conv_qk_b", 2), ("attn_norm_g_2", 1),
           ("fox_out_g_2", 0.5), ("sb_out_g_2", 0.5), ("xattn_norm_g_2", 1), ("mem_norm_g_2", 1),
           ("ffn_norm_g_2", 1), ("conv_w_2", 3 * 2 * FF / D), ("conv_b_2", 2 * FF / D), ("final_norm_g_2", 1)]
VCOL = {}
NVCOL = 0
for _name, _width in VECTORS:
    VCOL[_name] = NVCOL
    NVCOL += int(_width * KT)

CONSTS = ["ident", "ones", "neg_ones", "neg_le", "neg_ge", "npen_le", "npen_ge", "npen_lt"]


class Phase:

    def __init__(self, name, kind, weight, cols, n, x, segs=("x",), kts=KT, k0=0, natural=False, **more):
        self.name, self.kind, self.weight, self.cols, self.n = name, kind, weight, cols, n
        self.x, self.segs, self.kts, self.k0, self.natural = x, segs, kts, k0, natural
        self.more = more
        self.early_heads = False
        self.act_steps = ACT_STEPS.get(kind, 0)
        self.own_steps = OWN_STEPS.get(kind, 0) * len(segs)
        self.out_steps = OUT_STEPS.get(kind, 0)


ACT_STEPS = {"swiglu": 1, "convswiglu": 2, "convqk": 1, "sig_mul": 1, "func": 1}
OWN_STEPS = {"swiglu": 2, "convswiglu": 6, "convqk": 4, "sig_mul": 4, "mixb": 6}
OUT_STEPS = {"convqk": 1}
TOKENS = {"x": S, "ctx": C, "mem": C}


def ffn_phases(name, w_in, w_out, segs, gates, conv=False, stat=()):
    out = []
    for k0, kn in PARTS:
        out.append(Phase(f"{name}_in{k0}", "convswiglu" if conv else "swiglu", w_in, (k0 * P, FF + k0 * P), kn, "xn",
                         segs, f0=k0))
        out.append(Phase(f"{name}_out{k0}", "resid", w_out, 0, KT // 2, "hid", segs, kts=kn, k0=k0, gates=gates,
                         stat=stat if k0 == PARTS[-1][0] else ()))
    return out


class Norm:

    def __init__(self, name, src, seg, gain, shift=None, tiles=KT, out="split", out_tile=0, needs=(),
                 own_heads=False):
        self.name, self.src, self.seg, self.gain, self.shift = name, src, seg, gain, shift
        self.tiles, self.out, self.out_tile, self.needs = tiles, out, out_tile, needs
        self.tokens = TOKENS[seg]
        self.own_heads = own_heads
        self.stream = "x" if seg == "x" else "ctx"
        self.presummed = 0
        self.rooted = False
        self.inner = False
        self.tail = [self]


def program(nc, d, out):
    with ExitStack() as ctx:
        top = [(nc.sbuf_base + 31) // 32 * 32]

        def reserve(size):
            at = top[0]
            top[0] += (size + 31) // 32 * 32
            return at

        def place(name, columns, at, dtype=F32, partitions=P):
            return nc.alloc_sbuf_tensor_at(name, [partitions, columns], dtype, offset=at)

        TILE = S * 4
        at_resid, at_ctx, at_xh, at_xl = reserve(KT * TILE), reserve(KT * C * 4), reserve(KT * TILE), reserve(KT * TILE)
        at_b = [reserve(KT * TILE) for _ in range(4)] + [reserve(2 * HM * 2 * (DHM + 1) * 4)]
        at_raw = reserve(2 * UNIT * 4)
        at_wh, at_wl = reserve(2 * UNIT * 4), reserve(2 * UNIT * 4)
        at_s = reserve(5 * TILE)

        resid = place("resid", KT * S, at_resid)
        hctx = place("hctx", KT * C, at_ctx)
        xn_h = place("xn_h", KT * S, at_xh, F32R)
        xn_l = place("xn_l", KT * S, at_xl, F32R)
        hid_h = place("hid_h", KT * S, at_b[0], F32R)
        hid_l = place("hid_l", KT * S, at_b[1], F32R)
        xc_h = place("xc_h", KT * C, at_b[4], F32R)
        xc_l = place("xc_l", KT * C, at_b[4] + KT * C * 4, F32R)
        hidc_h = place("hidc_h", KT * C, at_b[2], F32R)
        hidc_l = place("hidc_l", KT * C, at_b[2] + KT * C * 4, F32R)
        sqc = [place(f"sqc{i}", C, at_b[3] + i * C * 4) for i in range(2)]
        tmpc = [place(f"tmpc{i}", C, at_b[3] + (2 + i) * C * 4) for i in range(2)]
        yc = [place(f"yc{i}", C, at_ctx + i * C * 4) for i in range(2)]
        ada_slots = [0, 1, 2, 4]
        pos = place("pos", KT * S, at_xl)
        buf = [place(f"buf{i}", KT * S, at) for i, at in enumerate(at_b)]
        raw = [place(f"raw{i}", UNIT, at_raw + i * UNIT * 4) for i in range(2)]
        w_h = [place(f"w_h{i}", UNIT, at_wh + i * UNIT * 4, F32R) for i in range(2)]
        w_l = [place(f"w_l{i}", UNIT, at_wl + i * UNIT * 4, F32R) for i in range(2)]
        sq = [place(f"sq{i}", S, at_s + i * TILE) for i in range(2)]
        tmp = [place(f"tmp{i}", S, at_s + (2 + i) * TILE) for i in range(2)]
        rstds = {"x": place("rstd", S, at_s + 4 * TILE),
                 "ctx": place("rstd_c", C, at_b[3] + 4 * C * 4 + (KT + 2) * CHUNK * 4)}
        ada_w = place("ada_w", KT * CHUNK, at_b[3] + 4 * C * 4)
        ada_acc = [place(f"ada_acc{w}", CHUNK, at_b[3] + 4 * C * 4 + (KT + w) * CHUNK * 4) for w in range(2)]
        silu_s = place("silu_s", KT * 2, reserve(KT * 2 * 4))
        ada_rows = place("ada_rows", S, at_xh)
        conv_b = [place(f"conv_b{i}", S, at_ctx + i * TILE) for i in range(2)]

        consts = place("consts", len(CONSTS) * P, reserve(len(CONSTS) * P * 4))
        vec = place("vec", NVCOL, reserve(NVCOL * 4))
        silu_c = place("silu_c", KT * 4 * 8, at_xh + TILE)
        mods = place("mods", NMOD * KT * 2, reserve(NMOD * KT * 2 * 4))
        eps, eps_root = place("eps", 1, reserve(4)), place("eps_root", 7, reserve(7 * 4))
        DER = ["ctx_gs1", "ctx_sh1", "ctx_ga1", "ctx_gs2", "ctx_sh2", "gs1", "sh1", "ga1", "gs2", "sh2", "ga2",
               "gs3", "sh3", "ga3"]
        der = place("der", len(DER) * KT, reserve(len(DER) * KT * 4))
        NG = (C + S) // CH
        gate_w = place("gate_w", KT * 4 * HM, reserve(KT * 4 * HM * 4))
        gate_wh = place("gate_wh", KT * 4 * HM, reserve(KT * 4 * HM * 4), F32R)
        gate_wl = place("gate_wl", KT * 4 * HM, reserve(KT * 4 * HM * 4), F32R)
        gate_pre = place("gate_pre", S + C, at_s + 2 * TILE)
        gate_b = place("gate_b", 4 * HM, reserve(4 * HM * 4))
        b_s = place("b_s", CH, reserve(CH * 4))
        GATE_ARRAYS = ["lf", "li", "lt", "neg_b", "a_col", "total", "cm_last", "m_in", "m_end"]
        at_gates = reserve(len(GATE_ARRAYS) * 64 * 4)
        lf, li, lt, neg_b, a_col, total, cm_last, m_in, m_end = [
            place(name, 64, at_gates + i * 64 * 4) for i, name in enumerate(GATE_ARRAYS)]
        decay_ws = place("decay_ws", 128, reserve(128 * 4))
        rows = place("rows", 2 * CH, reserve(2 * CH * 4))
        rows_in = place("rows_in", 2 * CH, at_s + 2 * TILE)
        diag = place("diag", 64, at_s + 2 * TILE + 2 * CH * 4)
        kc = place("kc", KT * C, at_b[3])
        vc = place("vc", KT * C, at_b[3] + KT * C * 4)
        state = place("state", 2 * HM * 2 * (DHM + 1), at_b[4])
        slot_at = [at_ctx, at_s]
        def scratch(name, columns, at):
            return [place(f"{name}{i}", columns, slot_at[i] + at * 4) for i in range(2)]
        m_inter, pen_d, emt = scratch("m_inter", CH, 0), scratch("pen_d", CH, CH), scratch("emt", CH, 2 * CH)
        p_st, q_int = scratch("p_st", CH, 3 * CH), scratch("q_int", 2 * CH, 4 * CH)
        n_bc, k_nat = scratch("n_bc", 2 * CH, 6 * CH), scratch("k_nat", 2 * CH, 8 * CH)
        den, h_new = scratch("den", CH, 10 * CH), scratch("h_new", 2 * CH, 11 * CH)
        emt.append(place("emt2", CH, reserve(CH * 4)))
        wv = scratch("wv", DHM + 1, 13 * CH)
        h_rstd = place("h_rstd", HM * S, at_ctx)
        v_nat = [place(f"v_nat{i}", D, at_ctx + i * D * 4) for i in range(2)]
        w_st = place("w_st", 4 * CH, at_b[4])
        HALF = KT // 2 * S
        half_buf = lambda name, i, h: place(name, HALF, at_b[i] + h * HALF * 4)
        fq, fk, sq_t, sk = half_buf("fq", 0, 0), half_buf("fk", 0, 1), half_buf("sq_t", 1, 0), half_buf("sk", 1, 1)
        fv, sv = half_buf("fv", 2, 0), half_buf("sv", 2, 1)
        fox_o, sb_o = half_buf("fox_o", 4, 0), half_buf("sb_o", 4, 1)
        SB_COLS = S * (S // CH + 1) // 2
        sp_a = [place(f"sp_a{i}", SB_COLS, at_b[3] + i * SB_COLS * 4) for i in range(3)]
        crow = place("crow", S, at_xl + 3 * TILE)
        p_t = [place(f"p_t{i}", S // CH * S, at_xh + i * KT * TILE // 2) for i in range(2)]
        p_nat = [place(f"p_nat{i}", S, at_xl + i * TILE) for i in range(3)]
        mem_k, mem_v = half_buf("mem_k", 2, 0), half_buf("mem_v", 2, 1)
        N_ATT = (HA + HX) * (S // CH)
        at_small = [at_gates]
        def small(name, columns, dtype=F32):
            at_small[0] += columns * 4
            return place(name, columns, at_small[0] - columns * 4, dtype)
        wf, wf_h, wf_l = small("wf", KT * HA), small("wf_h", KT * HA, F32R), small("wf_l", KT * HA, F32R)
        bf, fl, flt = small("bf", HA), small("fl", S // CH * HA), small("flt", S // CH * HA)
        neg_max, p_sum, p_inv = small("neg_max", N_ATT), small("p_sum", N_ATT), small("p_inv", N_ATT)
        assert at_small[0] <= at_gates + len(GATE_ARRAYS) * 64 * 4
        f_pre = place("f_pre", S, at_s + 2 * TILE)
        assert top[0] <= nc.sbuf_usable_end, (top[0], nc.sbuf_usable_end)

        bank = [ctx.enter_context(nc.psum_tensor(f"bank{i}", [P, 512], F32)) for i in range(8)]

        sum_bank = {"x": bank[6], "ctx": bank[7]}
        squares = {"x": sq, "ctx": sqc}

        def banks(slot, seg):
            if seg == "ctx":
                return [bank[3 * slot + 2][:, 0:C], bank[3 * slot + 2][:, C:2 * C]]
            return [bank[3 * slot + n][:, 0:TOKENS[seg]] for n in range(2)]

        def inputs(x, seg):
            if seg != "x":
                return (xc_h, xc_l, C) if x == "xn" else (hidc_h, hidc_l, C)
            return (xn_h, xn_l, S) if x == "xn" else (hid_h, hid_l, S)

        def const(name):
            i = CONSTS.index(name)
            return consts[:, i * P:(i + 1) * P]

        def vcol(name, i=0):
            return vec[:, bass.ds(i + VCOL[name], 1)]

        def dcol(name, i=0):
            return der[:, bass.ds(i + DER.index(name) * KT, 1)]

        def tile(t, i, n=S, stride=S):
            return t[:, bass.ds(i * stride, n)]

        def sem(name):
            return ctx.enter_context(nc.semaphore(name))

        loaded = [sem("loaded0"), sem("loaded1")]
        hi_ready = sem("hi_ready")
        lo_ready = sem("lo_ready")
        mm_done = sem("mm_done")
        bank_free = sem("bank_free")
        act_out = sem("act_out")
        dve_step = sem("dve_step")
        conv_out = sem("conv_out")
        const_in, vec_in, ctx_in, x_in = sem("const_in"), sem("vec_in"), sem("ctx_in"), sem("x_in")
        pos_added = sem("pos_added")
        ada_in = [sem(f"ada_in{i}") for i in range(4)]
        c_ready, ada_mm, ada_row, ada_turned = sem("c_ready"), sem("ada_mm"), sem("ada_row"), sem("ada_turned")
        ada_taken, c_zeroed, chain = sem("ada_taken"), sem("c_zeroed"), sem("chain")
        ada2_in, ada2_step, ada2_mm, ada2_taken = sem("ada2_in"), sem("ada2_step"), sem("ada2_mm"), sem("ada2_taken")
        sq_ready = {stream: sem(f"sq_ready_{stream}") for stream in ("x", "ctx")}
        sq_used = {stream: sem(f"sq_used_{stream}") for stream in ("x", "ctx")}
        std_ready, rstd_ready, eps_ready = sem("std_ready"), sem("rstd_ready"), sem("eps_ready")
        scaled, xh_ready, xn_ready = sem("scaled"), sem("xh_ready"), sem("xn_ready")
        out_stored = sem("out_stored")
        gate_in, bs_in, ws_in = sem("gate_in"), sem("bs_in"), sem("ws_in")
        gw_h, gw_l = sem("gw_h"), sem("gw_l")
        pre_mm, pre_taken, f_ready = sem("pre_mm"), sem("pre_taken"), sem("f_ready")
        gates_mm, abs_ready, ln_ready, lf_ready = sem("gates_mm"), sem("abs_ready"), sem("ln_ready"), sem("lf_ready")
        sums_mm, a_ready, rows_mm, diag_ready = sem("sums_mm"), sem("a_ready"), sem("rows_mm"), sem("diag_ready")
        last_mm, diff_ready, ws_ready = sem("last_mm"), sem("diff_ready"), sem("ws_ready")
        ml_a, ml_kt, ml_row, ml_exp, ml_kn = sem("ml_a"), sem("ml_kt"), sem("ml_row"), sem("ml_exp"), sem("ml_kn")
        ml_q, ml_p, ml_num, ml_upd, ml_h, ml_st = sem("ml_q"), sem("ml_p"), sem("ml_num"), sem("ml_upd"), sem("ml_h"), sem("ml_st")
        hn_mu, hn_c, hn_sq, hn_var, hn_v, hn_std = [sem("hn_" + s) for s in ("mu", "c", "sq", "var", "v", "std")]
        hn_done = sem("hn_done")
        sg_t, sg_v, sg_m, sg_y = sem("sg_t"), sem("sg_v"), sem("sg_m"), sem("sg_y")
        wf_in, mem_in = sem("wf_in"), sem("mem_in")
        fw_h, fw_l, fp_mm, fp_taken = sem("fw_h"), sem("fw_l"), sem("fp_mm"), sem("fp_taken")
        fg_mm, fg_pre, fg_ln, fg_lf, fg_rows, fg_crow = [sem("fg_" + s) for s in ("mm", "pre", "ln", "lf", "rows", "crow")]
        at_logits, at_max, at_exp, at_p = sem("at_logits"), sem("at_max"), sem("at_exp"), sem("at_p")
        at_tr, at_copy, at_pv, at_out = sem("at_tr"), sem("at_copy"), sem("at_pv"), sem("at_out")
        sb_z, sb_abs, sb_e, sb_ln, sb_sp = sem("sb_z"), sem("sb_abs"), sem("sb_e"), sem("sb_ln"), sem("sb_sp")
        sb_cum, sb_a, sb_pv, sb_out = sem("sb_cum"), sem("sb_a"), sem("sb_pv"), sem("sb_out")

        src_ctx = lambda k: hctx[:, k * C:(k + 1) * C]
        src_x = lambda k: resid[:, k * S:(k + 1) * S]
        residual = {"x": (resid, S), "ctx": (hctx, C)}
        at = lambda i: lambda k: tile(buf[i], k)
        nat = lambda t, width: lambda ch, k: t[:, :].rearrange("p (c w) -> p c w", w=width)[:, ch:ch + 2, bass.ds(k * 256, 256)]
        qkv = [2 * D, 2 * D + D, 2 * D + D + 4 * HM]
        o_at = 3 * D + 4 * HM
        stages = []
        stages.append(Norm("ctx_ffn1", src_ctx, "ctx", lambda k: dcol("ctx_gs1", k), "ctx_sh1"))
        stages.append(Norm("ffn1", src_x, "x", lambda k: dcol("gs1", k), "sh1"))
        mix = [Norm("mix", src_x, "x", lambda k: dcol("gs2", k), "sh2"),
               Norm("ctx_mix", src_ctx, "ctx", lambda k: dcol("ctx_gs2", k), "ctx_sh2", own_heads=True)]
        stages += ffn_phases("ffn1", "w_ffn1_in", "w_ffn1_out", ("x", "ctx"), ("ga1", "ctx_ga1"), stat=mix)
        m = 0
        for i, ph in enumerate([st for st in stages if isinstance(st, Phase)][:4]):
            ph.more["ada"] = m
            m += ph.n
        assert m == N_CHUNK
        stages.insert(stages.index(ph) + 2, dict(stage="ada_rest"))
        k_part = lambda name, o: Phase(name, "convqk", "w_in", D + o * 256, 2, "xn", ("x", "ctx"), c0=KT + 2 * o, dst={
            "x": lambda k: tile(buf[1], k + 2 * o), "ctx": lambda k: tile(kc, k + 2 * o, C, C)})
        v_part = lambda name, o, n: Phase(name, "natstore", "w_in", 2 * D + o * 256, n, "xn", ("x", "ctx"), natural=True, dst={
            "x": lambda ch, k: nat(buf[2], D)(ch, k + o), "ctx": lambda ch, k: nat(vc, D)(ch, k + o)})
        q_part = lambda name, o, n: Phase(name, "convqk", "w_in", o * 256, n, "xn", c0=2 * o,
                                       dst={"x": lambda k: tile(buf[0], k + 2 * o)})
        stages += [mix[0], q_part("q0", 0, 1), mix[1], q_part("q1", 1, 3), dict(stage="gate_pre"), k_part("k0", 0),
                   dict(stage="gates"), k_part("k2", 2), dict(stage="gate_sums"), v_part("v0", 0, 2), dict(stage="gate_rows"),
                   v_part("v2", 2, 1), dict(stage="gate_decays"), v_part("v3", 3, 1)]
        stages += [dict(stage="mlstm"), dict(stage="headnorm")]
        stages.append(Phase("ga", "func", "w_in", o_at + 3 * D, 4, "xn", func=ACT.Sigmoid, dst=at(2)))
        stages.append(Phase("o", "sig_mul", "w_in", o_at, 4, "xn", by=buf[3], after=[(hn_done, 8)]))
        stages.append(Phase("branch_a", "mul", "w_branch_a", 0, 4, "hid", dst=buf[2]))
        sgu_norm = Norm("sgu", at(1), "x", lambda k: vcol("g_sgu", k), out="f32")
        stages.append(Phase("vs", "func", "w_in", o_at + 2 * D, 4, "xn", func=ACT.Gelu_apprx_tanh, dst=at(1), stat=[sgu_norm]))
        stages.append(sgu_norm)
        stages.append(Phase("u", "func", "w_in", o_at + D, 4, "xn", func=ACT.Gelu_apprx_tanh, dst=at(0)))
        stages.append(Phase("gb", "func", "w_in", o_at + 4 * D, 4, "xn", func=ACT.Sigmoid, dst=at(3)))
        stages.append(dict(stage="sgu"))
        stages.append(Phase("branch_b", "mixb", "w_branch_b", 0, 4, "xn", by=buf[3], plus=buf[2], after=[(sg_y, 4)]))
        ffn2_norm = Norm("ffn2", src_x, "x", lambda k: dcol("gs3", k), "sh3")
        stages.append(Phase("out", "resid", "w_out", 0, 4, "hid", gates=("ga2",), stat=[ffn2_norm]))
        stages.append(ffn2_norm)
        final = Norm("final", src_x, "x", lambda k: vcol("g_final", k), out="f32")
        stages += ffn_phases("ffn2", "w_ffn2_in", "w_ffn2_out", ("x",), ("ga3",), stat=[final])
        stages.append(final)

        chunk_of = [list(range(NG)), [1, 0, 5, 4, 3, 2]]
        ml_steps = [(pos, di, e) for pos in range(NG) for di in range(2) for e in range(HM)]
        N_CTX = C // CH * 2 * HM
        N_X = len(ml_steps) - N_CTX
        N_UPD = len(ml_steps) - 2 * HM
        gcol = lambda di, g, e: di * 32 + g * HM + e
        update_bank = lambda w, kk: bank[(4 if w < N_CTX and w % 2 else 6) + kk][:, 0:DHM + 1]
        stages.append(Norm("attn", src_x, "x", lambda k: vcol("attn_norm_g_2", k)))
        W2 = HA * DHA
        for i, (name, to) in enumerate((("fq", fq), ("fk", fk), ("fv", fv), ("sq", sq_t), ("sk", sk), ("sv", sv))):
            if name[1] == "v":
                stages.append(Phase(name, "natstore", "w_in_2", i * W2, 2, "xn", natural=True, dst={"x": nat(to, W2)}))
            else:
                stages.append(Phase(name, "store", "w_in_2", i * W2, 2, "xn", scale=DHA ** -0.5 if name[1] == "q" else 1.0,
                                    dst=lambda k, to=to: tile(to, k)))
            if name in ("fq", "fk"):
                stages.append(dict(stage="f_pre" if name == "fq" else "fgates"))
        stages.append(dict(stage="fox"))
        fox_norm = Norm("fox_out", lambda k: tile(fox_o, k), "x", lambda k: vcol("fox_out_g_2", k), tiles=4,
                        needs=[(at_out, lambda k: 2 * (k + 1))])
        fox_norm.tail, fox_norm.rooted, fox_norm.inner = [], True, True
        stages += [dict(stage="fox_squares"), fox_norm, dict(stage="sb")]
        FOX_NORM_AT = 4
        stages.append(Norm("sb_out", lambda k: tile(sb_o, k), "x", lambda k: vcol("sb_out_g_2", k), tiles=4, out_tile=4,
                           needs=[(sb_out, lambda k: max(2 * (k + 1), HA - 1))]))
        xattn_norm = Norm("xattn", src_x, "x", lambda k: vcol("xattn_norm_g_2", k))
        mem_norm = Norm("mem", src_ctx, "mem", lambda k: vcol("mem_norm_g_2", k), needs=[(mem_in, lambda k: 16)],
                        own_heads=True)
        stages.append(Phase("out_2", "resid", "w_out_2", 0, 4, "xn", gates=(None,), stat=[xattn_norm, mem_norm]))
        q_part = lambda name, o, n: Phase(name, "store", "w_mq_2", o * 256, n, "xn", scale=DHX ** -0.5,
                                          dst=lambda k: tile(buf[3], k + 2 * o))
        stages += [xattn_norm, q_part("mem_q0", 0, 1), mem_norm, q_part("mem_q1", 1, 3)]
        stages.append(Phase("mem_k", "store", "w_mkv_2", 0, 4, "xn", ("mem",), scale=1.0, dst=lambda k: tile(mem_k, k, C, C)))
        stages.append(Phase("mem_v", "natstore", "w_mkv_2", D, 4, "xn", ("mem",), natural=True, dst={"mem": nat(mem_v, D)}))
        stages.append(dict(stage="xattn"))
        ffn3_norm = Norm("ffn3", src_x, "x", lambda k: vcol("ffn_norm_g_2", k))
        stages.append(Phase("mem_o", "resid", "w_mo_2", 0, 4, "hid", gates=(None,), after=[(at_out, HA + HX)],
                            stat=[ffn3_norm]))
        stages.append(ffn3_norm)
        final_2 = Norm("final_2", src_x, "x", lambda k: vcol("final_norm_g_2", k), out="f32")
        stages += ffn_phases("ffn3", "w_up_2", "w_down_2", ("x",), (None,), conv=True, stat=[final_2])
        stages.append(final_2)
        phases = [st for st in stages if isinstance(st, Phase)]

        NQ = S // CH
        att_steps = [(h, i) for h in range(HA + HX) for i in range(NQ)]
        ATT = {"fox": (0, HA * NQ), "xattn": (HA * NQ, N_ATT)}
        def keys_of(n):
            h, i = att_steps[n]
            return (i + 1) * CH if h < HA else C
        def heads_after(n, first):
            return [n // NQ] if n >= first and n % NQ == NQ - 1 else []
        SB_BANKS = [S, S, 2 * CH]
        SB_AT = {0: (0, 0), 1: (1, 0), 3: (1, 3 * CH), 2: (2, 0)}
        SB_WIDTH = lambda j: S - j * CH
        def sb_part(t, j):
            b, c = SB_AT[j]
            return t[:, b * S + c:b * S + c + SB_WIDTH(j)]

        units = acts = owns = outs = norms = ntiles = nsplit = 0
        nsq = {"x": 0, "ctx": 0}
        last_in_bank, rstd_used = {}, {}
        fresh = []
        made = None
        in_place = None
        for st in stages:
            if isinstance(st, Phase):
                st.base, st.act_base, st.own_base, st.out_base = units, acts, owns, outs
                units += st.n
                acts += st.n * st.act_steps
                owns += st.n * st.own_steps
                outs += st.n * st.out_steps
                st.wait_for = None
                for n in st.more.get("stat", ()):
                    n.presummed = 2 * (st.n - 1)
                    n.tail = st.more["stat"] if n is st.more["stat"][0] else []
                if st.x == "xn":
                    for n in [n for n in fresh if n.seg in st.segs]:
                        st.wait_for = ("norm", n.tile_base - n.out_tile)
                        fresh.remove(n)
                if st.x == "hid":
                    st.wait_for = made
                if st.kind in ("swiglu", "convswiglu"):
                    made = ("units", st.base, 1)
                if st.kind in ("sig_mul", "mixb"):
                    made = ("units", st.base, 2)
            elif isinstance(st, Norm):
                follows = stages[stages.index(st) + 1:][:1]
                st.next_phase = follows[0] if follows and isinstance(follows[0], Phase) else None
                if st.next_phase:
                    st.next_phase.early_heads = True
                st.index, st.tile_base, st.split_base, st.units_before = norms, ntiles, nsplit, units
                st.in_place_before = in_place
                in_place = ntiles if st.out != "split" else None
                st.sq_base, st.bank_before = nsq[st.stream], last_in_bank.get(st.stream)
                st.rstd_before = rstd_used.get(st.stream)
                rstd_used[st.stream] = ntiles + st.tiles
                nsq[st.stream] += st.tiles
                last_in_bank[st.stream] = norms
                norms += 1
                ntiles += st.tiles
                if st.out == "split":
                    nsplit += 0 if st.own_heads else st.tiles
                    fresh.append(st)
            else:
                st.update(units=units, outs=outs, ntiles=ntiles)
        first_norms = [st for st in stages[:2]]
        for n in first_norms:
            n.tail, n.rooted = [], True
        ALL = units
        ADA_GROUPS = [4, 2]
        CTX_CHUNKS = 2 * D // CHUNK
        ada_stages = [st for st in stages if isinstance(st, Phase) and "ada" in st.more]

        def ada_steps(ph, k):
            m0 = ph.more["ada"]
            each = KT * (2 if m0 < CTX_CHUNKS else 1)
            return k * each + (KT * (m0 + min(m0, CTX_CHUNKS)))

        def ada_chunk(ph, k):
            return k + ph.more["ada"]

        def for_ctx(m):
            return m < CTX_CHUNKS

        def run_units(eng, ph, body, peel=0):
            first = ph.n if ph.more.get("stat") else max(peel, 2 - ph.base, 0)
            for k in range(min(first, ph.n)):
                body(k, (ph.base + k) % 2)
            pairs = max(ph.n - first, 0) // 2
            if pairs >= 2:
                with eng.Fori(0, pairs) as i:
                    for j in range(2):
                        body(i * 2 + (first + j), (ph.base + first + j) % 2)
                first += 2 * pairs
            for k in range(first, ph.n):
                body(k, (ph.base + k) % 2)

        def half_count(base, k, slot):
            if isinstance(k, int):
                return (base + k) // 2 + 1
            return (k + (base - slot)) // 2 + 1

        block = ctx.enter_context(nc.Block())

        @block.sync
        def _(sp):
            sp.dma_start(vec[:, :], d["vectors"]).then_inc(vec_in, 16)
            sp.dma_start(consts[:, :], d["consts"]).then_inc(const_in, 16)
            w_ada = d["w_ada"].rearrange("(k p) n -> p k n", p=P)

            def ada_unit(u, slot):
                if u >= 4:
                    sp.wait_ge(ada_mm, u - 3)
                view = buf[ada_slots[slot]][:, :].rearrange("p (k n) -> p k n", n=512)
                sp.dma_start(view, w_ada[:, :, u * 512:(u + 1) * 512]).then_inc(ada_in[slot], 16)

            for u in range(2):
                ada_unit(u, u)
            sp.dma_start(hctx[:, :].rearrange("p (k n) -> p k n", n=C),
                         d["ctx"].rearrange("(k p) n -> p k n", p=P)).then_inc(ctx_in, 16)
            sp.dma_start(resid[:, :].rearrange("p (k n) -> p k n", n=S),
                         d["x"].rearrange("(k p) n -> p k n", p=P)).then_inc(x_in, 16)
            sp.dma_start(pos[:, :].rearrange("p (k n) -> p k n", n=S),
                         d["pos"].rearrange("(k p) n -> p k n", p=P)).then_inc(x_in, 16)
            for u in range(2, sum(ADA_GROUPS)):
                ada_unit(u, u % 4)

            def gemm(ph):
                w = d[ph.weight].rearrange("(k p) n -> p k n", p=P)

                def unit(k, slot):
                    u = k + ph.base
                    if not isinstance(u, int) or u >= 2:
                        sp.wait_ge(lo_ready, u - 1)
                    view = raw[slot][:, 0:ph.kts * 256].rearrange("p (k n) -> p k n", n=256)
                    if isinstance(ph.cols, tuple):
                        for n in range(2):
                            sp.dma_start(view[:, :, n * P:(n + 1) * P],
                                         w[:, ph.k0:ph.k0 + ph.kts, bass.ds(k * P + ph.cols[n], P)])\
                                .then_inc(loaded[slot], 16)
                    else:
                        half = ph.kts // 2
                        for k0, k1 in ((0, half), (half, ph.kts)):
                            sp.dma_start(view[:, k0:k1, :],
                                         w[:, ph.k0 + k0:ph.k0 + k1, bass.ds(k * 256 + ph.cols, 256)])\
                                .then_inc(loaded[slot], 16)

                run_units(sp, ph, unit)

            for st in stages:
                if isinstance(st, Phase):
                    gemm(st)
            for k in range(0, KT, 2):
                sp.wait_ge(xn_ready, ntiles - KT + k + 2)
                sp.dma_start(out.rearrange("(k p) n -> p k n", p=P)[:, k:k + 2],
                             resid[:, k * S:(k + 2) * S].rearrange("p (k n) -> p k n", n=S)).then_inc(out_stored, 16)
            sp.wait_ge(out_stored, KT // 2 * 16)

        @block.gpsimd
        def _(pool):
            def rests(u, slot):
                pool.wait_ge(hi_ready, u + 1)
                nc.gpsimd.tensor_tensor(w_l[slot][:, :], raw[slot][:, :], w_h[slot][:, :].bitcast(F32),
                                        ALU.subtract).then_inc(lo_ready, 1)

            def rests_between(first, end):
                for u in range(first, min(first + first % 2, end)):
                    rests(u, u % 2)
                first += first % 2
                with pool.Fori(first // 2, end // 2) as i:
                    for j in range(2):
                        rests(i * 2 + j, j)
                if end % 2:
                    rests(end - 1, 0)

            done = 0
            def mlstm(st):
                for j in range(N_X):
                    pos, di, e = ml_steps[N_CTX + j]
                    g, s = chunk_of[di][pos], j % 2
                    pool.wait_ge(ml_exp, j + 1)
                    pool.wait_ge(ml_st, N_CTX + j - 2 * HM + 1)
                    if j >= 2:
                        pool.wait_ge(ml_num, j - 1)
                    q = buf[0][:, :].rearrange("p (k t) -> p k t", t=S)[:, 2 * e:2 * e + 2, (g - 2) * CH:(g - 1) * CH]
                    nc.gpsimd.tensor_tensor(q_int[s][:, :].rearrange("p (k t) -> p k t", k=2), q,
                                            m_inter[s][:, :].unsqueeze(1).to_broadcast([P, 2, CH]), ALU.mult)
                    o = (di * HM + e) * 2 * (DHM + 1)
                    n = state[:, o:o + 2 * (DHM + 1)].rearrange("p (k n) -> p k n", k=2)[:, :, DHM:DHM + 1]
                    nc.gpsimd.tensor_copy(n_bc[s][:, :].rearrange("p (k t) -> p k t", k=2), n.to_broadcast([P, 2, CH]))\
                        .then_inc(ml_q, 1)

            POOL_STAGE = {"mlstm": mlstm}
            for st in stages:
                if isinstance(st, dict) and st["stage"] in POOL_STAGE:
                    ahead = min(st["units"] + 1, ALL)
                    rests_between(done, ahead)
                    done = ahead
                    POOL_STAGE[st["stage"]](st)
            rests_between(done, ALL)

        @block.scalar
        def _(act):
            def heads(u, slot, count):
                act.wait_ge(loaded[slot], count * 32)
                if not isinstance(u, int) or u >= 2:
                    act.wait_ge(mm_done, u - 1)
                nc.scalar.activation(w_h[slot][:, :], raw[slot][:, :], ACT.Copy).then_inc(hi_ready, 1)

            def gemm(ph):
                def unit(k, slot):
                    u = k + ph.base
                    last = ph is phases[-1] and isinstance(k, int) and k == ph.n - 1
                    early = ph.early_heads and isinstance(k, int) and k == 0
                    if not last and not early:
                        heads(u + 1, 1 - slot, half_count(ph.base, k + 1, 1 - slot))
                    if "ada" in ph.more:
                        if not isinstance(k, int) or ada_chunk(ph, k):
                            act.wait_ge(ada2_step, ada_steps(ph, k))
                        act.dma_start(ada_w[:, :].rearrange("p (k n) -> p k n", n=CHUNK),
                                      d["w_ada"].rearrange("(k p) n -> p k n", p=P)
                                      [:, :, bass.ds(ada_chunk(ph, k) * CHUNK + 3 * D, CHUNK)]).then_inc(ada2_in, 16)
                    if ph.more.get("stat") and k:
                        act.wait_ge(bank_free, u)
                        for n in ph.more["stat"]:
                            for i in (2 * k - 2, 2 * k - 1):
                                square(n, i)
                        if k == ph.n - 1 and ph.kind == "resid":
                            i = [p for p in phases if p.more.get("stat") and p.kind == "resid"].index(ph)
                            nc.scalar.activation(eps_root[:, i:i + 1], eps[:, :], ACT.Sqrt)
                    if ph.kind in ACT_STEPS:
                        act.wait_ge(mm_done, u + 1)
                    if ph.kind == "swiglu":
                        for seg, s in zip(ph.segs, (sq, sqc)):
                            ins = nc.scalar.activation(s[slot][:, 0:TOKENS[seg]], banks(slot, seg)[0], ACT.Silu)
                        ins.then_inc(act_out, 1)
                    elif ph.kind == "convswiglu":
                        b = banks(slot, "x")
                        for n, y in enumerate((sq[slot], conv_b[slot])):
                            ct = k + (n * FT + ph.more["f0"])
                            ins = nc.scalar.activation(y[:, :], b[n], ACT.Identity,
                                                       bias=vcol("conv_b_2", ct), scale=vcol("conv_w_2", ct + 4 * FT))
                        ins.then_inc(act_out, 1)
                        act.wait_ge(dve_step, k * 6 + (ph.own_base + 3))
                        nc.scalar.activation(sq[slot][:, :], sq[slot][:, :], ACT.Silu).then_inc(act_out, 1)
                    elif ph.kind == "convqk":
                        if not isinstance(k, int) or k + ph.out_base:
                            act.wait_ge(conv_out, k + ph.out_base)
                        for seg, y in zip(ph.segs, (sq, yc)):
                            for n in range(2):
                                ct = k * 2 + (n + ph.more["c0"])
                                ins = nc.scalar.activation(y[n][:, 0:TOKENS[seg]], banks(slot, seg)[n], ACT.Identity,
                                                           bias=vcol("conv_qk_b", ct),
                                                           scale=vcol("conv_qk_w", ct + 2 * KT))
                        ins.then_inc(act_out, 1)
                        act.wait_ge(bank_free, u + 1)
                        for seg, y in zip(ph.segs, (sq, yc)):
                            for n in range(2):
                                ins = nc.scalar.activation(ph.more["dst"][seg](k * 2 + n), y[n][:, 0:TOKENS[seg]],
                                                           ACT.Silu)
                        ins.then_inc(conv_out, 1)
                    elif ph.kind == "sig_mul":
                        act.wait_ge(bank_free, u)
                        for n in range(2):
                            ins = nc.scalar.activation(sq[n][:, :], banks(slot, "x")[n], ACT.Sigmoid)
                        ins.then_inc(act_out, 1)
                    elif ph.kind == "func":
                        for n in range(2):
                            ins = nc.scalar.activation(ph.more["dst"](k * 2 + n), banks(slot, "x")[n],
                                                       ph.more["func"])
                        ins.then_inc(act_out, 1)

                run_units(act, ph, unit, peel=ph.n if ph is phases[-1] else max(ph.out_steps, int(ph.early_heads), int("ada" in ph.more)))

            def square(n, k):
                t = n.sq_base + k
                if n.in_place_before is not None:
                    act.wait_ge(xn_ready, n.in_place_before + k + 1)
                for s, value in n.needs:
                    act.wait_ge(s, value(k))
                if t >= 2:
                    act.wait_ge(sq_used[n.stream], t - 1)
                nc.scalar.activation(squares[n.stream][t % 2][:, 0:n.tokens], n.src(k), ACT.Square)\
                    .then_inc(sq_ready[n.stream], 1)

            def root(n):
                rstd = rstds[n.stream][:, 0:n.tokens]
                if n.rstd_before:
                    act.wait_ge(xn_ready, n.rstd_before)
                act.wait_ge(sq_used[n.stream], n.sq_base + n.tiles)
                nc.scalar.activation(rstd, sum_bank[n.stream][:, 0:n.tokens], ACT.Sqrt, bias=eps[:, :],
                                     scale=1.0 / (n.tiles * P)).then_inc(std_ready, 1)

            def norm(n):
                T = n.tokens
                if n.units_before:
                    act.wait_ge(bank_free, n.units_before)
                for m in n.tail:
                    for k in range(m.presummed, m.tiles):
                        square(m, k)
                if not n.rooted:
                    root(n)
                if n.next_phase:
                    base = n.next_phase.base
                    heads(base + 1, (base + 1) % 2, half_count(base, 1, 0))
                if n.out == "split" and not n.own_heads:
                    for k in range(n.tiles):
                        act.wait_ge(scaled, n.split_base + k + 1)
                        head, _, stride = inputs("xn", n.seg)
                        dst = head[:, (n.out_tile + k) * stride:(n.out_tile + k) * stride + T]
                        if n.shift:
                            ins = nc.scalar.activation(dst, tmp[k % 2][:, 0:T], ACT.Identity, bias=dcol(n.shift, k))
                        else:
                            ins = nc.scalar.activation(dst, tmp[k % 2][:, 0:T], ACT.Copy)
                        ins.then_inc(xh_ready, 1)

            act.wait_ge(vec_in, 16)
            cv = VCOL["c"]
            act.wait_ge(c_zeroed, 1)
            for g in range(4):
                to = silu_c[:, g * KT * 8:(g + 1) * KT * 8].rearrange("p (k w) -> p w k", w=8)[:, 2 * g:2 * g + 2]
                ins = nc.scalar.activation(to, vec[:, cv:cv + 2 * KT].rearrange("p (w k) -> p w k", w=2), ACT.Silu)
            ins.then_inc(c_ready, 1)
            nc.scalar.activation(silu_s[:, :].rearrange("p (k w) -> p w k", w=2),
                                 vec[:, cv:cv + 2 * KT].rearrange("p (w k) -> p w k", w=2), ACT.Silu)\
                .then_inc(c_ready, 1)
            act.dma_start(gate_w[:, :].rearrange("p (k n) -> p k n", n=4 * HM),
                          d["gate_w"].rearrange("(k p) n -> p k n", p=P)).then_inc(gate_in, 16)
            act.dma_start(gate_b[:, :], d["gate_b"]).then_inc(gate_in, 16)
            act.wait_ge(gate_in, 32)
            nc.scalar.activation(gate_wh[:, :], gate_w[:, :], ACT.Copy).then_inc(gw_h, 1)
            act.dma_start(b_s[0:4, :], d["b_s"]).then_inc(bs_in, 16)

            def gate_pre_acts(st):
                pass

            def gates(st):
                act.wait_ge(f_ready, 1)
                nc.scalar.activation(lt[:, :], lf[:, :], ACT.Abs).then_inc(abs_ready, 1)
                act.wait_ge(abs_ready, 1)
                nc.scalar.activation(lt[:, :], lt[:, :], ACT.Exp, scale=-1.0).then_inc(ln_ready, 1)
                act.wait_ge(ln_ready, 1)
                nc.scalar.activation(lt[:, :], lt[:, :], ACT.Ln, bias=1.0).then_inc(ln_ready, 1)

            def gate_decays(st):
                act.wait_ge(diff_ready, 1)
                nc.scalar.activation(decay_ws[:, :], decay_ws[:, :], ACT.Exp).then_inc(ws_ready, 1)

            def mlstm(st):
                def exps(j):
                    pos, di, e = ml_steps[N_CTX + j]
                    c, s = gcol(di, chunk_of[di][pos], e), j % 2
                    act.wait_ge(ml_row, j + 1)
                    nc.scalar.activation(pen_d[s][:, :], pen_d[s][:, :], ACT.Exp, scale=-1.0, bias=a_col[:, c:c + 1])
                    nc.scalar.activation(m_inter[s][:, :], m_inter[s][:, :], ACT.Exp, scale=-1.0, bias=m_in[:, c:c + 1])
                    nc.scalar.activation(emt[j % 3][:, :], emt[j % 3][:, :], ACT.Exp).then_inc(ml_exp, 1)

                def naturals(w):
                    pos, di, e = ml_steps[w]
                    g, s = chunk_of[di][pos], w % 2
                    ws = decay_ws[:, 64 + gcol(di, g, e):65 + gcol(di, g, e)]
                    act.wait_ge(ml_kt, w + 1)
                    if w >= 2:
                        act.wait_ge(ml_upd, w - 1)
                    v = vc[:, g * D:(g + 1) * D] if g < 2 else buf[2][:, (g - 2) * D:(g - 1) * D]
                    nc.scalar.activation(k_nat[s][:, :], bank[2 + s][:, 0:2 * CH], ACT.Copy, scale=DHM ** -0.5)
                    nc.scalar.activation(wv[s][:, 0:DHM], v[:, e * DHM:(e + 1) * DHM], ACT.Copy, scale=ws)
                    nc.scalar.activation(wv[s][:, DHM:DHM + 1], ws, ACT.Copy).then_inc(ml_kn, 1)

                act.wait_ge(bank_free, st["units"])
                for w in range(N_CTX):
                    naturals(w)
                for j in range(N_X):
                    exps(j)
                    if N_CTX + j < N_UPD:
                        naturals(N_CTX + j)
                act.wait_ge(ml_num, N_X)
                act.dma_start(w_st[:, :], d["w_st"]).then_inc(ws_in, 16)

            def headnorm(st):
                for k in range(KT):
                    act.wait_ge(hn_c, k + 1)
                    if k >= 2:
                        act.wait_ge(hn_var, k - 1)
                    nc.scalar.activation(sq[k % 2][:, :], buf[3][:, k * S:(k + 1) * S], ACT.Square).then_inc(hn_sq, 1)
                act.wait_ge(hn_v, HM)
                nc.scalar.activation(h_rstd[:, :], h_rstd[:, :], ACT.Sqrt).then_inc(hn_std, 1)
                act.dma_start(wf[:, :].rearrange("p (k n) -> p k n", n=HA), d["wf"].rearrange("(k p) n -> p k n", p=P))        .then_inc(wf_in, 16)
                act.dma_start(bf[:, :], d["bf"]).then_inc(wf_in, 16)

            def sgu(st):
                for n in range(S // CH):
                    act.wait_ge(sg_t, n + 1)
                    if n >= 2:
                        act.wait_ge(sg_m, n - 1)
                    for h in range(2):
                        ins = nc.scalar.activation(v_nat[n % 2][:, h * 512:(h + 1) * 512], bank[n % 2 * 2 + h][:, :], ACT.Copy)
                    ins.then_inc(sg_v, 1)
                act.wait_ge(wf_in, 32)
                nc.scalar.activation(wf_h[:, :], wf[:, :], ACT.Copy).then_inc(fw_h, 1)

            def nothing(st):
                pass

            ada_rest = nothing
            def f_preacts(st):
                act.wait_ge(bank_free, st["units"])
                act.dma_start(hctx[:, :].rearrange("p (k n) -> p k n", n=C),
                              d["mem"].rearrange("(k p) n -> p k n", p=P)).then_inc(mem_in, 16)

            def fgates(st):
                act.wait_ge(fg_pre, 1)
                nc.scalar.activation(flt[:, :], fl[:, :], ACT.Abs).then_inc(fg_ln, 1)
                act.wait_ge(fg_ln, 1)
                nc.scalar.activation(flt[:, :], flt[:, :], ACT.Exp, scale=-1.0).then_inc(fg_ln, 1)
                act.wait_ge(fg_ln, 2)
                nc.scalar.activation(flt[:, :], flt[:, :], ACT.Ln, bias=1.0).then_inc(fg_ln, 1)

            def softmax_attention(st):
                n0, n1 = ATT[st["stage"]]
                for n in range(n0, n1 + 2):
                    if n < n1:
                        act.wait_ge(at_max, n + 1)
                        if n >= 3:
                            act.wait_ge(at_tr, n - 2)
                        T = keys_of(n)
                        nc.scalar.activation(p_nat[n % 3][:, 0:T], bank[n % 3][:, 0:T], ACT.Exp, bias=neg_max[:, n:n + 1],
                                             accum_out=p_sum[:, n:n + 1]).then_inc(at_exp, 1)
                    if n - 2 >= n0:
                        m = n - 2
                        h, i = att_steps[m]
                        act.wait_ge(at_tr, m + 1)
                        if i == 0 and h >= 2:
                            act.wait_ge(at_pv, h - 1)
                        T = keys_of(m)
                        to = p_t[h % 2][:, :].rearrange("p (j t) -> p j t", t=S)[:, 0:T // CH, i * CH:(i + 1) * CH]
                        nc.scalar.activation(to, bank[3 + m % 2][:, 0:T].rearrange("p (j t) -> p j t", t=CH), ACT.Copy)\
                            .then_inc(at_copy, 1)

            def sb(st):
                def logs(h):
                    s, sp = h % 2, sp_a[h % 3]
                    act.wait_ge(sb_z, h + 1)
                    if h >= 3:
                        act.wait_ge(sb_pv, h - 2)
                    for b, T in enumerate(SB_BANKS):
                        nc.scalar.activation(sp[:, b * S:b * S + T], bank[3 * s + b][:, 0:T], ACT.Abs).then_inc(sb_abs, 1)
                    act.wait_ge(sb_abs, 3 * h + 3)
                    nc.scalar.activation(sp[:, :], sp[:, :], ACT.Exp, scale=-1.0).then_inc(sb_e, 1)
                    act.wait_ge(sb_e, h + 1)
                    nc.scalar.activation(sp[:, :], sp[:, :], ACT.Ln, bias=1.0).then_inc(sb_ln, 1)

                def weights(h):
                    s = h % 2
                    act.wait_ge(sb_cum, h + 1)
                    for b, T in enumerate(SB_BANKS):
                        ins = nc.scalar.activation(sp_a[h % 3][:, b * S:b * S + T], bank[3 * s + b][:, 0:T], ACT.Exp)
                    ins.then_inc(sb_a, 1)

                for h in range(HA + 1):
                    if h < HA:
                        logs(h)
                    if h:
                        weights(h - 1)
                    if h == FOX_NORM_AT:
                        norm(fox_norm)

            def fox_squares(st):
                for k in range(fox_norm.tiles):
                    square(fox_norm, k)
                root(fox_norm)

            ACT_STAGE = {"ada_rest": ada_rest, "gate_pre": gate_pre_acts, "gates": gates, "gate_sums": nothing, "gate_rows": nothing, "gate_decays": gate_decays, "mlstm": mlstm,
                         "headnorm": headnorm, "sgu": sgu, "f_pre": f_preacts, "fgates": fgates, "fox": softmax_attention, "fox_squares": fox_squares, "sb": sb,
                         "xattn": softmax_attention}
            act.wait_ge(eps_ready, 1)
            act.wait_ge(ctx_in, 16)
            for n in first_norms:
                if n.seg == "x":
                    act.wait_ge(pos_added, 1)
                for k in range(n.tiles):
                    square(n, k)
            for n in first_norms:
                root(n)
            heads(0, 0, 1)
            for st in stages:
                if isinstance(st, Phase):
                    gemm(st)
                elif isinstance(st, Norm):
                    if not st.inner:
                        norm(st)
                else:
                    ACT_STAGE[st["stage"]](st)

        @block.tensor
        def _(pe):
            def gemm(ph):
                for s, value in ph.more.get("after", ()):
                    pe.wait_ge(s, value)

                def unit(k, slot):
                    u = k + ph.base
                    pe.wait_ge(lo_ready, u + 1)
                    if not isinstance(u, int) or u >= 2:
                        pe.wait_ge(bank_free, u - 1)
                    first = isinstance(k, int) and k == 0 and ph.wait_for

                    def input_ready(kt):
                        if first and ph.wait_for[0] == "norm":
                            pe.wait_ge(xn_ready, ph.wait_for[1] + kt + 1)
                        elif first:
                            pe.wait_ge(bank_free, ph.wait_for[1] + kt // ph.wait_for[2] + 1)

                    if ph.natural:
                        for seg in ph.segs:
                            head, rest, stride = inputs(ph.x, seg)
                            for ch in range(TOKENS[seg] // P):
                                to = bank[3 * slot + 2 * (seg == "ctx") + ch // 2][:, (ch % 2) * 256:(ch % 2 + 1) * 256]
                                for kt in range(ph.kts):
                                    if ch == 0 and seg == ph.segs[0]:
                                        input_ready(kt)
                                    xs = slice(kt * stride + ch * P, kt * stride + (ch + 1) * P)
                                    ws = slice(kt * 256, (kt + 1) * 256)
                                    pe.matmul(to, head[:, xs], w_h[slot][:, ws], start=(kt == 0), stop=False)
                                    pe.matmul(to, rest[:, xs], w_h[slot][:, ws], start=False, stop=False)
                                    ins = pe.matmul(to, head[:, xs], w_l[slot][:, ws], start=False,
                                                    stop=(kt == ph.kts - 1))
                    else:
                        for kt in range(ph.kts):
                            input_ready(kt)
                            for n in range(2):
                                ws = slice(kt * 256 + n * P, kt * 256 + (n + 1) * P)
                                for w, part in ((w_h, 0), (w_h, 1), (w_l, 0)):
                                    for seg in ph.segs:
                                        x = inputs(ph.x, seg)
                                        xs = slice(kt * x[2], kt * x[2] + TOKENS[seg])
                                        opens = kt == 0 and w is w_h and part == 0 and not (seg == "ctx" and n)
                                        ins = pe.matmul(banks(slot, seg)[n], w[slot][:, ws], x[part][:, xs],
                                                        start=opens, stop=(kt == ph.kts - 1 and w is w_l),
                                                        skip_group_check=(seg == "ctx"))
                    ins.then_inc(mm_done, 1)
                    if "ada" in ph.more and not (isinstance(k, int) and ada_chunk(ph, k) == 0):
                        ada_columns(ada_steps(ph, k), isinstance(k, int) and for_ctx(ada_chunk(ph, k) - 1)
                                    or not isinstance(k, int) and for_ctx(ph.more["ada"]))
                    if ph.more.get("stat") and k:
                        for n in ph.more["stat"]:
                            for i in (2 * k - 2, 2 * k - 1):
                                add_square(n, i)

                run_units(pe, ph, unit, peel=1 if ph.wait_for or "ada" in ph.more else 0)

            def ada_columns(steps, with_ctx):
                pe.wait_ge(ada2_step, steps)
                for w in range(1 + with_ctx):
                    for n in range(CHUNK // P):
                        ins = pe.matmul(bank[7][:, w * 2 + n:w * 2 + n + 1], ada_acc[w][:, n * P:(n + 1) * P],
                                        const("ones")[:, 0:1], start=True, stop=True)
                ins.then_inc(ada2_mm, 1)

            def add_square(n, k):
                t = n.sq_base + k
                pe.wait_ge(sq_ready[n.stream], t + 1)
                if k == 0 and n.bank_before is not None:
                    pe.wait_ge(std_ready, n.bank_before + 1)
                pe.matmul(sum_bank[n.stream][:, 0:n.tokens], const("ones"), squares[n.stream][t % 2][:, 0:n.tokens],
                          start=(k == 0), stop=(k == n.tiles - 1)).then_inc(sq_used[n.stream], 1)

            def norm(n):
                for m in n.tail:
                    for k in range(m.presummed, m.tiles):
                        add_square(m, k)

            pe.wait_ge(c_ready, 1)

            def ada_unit(grp, g):
                pe.wait_ge(ada_in[g], grp * 16 + 16)
                if g == 0 and grp:
                    pe.wait_ge(ada_row, grp)
                for kt in range(KT):
                    o = (g * KT + kt) * 8
                    ins = pe.matmul(bank[0][0:8, :], silu_c[:, o:o + 8],
                                    buf[ada_slots[g]][:, kt * 512:(kt + 1) * 512], start=(g == 0 and kt == 0),
                                    stop=(g == ADA_GROUPS[grp] - 1 and kt == KT - 1))
                ins.then_inc(ada_mm, 1)

            def ada_turn(grp):
                pe.wait_ge(ada_row, grp + 1)
                if grp:
                    pe.wait_ge(ada_taken, grp)
                for n in range(4):
                    ins = pe.matmul(bank[1][:, n * 8:n * 8 + 8], ada_rows[0:8, n * P:(n + 1) * P],
                                    const("ident")[0:8, 0:8], start=True, stop=True)
                ins.then_inc(ada_turned, 1)

            pe.wait_ge(const_in, 16)
            for g in range(ADA_GROUPS[0]):
                if g == 2:
                    for n in first_norms:
                        for k in range(n.tiles):
                            add_square(n, k)
                ada_unit(0, g)
            for g in range(ADA_GROUPS[1]):
                ada_unit(1, g)
                if g == 0:
                    ada_turn(0)
            ada_turn(1)
            pe.wait_ge(ada_taken, 2)

            def ada_rest(st):
                ada_columns(ada_steps(ada_stages[-1], ada_stages[-1].n), False)

            def one_hot(n, r):
                return const("ident")[0:n, r:r + 1].to_broadcast([n, P])

            def gate_pre_acts(st):
                pe.wait_ge(gw_l, 1)
                pe.wait_ge(xn_ready, st["ntiles"])
                for to, seg in ((bank[6], "ctx"), (bank[7], "x")):
                    head, rest, stride = inputs("xn", seg)
                    for kt in range(KT):
                        ws = slice(kt * 4 * HM, (kt + 1) * 4 * HM)
                        for w, part in ((gate_wh, head), (gate_wh, rest), (gate_wl, head)):
                            ins = pe.matmul(to[0:4 * HM, 0:stride], w[:, ws], part[:, kt * stride:(kt + 1) * stride],
                                            start=(kt == 0 and part is head and w is gate_wh), stop=(kt == KT - 1 and w is gate_wl))
                ins.then_inc(pre_mm, 1)

            def gates(st):
                pe.wait_ge(pre_taken, 1)
                for g in range(NG):
                    ins = pe.transpose(bank[7][:, g * 16:(g + 1) * 16], gate_pre[0:16, g * CH:(g + 1) * CH],
                                       const("ident")[0:16, 0:16])
                ins.then_inc(gates_mm, 1)

            def gate_sums(st):
                pe.wait_ge(lf_ready, 1)
                pe.matmul(bank[7][:, 128:160], const("neg_le"), lf[:, 0:32], start=True, stop=True)
                pe.matmul(bank[7][:, 160:192], const("neg_ge"), lf[:, 32:64], start=True, stop=True)
                pe.matmul(bank[7][:, 192:256], const("ones"), lf[:, :], start=True, stop=True).then_inc(sums_mm, 1)

            def gate_rows(st):
                pe.wait_ge(a_ready, 1)
                pe.transpose(bank[6][0:64, 0:CH], a_col[:, :], const("ident"))
                pe.transpose(bank[6][0:64, CH:2 * CH], neg_b[:, :], const("ident")).then_inc(rows_mm, 1)

            def gate_decays(st):
                pe.wait_ge(diag_ready, 1)
                pe.matmul(bank[7][:, 256:320], const("ones")[0:64, :], diag[0:64, :], start=True, stop=True).then_inc(last_mm, 1)

            def mlstm(st):
                def key(g, ct):
                    if g < 2:
                        return kc[:, ct * C + g * CH:ct * C + (g + 1) * CH]
                    return buf[1][:, ct * S + (g - 2) * CH:ct * S + (g - 1) * CH]

                def chain_state(di, e, kk, a, b):
                    o = ((di * HM + e) * 2 + kk) * (DHM + 1)
                    return state[:, o + a:o + b]

                def keys_by_token(w):
                    pos, di, e = ml_steps[w]
                    if w >= 2:
                        pe.wait_ge(ml_kn, w - 1)
                    for kk in range(2):
                        ins = pe.transpose(bank[2 + w % 2][:, kk * CH:(kk + 1) * CH], key(chunk_of[di][pos], e * 2 + kk),
                                           const("ident"))
                    ins.then_inc(ml_kt, 1)

                def scores(j):
                    pos, di, e = ml_steps[N_CTX + j]
                    g = chunk_of[di][pos]
                    if j >= 2:
                        pe.wait_ge(ml_p, j - 1)
                    pe.matmul(bank[j % 2][:, 0:2 * CH], one_hot(64, gcol(di, g, e)), rows[0:64, :], start=True, stop=True)
                    for kk in range(2):
                        ct = e * 2 + kk
                        ins = pe.matmul(bank[j % 2][:, 2 * CH:3 * CH], key(g, ct),
                                        buf[0][:, ct * S + (g - 2) * CH:ct * S + (g - 1) * CH], start=(kk == 0), stop=(kk == 1))
                    ins.then_inc(ml_a, 1)

                def outputs(j):
                    pos, di, e = ml_steps[N_CTX + j]
                    g, s = chunk_of[di][pos], j % 2
                    pe.wait_ge(ml_p, j + 1)
                    pe.wait_ge(ml_q, j + 1)
                    if j >= 2:
                        pe.wait_ge(ml_h, j - 1)
                    to = bank[4 + s]
                    for vv in range(2):
                        o = (g - 2) * D + e * DHM + vv * CH
                        pe.matmul(to[:, vv * CH:(vv + 1) * CH], buf[2][:, o:o + CH], p_st[s][:, :], start=True, stop=False)
                        for kk in range(2):
                            pe.matmul(to[:, vv * CH:(vv + 1) * CH], chain_state(di, e, kk, vv * CH, (vv + 1) * CH),
                                      q_int[s][:, kk * CH:(kk + 1) * CH], start=False, stop=(kk == 1))
                    pe.matmul(to[:, 2 * CH:3 * CH], const("ones"), p_st[s][:, :], start=True, stop=False)
                    for kk in range(2):
                        ins = pe.matmul(to[:, 2 * CH:3 * CH], n_bc[s][:, kk * CH:(kk + 1) * CH],
                                        q_int[s][:, kk * CH:(kk + 1) * CH], start=False, stop=(kk == 1))
                    ins.then_inc(ml_num, 1)

                def update(w):
                    pe.wait_ge(ml_kn, w + 1)
                    taken = w - 1 if w < N_CTX else w
                    if taken > 0:
                        pe.wait_ge(ml_st, taken)
                    for kk in range(2):
                        ins = pe.matmul(update_bank(w, kk), k_nat[w % 2][:, kk * CH:(kk + 1) * CH], wv[w % 2][:, :],
                                        start=True, stop=True)
                    ins.then_inc(ml_upd, 1)

                pe.wait_ge(conv_out, st["outs"])
                pe.wait_ge(bank_free, st["units"])
                pe.wait_ge(ws_ready, 1)
                for w in range(N_CTX + 1):
                    if w < N_CTX:
                        keys_by_token(w)
                    if w:
                        update(w - 1)
                for j in range(N_X + 1):
                    w = N_CTX + j
                    if j < N_X:
                        scores(j)
                        if w < N_UPD:
                            keys_by_token(w)
                    if j:
                        outputs(j - 1)
                        if w - 1 < N_UPD:
                            update(w - 1)

            def headnorm(st):
                pe.wait_ge(ml_h, N_X)
                for e in range(HM):
                    for i in range(2):
                        ct = e * 2 + i
                        ins = pe.matmul(bank[e][:, :], const("ones"), buf[3][:, ct * S:(ct + 1) * S], start=(i == 0), stop=(i == 1))
                    ins.then_inc(hn_mu, 1)
                for k in range(KT):
                    pe.wait_ge(hn_sq, k + 1)
                    pe.matmul(bank[4 + k // 2][:, :], const("ones"), sq[k % 2][:, :], start=(k % 2 == 0), stop=(k % 2 == 1))\
                        .then_inc(hn_var, 1)

            def sgu(st):
                def turn(n):
                    if n >= 2:
                        pe.wait_ge(sg_v, n - 1)
                    for ct in range(KT):
                        ins = pe.transpose(bank[n % 2 * 2 + ct // 4][:, ct % 4 * CH:(ct % 4 + 1) * CH],
                                           buf[1][:, ct * S + n * CH:ct * S + (n + 1) * CH], const("ident"))
                    ins.then_inc(sg_t, 1)

                def mix(n):
                    pe.wait_ge(sg_v, n + 1)
                    if n >= 2:
                        pe.wait_ge(sg_y, n - 1)
                    for ct in range(KT):
                        to, g = bank[4 + n % 2 * 2 + ct // 4][:, ct % 4 * CH:(ct % 4 + 1) * CH], ct // 2
                        pe.matmul(to, v_nat[n % 2][:, ct * CH:(ct + 1) * CH], w_st[:, g * CH:(g + 1) * CH], start=True, stop=False)
                        ins = pe.matmul(to, one_hot(4, g), b_s[0:4, :], start=False, stop=True)
                    ins.then_inc(sg_m, 1)

                pe.wait_ge(xn_ready, st["ntiles"])
                pe.wait_ge(bank_free, st["units"])
                pe.wait_ge(ws_in, 16)
                pe.wait_ge(bs_in, 16)
                for n in range(S // CH + 1):
                    if n < S // CH:
                        turn(n)
                    if n:
                        mix(n - 1)

            def f_preacts(st):
                pe.wait_ge(fw_l, 1)
                pe.wait_ge(xn_ready, st["ntiles"])
                for kt in range(KT):
                    ws, xs = slice(kt * HA, (kt + 1) * HA), slice(kt * S, (kt + 1) * S)
                    for w, part in ((wf_h, xn_h), (wf_h, xn_l), (wf_l, xn_h)):
                        ins = pe.matmul(bank[7][0:HA, :], w[:, ws], part[:, xs], start=(kt == 0 and part is xn_h and w is wf_h),
                                        stop=(kt == KT - 1 and w is wf_l))
                ins.then_inc(fp_mm, 1)

            def fgates(st):
                pe.wait_ge(fp_taken, 1)
                for c in range(S // CH):
                    ins = pe.transpose(bank[7][:, c * HA:(c + 1) * HA], f_pre[0:HA, c * CH:(c + 1) * CH],
                                       const("ident")[0:HA, 0:HA])
                ins.then_inc(fg_mm, 1)

            def softmax_attention(st):
                n0, n1 = ATT[st["stage"]]

                def logits(n):
                    h, i = att_steps[n]
                    T = keys_of(n)
                    to = bank[n % 3][:, 0:T]
                    if n >= 3:
                        pe.wait_ge(at_exp, n - 2)
                    if h < HA:
                        pair, half = h // 2, slice(h % 2 * DHA, (h % 2 + 1) * DHA)
                        pe.matmul(to, fq[half, pair * S + i * CH:pair * S + (i + 1) * CH], fk[half, pair * S:pair * S + T],
                                  start=True, stop=False)
                        pe.matmul(to, one_hot(HA, h), crow[0:HA, 0:T], start=False, stop=False)
                        ins = pe.matmul(bank[n % 3][:, T - CH:T], const("ident"), const("npen_ge"), start=False, stop=True)
                    else:
                        for kk in range(DHX // P):
                            ct = (h - HA) * (DHX // P) + kk
                            ins = pe.matmul(to, buf[3][:, ct * S + i * CH:ct * S + (i + 1) * CH], mem_k[:, ct * C:(ct + 1) * C],
                                            start=(kk == 0), stop=(kk == DHX // P - 1))
                    ins.then_inc(at_logits, 1)

                def turn(n):
                    pe.wait_ge(at_p, n + 1)
                    if n >= 2:
                        pe.wait_ge(at_copy, n - 1)
                    for j in range(keys_of(n) // CH):
                        ins = pe.transpose(bank[3 + n % 2][:, j * CH:(j + 1) * CH], p_nat[n % 3][:, j * CH:(j + 1) * CH],
                                           const("ident"))
                    ins.then_inc(at_tr, 1)

                def values(h):
                    pe.wait_ge(at_copy, (h + 1) * NQ)
                    if h < HA:
                        if h >= 2:
                            pe.wait_ge(at_out, h - 1)
                        for j in range(NQ):
                            vs = fv[:, j * W2 + h // 2 * P:j * W2 + (h // 2 + 1) * P]
                            ins = pe.matmul(bank[5 + h % 2 * 2][:, j * CH:S], vs, p_t[h % 2][:, j * S + j * CH:(j + 1) * S],
                                            start=(j == 0), stop=(j == NQ - 1))
                    else:
                        pe.wait_ge(at_out, h)
                        for n in range(DHX // P):
                            for j in range(C // CH):
                                o = j * D + (h - HA) * DHX + n * P
                                ins = pe.matmul(bank[5 + n][:, :], mem_v[:, o:o + P], p_t[h % 2][:, j * S:(j + 1) * S],
                                                start=(j == 0), stop=(j == C // CH - 1))
                    ins.then_inc(at_pv, 1)

                pe.wait_ge(bank_free, st["units"])
                if n0 == 0:
                    pe.wait_ge(fg_lf, 1)
                    for c in range(NQ):
                        for b in range(c + 1):
                            ins = pe.matmul(bank[7][0:HA, c * CH:(c + 1) * CH], fl[:, b * HA:(b + 1) * HA],
                                            const("neg_le" if b == c else "neg_ones"), start=(b == 0), stop=(b == c))
                    ins.then_inc(fg_rows, 1)
                    pe.wait_ge(fg_crow, 1)
                for n in range(n0, n1 + 3):
                    if n < n1:
                        logits(n)
                    if n0 <= n - 2 < n1:
                        turn(n - 2)
                    for h in heads_after(n - 3, n0):
                        values(h)

            def fox_squares(st):
                for k in range(fox_norm.tiles):
                    add_square(fox_norm, k)

            def sb(st):
                def scores(h):
                    s, half = h % 2, slice(h % 2 * DHA, (h % 2 + 1) * DHA)
                    if h >= 2:
                        pe.wait_ge(sb_a, h - 1)
                    for j in range(NQ):
                        b, c = SB_AT[j]
                        o = h // 2 * S + j * CH
                        ins = pe.matmul(bank[3 * s + b][:, c:c + SB_WIDTH(j)], sk[half, o:o + CH],
                                        sq_t[half, o:(h // 2 + 1) * S], start=(c == 0), stop=True, skip_group_check=True)
                    ins.then_inc(sb_z, 1)

                def sums(h):
                    s = h % 2
                    pe.wait_ge(sb_sp, h + 1)
                    for j in range(NQ):
                        b, c = SB_AT[j]
                        W = SB_WIDTH(j)
                        for jj in range(j, NQ):
                            pe.matmul(bank[3 * s + b][:, c + W - SB_WIDTH(jj):c + W], const("neg_ge" if jj == j else "neg_ones"),
                                      sb_part(sp_a[h % 3], jj), start=False, stop=False, skip_group_check=True)
                        ins = pe.matmul(bank[3 * s + b][:, c:c + CH], const("ident"), const("npen_lt"), start=False, stop=True,
                                        skip_group_check=True)
                    ins.then_inc(sb_cum, 1)

                def values(h):
                    pe.wait_ge(sb_a, h + 1)
                    if h >= 2:
                        pe.wait_ge(sb_out, h - 1)
                    for j in range(NQ):
                        vs = sv[:, j * W2 + h // 2 * P:j * W2 + (h // 2 + 1) * P]
                        ins = pe.matmul(bank[6 + h % 2][:, j * CH:S], vs, sb_part(sp_a[h % 3], j), start=(j == 0),
                                        stop=(j == NQ - 1))
                    ins.then_inc(sb_pv, 1)

                pe.wait_ge(at_out, HA)
                scores(0)
                for h in range(HA + 1):
                    if h + 1 < HA:
                        scores(h + 1)
                    if h < HA:
                        sums(h)
                    if h:
                        values(h - 1)

            PE_STAGE = {"ada_rest": ada_rest, "gate_pre": gate_pre_acts, "gates": gates, "gate_sums": gate_sums, "gate_rows": gate_rows, "gate_decays": gate_decays, "mlstm": mlstm,
                         "headnorm": headnorm, "sgu": sgu, "f_pre": f_preacts, "fgates": fgates, "fox": softmax_attention, "fox_squares": fox_squares, "sb": sb,
                         "xattn": softmax_attention}
            for st in stages:
                if isinstance(st, Phase):
                    gemm(st)
                elif isinstance(st, Norm):
                    if not st.inner:
                        norm(st)
                else:
                    PE_STAGE[st["stage"]](st)

        @block.vector
        def _(dve):
            steps = [0]

            def then(ins):
                steps[0] += 1
                ins.then_inc(chain, 1)
                dve.wait_ge(chain, steps[0])

            def gemm(ph):
                def unit(k, slot):
                    u = k + ph.base
                    own = lambda i: k * ph.own_steps + (ph.own_base + i)
                    if ph.act_steps:
                        dve.wait_ge(act_out, k * ph.act_steps + (ph.act_base + 1))
                    else:
                        dve.wait_ge(mm_done, u + 1)

                    def split(fulls, where, done):
                        count = len(fulls)
                        for i, (full, (head, rest)) in enumerate(zip(fulls, where)):
                            dve.wait_ge(dve_step, own(done + i + 1))
                            nc.vector.tensor_copy(head, full).then_inc(dve_step, 1)
                        for i, (full, (head, rest)) in enumerate(zip(fulls, where)):
                            dve.wait_ge(dve_step, own(done + count + i + 1))
                            ins = nc.vector.tensor_tensor(rest, full, head.bitcast(F32), ALU.subtract)
                        ins.then_inc(bank_free, 1)

                    def hidden(seg, i):
                        head, rest, stride = inputs("hid", seg)
                        return tile(head, i, TOKENS[seg], stride), tile(rest, i, TOKENS[seg], stride)

                    if ph.kind == "swiglu":
                        fulls = []
                        for seg, s, t in zip(ph.segs, (sq, sqc), (tmp, tmpc)):
                            fulls.append(t[slot][:, 0:TOKENS[seg]])
                            nc.vector.tensor_tensor(fulls[-1], s[slot][:, 0:TOKENS[seg]], banks(slot, seg)[1],
                                                    ALU.mult).then_inc(dve_step, 1)
                        split(fulls, [hidden(seg, k) for seg in ph.segs], 0)
                    elif ph.kind == "convswiglu":
                        b = banks(slot, "x")
                        y = (sq[slot], conv_b[slot])
                        tap = lambda n, w: vcol("conv_w_2", k + (n * FT + ph.more["f0"] + 2 * FT * w))
                        for back in (1, 2):
                            for n in range(2):
                                if back == 2:
                                    dve.wait_ge(dve_step, own(n + 1))
                                nc.vector.scalar_tensor_tensor(y[n][:, back:S], b[n][:, 0:S - back], tap(n, 2 - back),
                                                               y[n][:, back:S], ALU.mult, ALU.add)\
                                    .then_inc(dve_step, 1)
                        dve.wait_ge(dve_step, own(4))
                        dve.wait_ge(act_out, k * 2 + (ph.act_base + 2))
                        nc.vector.tensor_tensor(tmp[slot][:, :], y[0][:, :], y[1][:, :], ALU.mult).then_inc(dve_step, 1)
                        split([tmp[slot][:, :]], [hidden("x", k)], 4)
                    elif ph.kind == "resid":
                        for seg, gate in zip(ph.segs, ph.more["gates"]):
                            h, stride = residual[seg]
                            for n in range(2):
                                to, b = tile(h, k * 2 + n, TOKENS[seg], stride), banks(slot, seg)[n]
                                if gate:
                                    ins = nc.vector.scalar_tensor_tensor(to, b, dcol(gate, k * 2 + n), to, ALU.mult,
                                                                         ALU.add)
                                else:
                                    ins = nc.vector.tensor_tensor(to, b, to, ALU.add)
                        ins.then_inc(bank_free, 1)
                    elif ph.kind == "convqk":
                        tap = lambda n, w: vcol("conv_qk_w", k * 2 + (n + ph.more["c0"] + 2 * KT * w))
                        todo = [(y[n], banks(slot, seg)[n], n, TOKENS[seg])
                                for seg, y in zip(ph.segs, (sq, yc)) for n in range(2)]
                        for y, b, n, T in todo:
                            nc.vector.scalar_tensor_tensor(y[:, 1:T], b[:, 0:T - 1], tap(n, 0), y[:, 1:T],
                                                           ALU.mult, ALU.add).then_inc(dve_step, 1)
                        for i, (y, b, n, T) in enumerate(todo):
                            dve.wait_ge(dve_step, own(i + 1))
                            ins = nc.vector.scalar_tensor_tensor(y[:, 0:T - 1], b[:, 1:T], tap(n, 2), y[:, 0:T - 1],
                                                                 ALU.mult, ALU.add).then_inc(dve_step, 1)
                        dve.wait_ge(dve_step, own(2 * len(todo)))
                        dve.wait_ge(bank_free, u)
                        dve.sem_inc(bank_free, 1)
                    elif ph.kind == "sig_mul":
                        dve.wait_ge(bank_free, u)
                        fulls = [tmp[n][:, :] for n in range(2)]
                        for n in range(2):
                            nc.vector.tensor_tensor(fulls[n], sq[n][:, :], tile(ph.more["by"], k * 2 + n), ALU.mult)\
                                .then_inc(dve_step, 1)
                        split(fulls, [hidden("x", k * 2 + n) for n in range(2)], 0)
                    elif ph.kind == "mixb":
                        dve.wait_ge(bank_free, u)
                        fulls = [tmp[n][:, :] for n in range(2)]
                        for n in range(2):
                            nc.vector.tensor_tensor(fulls[n], banks(slot, "x")[n], tile(ph.more["by"], k * 2 + n),
                                                    ALU.mult).then_inc(dve_step, 1)
                        for n in range(2):
                            dve.wait_ge(dve_step, own(n + 1))
                            nc.vector.tensor_tensor(fulls[n], fulls[n], tile(ph.more["plus"], k * 2 + n), ALU.add)\
                                .then_inc(dve_step, 1)
                        split(fulls, [hidden("x", k * 2 + n) for n in range(2)], 2)
                    elif ph.kind == "func":
                        dve.wait_ge(bank_free, u)
                        dve.sem_inc(bank_free, 1)
                    elif ph.kind == "mul":
                        for n in range(2):
                            to = tile(ph.more["dst"], k * 2 + n)
                            ins = nc.vector.tensor_tensor(to, banks(slot, "x")[n], to, ALU.mult)
                        ins.then_inc(bank_free, 1)
                    elif ph.kind == "store":
                        for n in range(2):
                            ins = nc.vector.tensor_scalar(ph.more["dst"](k * 2 + n), banks(slot, ph.segs[0])[n],
                                                          ph.more["scale"], None, ALU.mult)
                        ins.then_inc(bank_free, 1)
                    elif ph.kind == "natstore":
                        for seg in ph.segs:
                            for n in range(TOKENS[seg] // 256):
                                b = bank[3 * slot + 2 * (seg == "ctx") + n]
                                ins = nc.vector.tensor_copy(ph.more["dst"][seg](2 * n, k),
                                                            b[:, :].rearrange("p (c w) -> p c w", w=256))
                        ins.then_inc(bank_free, 1)

                    if "ada" in ph.more:
                        if not (isinstance(k, int) and ada_chunk(ph, k) == 0):
                            ada_columns(ada_chunk(ph, k) - 1, isinstance(k, int) and for_ctx(ada_chunk(ph, k) - 1)
                                        or not isinstance(k, int) and for_ctx(ph.more["ada"]))
                        dve.wait_ge(ada2_in, ada_chunk(ph, k) * 16 + 16)
                        ways = 2 if for_ctx(ph.more["ada"]) else 1
                        for kt in range(KT):
                            w_kt = ada_w[:, kt * CHUNK:(kt + 1) * CHUNK]
                            for w in range(ways):
                                by = silu_s[:, kt * 2 + w:kt * 2 + w + 1]
                                if kt:
                                    dve.wait_ge(ada2_step, ada_steps(ph, k) + ((kt - 1) * ways + w + 1))
                                    ins = nc.vector.scalar_tensor_tensor(ada_acc[w][:, :], w_kt, by, ada_acc[w][:, :],
                                                                         ALU.mult, ALU.add)
                                else:
                                    ins = nc.vector.tensor_scalar(ada_acc[w][:, :], w_kt, by, None, ALU.mult)
                                ins.then_inc(ada2_step, 1)

                run_units(dve, ph, unit, peel=int("ada" in ph.more))

            def ada_columns(m, with_ctx):
                dve.wait_ge(ada2_mm, m + 1)
                bias = vec[:, bass.ds(m * 2 + VCOL["b_ada"] + 3 * KT, 2)]
                to = mods[:, bass.ds(m * 4 + 6 * KT, 4)].rearrange("p (n w) -> p n w", w=2)
                for w in range(1 + with_ctx):
                    ins = nc.vector.tensor_tensor(to[:, :, w], bank[7][:, w * 2:w * 2 + 2], bias, ALU.add)
                ins.then_inc(ada2_taken, 1)

            def root(n):
                rstd = rstds[n.stream][:, 0:n.tokens]
                dve.wait_ge(std_ready, n.index + 1)
                nc.vector.reciprocal(rstd, rstd).then_inc(rstd_ready, 1)
                dve.wait_ge(rstd_ready, n.index + 1)

            def norm(n):
                T = n.tokens
                rstd = rstds[n.stream]
                if not n.rooted:
                    root(n)
                if n.out != "split":
                    for k in range(n.tiles):
                        nc.vector.scalar_tensor_tensor(n.src(k), n.src(k), n.gain(k), rstd[:, 0:T], ALU.mult,
                                                       ALU.mult).then_inc(xn_ready, 1)
                    return
                for k in range(n.tiles + 1):
                    if k < n.tiles:
                        if k >= 2 or n.tile_base:
                            dve.wait_ge(xn_ready, n.tile_base + max(k - 1, 0))
                        ins = nc.vector.scalar_tensor_tensor(tmp[k % 2][:, 0:T], n.src(k), n.gain(k), rstd[:, 0:T],
                                                             ALU.mult, ALU.mult)
                        if not n.own_heads:
                            ins.then_inc(scaled, 1)
                        else:
                            then(ins)
                    if k:
                        head, rest, stride = inputs("xn", n.seg)
                        o = (n.out_tile + k - 1) * stride
                        head, rest, full = head[:, o:o + T], rest[:, o:o + T], tmp[(k - 1) % 2][:, 0:T]
                        if not n.own_heads:
                            dve.wait_ge(xh_ready, n.split_base + k)
                        elif n.shift:
                            then(nc.vector.tensor_scalar(head, full, dcol(n.shift, k - 1), None, ALU.add))
                        else:
                            then(nc.vector.tensor_copy(head, full))
                        if n.shift:
                            ins = nc.vector.scalar_tensor_tensor(rest, full, dcol(n.shift, k - 1), head.bitcast(F32),
                                                                 ALU.add, ALU.subtract)
                        else:
                            ins = nc.vector.tensor_tensor(rest, full, head.bitcast(F32), ALU.subtract)
                        ins.then_inc(xn_ready, 1)

            nc.vector.memset(eps[:, :], EPS).then_inc(eps_ready, 1)
            nc.vector.memset(silu_c[:, :], 0.0).then_inc(c_zeroed, 1)
            dve.wait_ge(x_in, 32)
            nc.vector.tensor_tensor(resid[:, :], resid[:, :], pos[:, :], ALU.add).then_inc(pos_added, 1)
            for n in first_norms:
                root(n)
            dve.wait_ge(vec_in, 16)

            for grp, units in enumerate(ADA_GROUPS):
                dve.wait_ge(ada_mm, sum(ADA_GROUPS[:grp + 1]))
                nc.vector.tensor_copy(ada_rows[0:8, :], bank[0][0:8, :]).then_inc(ada_row, 1)
                dve.wait_ge(ada_turned, grp + 1)
                o = VCOL["b_ada"] + grp * 16
                bias = vec[:, o:o + 4 * units].rearrange("p (g n) -> p g n", n=4)
                turned = bank[1][:, 0:32].rearrange("p (n g w) -> p g n w", n=4, w=2)[:, 0:units]
                to = mods[:, grp * 32:grp * 32 + 8 * units].rearrange("p (g n w) -> p g n w", n=4, w=2)
                for w in range(2):
                    ins = nc.vector.tensor_tensor(to[:, :, :, w], turned[:, :, :, w], bias, ALU.add)
                ins.then_inc(ada_taken, 1)
            dve.wait_ge(ada_taken, len(ADA_GROUPS))
            mod = lambda j, w: mods[:, :].rearrange("p (j k w) -> p j k w", j=NMOD, w=2)[:, j, :, w]
            dst = lambda name: der[:, DER.index(name) * KT:(DER.index(name) + 1) * KT]
            gains = {"1": "g_ffn1", "2": "g_mix", "3": "g_ffn2"}
            def derive(names):
                for name in names:
                    w, j = int(name.startswith("ctx")), 3 * int(name[-1]) - 3
                    what = name[-3:-1]
                    if what == "gs":
                        g = VCOL[gains[name[-1]]]
                        ins = nc.vector.scalar_tensor_tensor(dst(name), mod(j + 1, w), 1.0, vec[:, g:g + KT], ALU.add,
                                                             ALU.mult)
                    elif what == "sh":
                        ins = nc.vector.tensor_copy(dst(name), mod(j, w))
                    else:
                        ins = nc.vector.tensor_scalar(dst(name), mod(j + 2, w), 1.0 if name[-1] == "2" else 0.5, None,
                                                      ALU.mult)
                    then(ins)

            derive([name for name in DER if name.endswith("1")])

            def ada_rest(st):
                ada_columns(N_CHUNK - 1, False)
                dve.wait_ge(ada2_taken, N_CHUNK)
                derive([name for name in DER if not name.endswith("1")])

            def gate_pre_acts(st):
                dve.wait_ge(pre_mm, 1)
                nc.vector.tensor_copy(gate_pre[0:4 * HM, 0:C], bank[6][0:4 * HM, 0:C])
                nc.vector.tensor_copy(gate_pre[0:4 * HM, C:C + S], bank[7][0:4 * HM, :]).then_inc(pre_taken, 1)

            dve.wait_ge(gw_h, 1)
            nc.vector.tensor_tensor(gate_wl[:, :], gate_w[:, :], gate_wh[:, :].bitcast(F32), ALU.subtract).then_inc(gw_l, 1)

            def gates(st):
                dve.wait_ge(gates_mm, 1)
                dve.wait_ge(gate_in, 32)
                then(nc.vector.memset(lf[:, :], 0.0))
                then(nc.vector.memset(li[:, :], 0.0))
                pre = bank[7][:, 0:NG * 16].rearrange("p (g n) -> p g n", n=16)
                for di in range(2):
                    for to, typ in ((li, 0), (lf, 1)):
                        o = di * 2 * HM + typ * HM
                        view = to[:, di * 32:di * 32 + NG * HM].rearrange("p (g e) -> p g e", e=HM)
                        bias = gate_b[:, o:o + HM].unsqueeze(1).to_broadcast([P, NG, HM])
                        then(nc.vector.tensor_tensor(view, pre[:, :, o:o + HM], bias, ALU.add))
                dve.sem_inc(f_ready, 1)
                dve.wait_ge(ln_ready, 2)
                nc.vector.scalar_tensor_tensor(lf[:, :], lf[:, :], 0.0, lt[:, :], ALU.min, ALU.subtract).then_inc(lf_ready, 1)

            def gate_sums(st):
                dve.wait_ge(sums_mm, 1)
                then(nc.vector.tensor_copy(neg_b[:, :], bank[7][:, 128:192]))
                then(nc.vector.tensor_copy(total[:, :], bank[7][:, 192:256]))
                nc.vector.tensor_tensor(a_col[:, :], li[:, :], neg_b[:, :], ALU.add).then_inc(a_ready, 1)

            def gate_rows(st):
                dve.wait_ge(rows_mm, 1)
                then(nc.vector.tensor_copy(rows_in[0:64, :], bank[6][0:64, 0:2 * CH]))
                then(nc.vector.tensor_copy(rows[0:64, CH:2 * CH], rows_in[0:64, CH:2 * CH]))
                fw, bw = rows_in[0:32, 0:CH], rows_in[32:64, 0:CH][:, ::-1]
                then(nc.vector.tensor_tensor_scan(rows[0:32, 0:CH], fw, fw, -BIG, ALU.max, ALU.max))
                then(nc.vector.tensor_tensor_scan(rows[32:64, 0:CH][:, ::-1], bw, bw, -BIG, ALU.max, ALU.max))
                then(nc.vector.tensor_scalar(diag[0:32, :], const("ident")[0:32, 0:64], rows[0:32, CH - 1:CH], None, ALU.mult))
                nc.vector.tensor_scalar(diag[32:64, :], const("ident")[32:64, 0:64], rows[32:64, 0:1], None, ALU.mult)\
                    .then_inc(diag_ready, 1)

            def gate_decays(st):
                dve.wait_ge(last_mm, 1)
                then(nc.vector.tensor_copy(cm_last[:, :], bank[7][:, 256:320]))
                then(nc.vector.memset(m_in[:, :], 0.0))
                then(nc.vector.tensor_copy(m_end[:, :], cm_last[:, :]))
                for pos in range(NG):
                    for di in range(2):
                        c = gcol(di, chunk_of[di][pos], 0)
                        then(nc.vector.tensor_tensor(m_end[:, c:c + HM], m_in[:, c:c + HM], cm_last[:, c:c + HM], ALU.max))
                        if pos < NG - 1:
                            t = gcol(di, chunk_of[di][pos + 1], 0)
                            then(nc.vector.tensor_tensor(m_in[:, t:t + HM], m_end[:, c:c + HM], total[:, c:c + HM], ALU.add))
                nc.vector.tensor_tensor(decay_ws[:, 0:64], m_in[:, :], m_end[:, :], ALU.subtract)
                nc.vector.tensor_tensor(decay_ws[:, 64:128], a_col[:, :], m_end[:, :], ALU.subtract).then_inc(diff_ready, 1)

            def mlstm(st):
                def chain_state(di, e):
                    o = (di * HM + e) * 2 * (DHM + 1)
                    return state[:, o:o + 2 * (DHM + 1)].rearrange("p (k n) -> p k n", k=2)

                def maxima(j):
                    pos, di, e = ml_steps[N_CTX + j]
                    c, s = gcol(di, chunk_of[di][pos], e), j % 2
                    m = m_in[:, c:c + 1]
                    dve.wait_ge(ml_a, j + 1)
                    if j >= 2:
                        dve.wait_ge(ml_p, j - 1)
                        dve.wait_ge(ml_q, j - 1)
                    if j >= 3:
                        dve.wait_ge(ml_h, j - 2)
                    then(nc.vector.tensor_scalar(m_inter[s][:, :], bank[s][:, 0:CH], m, None, ALU.max))
                    nc.vector.scalar_tensor_tensor(pen_d[s][:, :], bank[s][:, 0:CH], m, const(("npen_le", "npen_ge")[di]),
                                                   ALU.max, ALU.subtract)
                    nc.vector.tensor_tensor(emt[j % 3][:, :], bank[s][:, CH:2 * CH], m_inter[s][:, :], ALU.subtract)\
                        .then_inc(ml_row, 1)

                def weigh(j):
                    pos, di, e = ml_steps[N_CTX + j]
                    g, s = chunk_of[di][pos], j % 2
                    dve.wait_ge(ml_exp, j + 1)
                    if j >= 2:
                        dve.wait_ge(ml_num, j - 1)
                    nc.vector.scalar_tensor_tensor(p_st[s][:, :], bank[s][:, 2 * CH:3 * CH], DHM ** -0.5, pen_d[s][:, :],
                                                   ALU.mult, ALU.mult).then_inc(ml_p, 1)

                def hidden_out(j):
                    pos, di, e = ml_steps[N_CTX + j]
                    c, s = chunk_of[di][pos] - 2, j % 2
                    dve.wait_ge(ml_num, j + 1)
                    then(nc.vector.scalar_tensor_tensor(den[s][:, :], bank[4 + s][:, 2 * CH:3 * CH], -1.0, emt[j % 3][:, :],
                                                        ALU.mult, ALU.max))
                    then(nc.vector.tensor_tensor(den[s][:, :], bank[4 + s][:, 2 * CH:3 * CH], den[s][:, :], ALU.max))
                    then(nc.vector.reciprocal(den[s][:, :], den[s][:, :]))
                    num = bank[4 + s][:, 0:2 * CH].rearrange("p (k t) -> p k t", k=2)
                    by = den[s][:, :].unsqueeze(1).to_broadcast([P, 2, CH])
                    h = buf[3][:, :].rearrange("p (k t) -> p k t", t=S)[:, 2 * e:2 * e + 2, c * CH:(c + 1) * CH]
                    if (c < 2) == (di == 0):
                        nc.vector.tensor_tensor(h, num, by, ALU.mult).then_inc(ml_h, 1)
                    else:
                        new = h_new[s][:, :].rearrange("p (k t) -> p k t", k=2)
                        then(nc.vector.tensor_tensor(new, num, by, ALU.mult))
                        nc.vector.tensor_tensor(h, h, new, ALU.add).then_inc(ml_h, 1)

                def carry(w):
                    pos, di, e = ml_steps[w]
                    c = gcol(di, chunk_of[di][pos], e)
                    dve.wait_ge(ml_upd, w + 1)
                    if pos:
                        dve.wait_ge(ml_st, w - 2 * HM + 1)
                    for kk in range(2):
                        to, new = chain_state(di, e)[:, kk, :], update_bank(w, kk)
                        if pos:
                            ins = nc.vector.scalar_tensor_tensor(to, to, decay_ws[:, c:c + 1], new, ALU.mult, ALU.add)
                        else:
                            ins = nc.vector.tensor_copy(to, new)
                    ins.then_inc(ml_st, 1)

                dve.wait_ge(ws_ready, 1)
                for w in range(N_CTX):
                    carry(w)
                for j in range(N_X + 2):
                    if 1 <= j <= N_X:
                        weigh(j - 1)
                    if j < N_X:
                        maxima(j)
                    if j >= 2:
                        if N_CTX + j - 2 < N_UPD:
                            carry(N_CTX + j - 2)
                        hidden_out(j - 2)

            def headnorm(st):
                for k in range(KT):
                    dve.wait_ge(hn_mu, k // 2 + 1)
                    h = buf[3][:, k * S:(k + 1) * S]
                    nc.vector.scalar_tensor_tensor(h, bank[k // 2][:, :], -1.0 / DHM, h, ALU.mult, ALU.add).then_inc(hn_c, 1)
                for e in range(HM):
                    dve.wait_ge(hn_var, 2 * e + 2)
                    nc.vector.tensor_scalar(h_rstd[:, e * S:(e + 1) * S], bank[4 + e][:, :], 1.0 / DHM, EPS, ALU.mult, ALU.add)\
                        .then_inc(hn_v, 1)
                dve.wait_ge(hn_std, 1)
                then(nc.vector.reciprocal(h_rstd[:, :], h_rstd[:, :]))
                for k in range(KT):
                    h = buf[3][:, k * S:(k + 1) * S]
                    nc.vector.scalar_tensor_tensor(h, h, vcol("g_head", k), h_rstd[:, k // 2 * S:(k // 2 + 1) * S], ALU.mult,
                                                   ALU.mult).then_inc(hn_done, 1)

            def sgu(st):
                for n in range(S // CH):
                    dve.wait_ge(sg_m, n + 1)
                    for h in range(2):
                        part = lambda t: t[:, :].rearrange("p (k t) -> p k t", t=S)[:, 4 * h:4 * h + 4, n * CH:(n + 1) * CH]
                        full = tmp[h][:, :].rearrange("p (k t) -> p k t", t=CH)
                        if n:
                            dve.wait_ge(sg_y, n)
                        then(nc.vector.tensor_tensor(full, bank[4 + n % 2 * 2 + h][:, :].rearrange("p (k t) -> p k t", t=CH),
                                                     part(buf[0]), ALU.mult))
                        then(nc.vector.tensor_copy(part(xn_h), full))
                        ins = nc.vector.tensor_tensor(part(xn_l), full, part(xn_h).bitcast(F32), ALU.subtract)
                    ins.then_inc(sg_y, 1)
                dve.wait_ge(fw_h, 1)
                nc.vector.tensor_tensor(wf_l[:, :], wf[:, :], wf_h[:, :].bitcast(F32), ALU.subtract).then_inc(fw_l, 1)

            def f_preacts(st):
                dve.wait_ge(fp_mm, 1)
                nc.vector.tensor_copy(f_pre[0:HA, :], bank[7][0:HA, :]).then_inc(fp_taken, 1)

            def fgates(st):
                dve.wait_ge(fg_mm, 1)
                nc.vector.tensor_tensor(fl[:, :].rearrange("p (c h) -> p c h", h=HA),
                                        bank[7][:, 0:S // CH * HA].rearrange("p (c h) -> p c h", h=HA),
                                        bf[:, :].unsqueeze(1).to_broadcast([P, S // CH, HA]), ALU.add).then_inc(fg_pre, 1)
                dve.wait_ge(fg_ln, 3)
                nc.vector.scalar_tensor_tensor(fl[:, :], fl[:, :], 0.0, flt[:, :], ALU.min, ALU.subtract).then_inc(fg_lf, 1)

            def softmax_attention(st):
                n0, n1 = ATT[st["stage"]]

                def maxima(n):
                    dve.wait_ge(at_logits, n + 1)
                    nc.vector.tensor_reduce(neg_max[:, n:n + 1], bank[n % 3][:, 0:keys_of(n)], AX.X, ALU.max, negate=True)\
                        .then_inc(at_max, 1)

                def normalise(n):
                    dve.wait_ge(at_exp, n + 1)
                    p = p_nat[n % 3][:, 0:keys_of(n)]
                    then(nc.vector.reciprocal(p_inv[:, n:n + 1], p_sum[:, n:n + 1]))
                    nc.vector.tensor_scalar(p, p, p_inv[:, n:n + 1], None, ALU.mult).then_inc(at_p, 1)

                def result(h):
                    dve.wait_ge(at_pv, h + 1)
                    if h < HA:
                        half = slice(h % 2 * DHA, (h % 2 + 1) * DHA)
                        nc.vector.tensor_copy(fox_o[half, h // 2 * S:(h // 2 + 1) * S], bank[5 + h % 2 * 2][half, :])\
                            .then_inc(at_out, 1)
                    else:
                        for n in range(DHX // P):
                            ct = (h - HA) * (DHX // P) + n
                            then(nc.vector.tensor_copy(tile(hid_h, ct), bank[5 + n][:, :]))
                            ins = nc.vector.tensor_tensor(tile(hid_l, ct), bank[5 + n][:, :], tile(hid_h, ct).bitcast(F32),
                                                          ALU.subtract)
                        ins.then_inc(at_out, 1)

                if n0 == 0:
                    dve.wait_ge(fg_rows, 1)
                    nc.vector.tensor_copy(crow[0:HA, :], bank[7][0:HA, :]).then_inc(fg_crow, 1)
                for n in range(n0, n1 + 4):
                    if n < n1:
                        maxima(n)
                    for h in heads_after(n - 4, n0):
                        result(h)
                    if n0 <= n - 1 < n1:
                        normalise(n - 1)

            def sb(st):
                def softplus(h):
                    s = h % 2
                    dve.wait_ge(sb_ln, h + 1)
                    for b, T in enumerate(SB_BANKS):
                        sp = sp_a[h % 3][:, b * S:b * S + T]
                        then(nc.vector.scalar_tensor_tensor(sp, bank[3 * s + b][:, 0:T], 0.0, sp, ALU.max, ALU.add))
                    for j in range(NQ):
                        sp = sb_part(sp_a[h % 3], j)[:, 0:CH]
                        ins = nc.vector.scalar_tensor_tensor(sp, const("npen_lt"), 0.0, sp, ALU.is_ge, ALU.mult)
                    ins.then_inc(sb_sp, 1)

                def result(h):
                    half = slice(h % 2 * DHA, (h % 2 + 1) * DHA)
                    dve.wait_ge(sb_pv, h + 1)
                    nc.vector.tensor_copy(sb_o[half, h // 2 * S:(h // 2 + 1) * S], bank[6 + h % 2][half, :]).then_inc(sb_out, 1)

                for h in range(HA + 2):
                    if h < HA:
                        softplus(h)
                    if h >= 2:
                        result(h - 2)
                    if h == FOX_NORM_AT:
                        norm(fox_norm)

            def fox_squares(st):
                root(fox_norm)

            DVE_STAGE = {"ada_rest": ada_rest, "gate_pre": gate_pre_acts, "gates": gates, "gate_sums": gate_sums, "gate_rows": gate_rows, "gate_decays": gate_decays, "mlstm": mlstm,
                         "headnorm": headnorm, "sgu": sgu, "f_pre": f_preacts, "fgates": fgates, "fox": softmax_attention, "fox_squares": fox_squares, "sb": sb,
                         "xattn": softmax_attention}
            for st in stages:
                if isinstance(st, Phase):
                    gemm(st)
                elif isinstance(st, Norm):
                    if not st.inner:
                        norm(st)
                else:
                    DVE_STAGE[st["stage"]](st)


WEIGHTS = ["w_ada", "w_ffn1_in", "w_ffn1_out", "w_in", "w_branch_a", "w_branch_b", "w_out", "w_ffn2_in", "w_ffn2_out",
           "w_in_2", "w_out_2", "w_mq_2", "w_mkv_2", "w_mo_2", "w_up_2", "w_down_2"]


def _constants():
    i = np.arange(P)
    row, col = i[:, None], i[None, :]
    one, big = np.float32(1), np.float32(BIG)
    mats = {"ident": (row == col) * one, "ones": np.ones((P, P), np.float32), "neg_ones": -np.ones((P, P), np.float32),
            "neg_le": -((row <= col) * one), "neg_ge": -((row >= col) * one),
            "npen_le": -((row > col) * big), "npen_ge": -((row < col) * big), "npen_lt": -((row >= col) * big)}
    return np.concatenate([mats[n].astype(np.float32) for n in CONSTS], axis=1)


def _positions():
    t = np.arange(S)
    freqs = np.exp(-np.log(np.float32(10000.0)) * np.arange(D // 4, dtype=np.float32) / np.float32(D // 4))
    ar = (t // 64).astype(np.float32)[:, None] * freqs
    ac = (t % 64).astype(np.float32)[:, None] * freqs
    return np.ascontiguousarray(np.concatenate([np.sin(ar), np.cos(ar), np.sin(ac), np.cos(ac)], axis=-1).T)


def kernel(**inputs):
    import concourse.bacc as bacc
    from concourse.bass_utils import run_bass_kernel_spmd as run

    v = {name: np.asarray(a) for name, a in inputs.items()}
    nc = bacc.Bacc("TRN2", target_bir_lowering=False, num_devices=1)
    arrays = {
        "vectors": np.concatenate([np.ascontiguousarray(v[name]).reshape(-1, P).T for name, _ in VECTORS], axis=1),
        "consts": _constants(),
        "pos": _positions(),
        "x": v["x"][0].T,
        "ctx": v["ctx"][0].T,
        "gate_w": v["w_in"][0][:, 3 * D:3 * D + 4 * HM],
        "gate_b": np.broadcast_to(v["b_gates"], (P, 4 * HM)),
        "w_st": v["w_s"][0].transpose(2, 0, 1).reshape(CH, 4 * CH),
        "b_s": v["b_s"][0],
        "mem": v["mem_2"][0].T,
        "wf": v["w_in_2"][0][:, 6 * HA * DHA:],
        "bf": np.broadcast_to(v["b_forget_2"], (P, HA)),
    }
    for name in WEIGHTS:
        arrays[name] = v[name][0]
    maps, d = {}, {}
    for name, a in arrays.items():
        maps[f"in_{name}"] = np.ascontiguousarray(a)
        d[name] = nc.dram_tensor(f"in_{name}", a.shape, F32, kind="ExternalInput").ap()
    out = nc.dram_tensor("out_t", (D, S), F32, kind="ExternalOutput").ap()
    program(nc, d, out)
    got = run(nc, [maps], core_ids=[0]).results[0]["out_t"]
    return np.ascontiguousarray(got.T)[None]
```
